# Optimizing a Trainium2 kernel written in Bass

```python
import math
import jax, jax.numpy as jnp
from jax import lax
import numpy as np

D_MODEL = 1024
BATCH = 1
SEQ = 1024
DEPTH = 1

MLA_HEADS = 8
MLA_NOPE = 64
MLA_ROPE = 32
MLA_V = 64
MLA_Q_RANK = 256
MLA_KV_RANK = 128
ROPE_THETA = 10000.0
DIFF_HEADS = 4
DIFF_HEAD_DIM = 64
DIFF_V = 2 * DIFF_HEAD_DIM
T5_BUCKETS = 32
T5_MAX_DIST = 128
N_EXPERTS = 32
TOP_K = 4
D_EXPERT = 1024
SWIGLU_LIMIT = 7.0
SWIGLU_ALPHA = 1.702
Q_BLOCK = 128
EXPERT_BLOCK = 128
NORM_EPS = 1e-5
NEG_INF = -1e30
OFF_KV = MLA_Q_RANK
OFF_DQ = OFF_KV + MLA_KV_RANK + MLA_ROPE
OFF_DK = OFF_DQ + DIFF_HEADS * 2 * DIFF_HEAD_DIM
OFF_DV = OFF_DK + DIFF_HEADS * 2 * DIFF_HEAD_DIM
OFF_GATE = OFF_DV + DIFF_HEADS * DIFF_V
IN_TOTAL = OFF_GATE + 2 * D_MODEL
IN_SPLITS = (OFF_KV, OFF_DQ, OFF_DK, OFF_DV, OFF_GATE)

kernel_name = "hybrid_mla_diffattn_t5_moe"

def rmsnorm(x, g):
    xf = x.astype(jnp.float32)
    y = xf * lax.rsqrt(jnp.mean(xf * xf, axis=-1, keepdims=True) + NORM_EPS)
    return (y * g.astype(jnp.float32)).astype(x.dtype)

def apply_rope(x, cos, sin):
    half = x.shape[-1] // 2
    x1, x2 = x[..., :half], x[..., half:]
    return jnp.concatenate([x1 * cos - x2 * sin, x1 * sin + x2 * cos], axis=-1).astype(x.dtype)

def to_blocks(a):
    b, s = a.shape[0], a.shape[1]
    a = a.reshape((b, s // Q_BLOCK, Q_BLOCK) + a.shape[2:])
    return jnp.moveaxis(a, 1, 0)

def from_blocks(a):
    a = jnp.moveaxis(a, 0, 1)
    return a.reshape((a.shape[0], a.shape[1] * a.shape[2]) + a.shape[3:])

def t5_bucket(q_pos, k_pos):
    n = jnp.maximum(q_pos - k_pos, 0)
    max_exact = T5_BUCKETS // 2
    nf = jnp.maximum(n, 1).astype(jnp.float32)
    large = max_exact + (jnp.log(nf / max_exact) / math.log(T5_MAX_DIST / max_exact)
                         * (T5_BUCKETS - max_exact)).astype(jnp.int32)
    large = jnp.minimum(large, T5_BUCKETS - 1)
    return jnp.where(n < max_exact, n, large)

def mla_attention(q_nope, q_rope, k_nope, k_rope, v, pos):
    scale = (MLA_NOPE + MLA_ROPE) ** -0.5

    def block(args):
        qn, qr, qp = args
        s = (jnp.einsum('bqhd,bkhd->bhqk', qn, k_nope)
             + jnp.einsum('bqhr,bkr->bhqk', qr, k_rope)).astype(jnp.float32) * scale
        causal = qp[:, :, None] >= pos[:, None, :]
        s = jnp.where(causal[:, None], s, NEG_INF)
        p = jax.nn.softmax(s, axis=-1).astype(v.dtype)
        return jnp.einsum('bhqk,bkhd->bqhd', p, v)

    out = lax.map(block, (to_blocks(q_nope), to_blocks(q_rope), to_blocks(pos)))
    return from_blocks(out)

def diff_attention(q, k, v, pos, rel_bias, lam):
    scale = DIFF_HEAD_DIM ** -0.5

    def block(args):
        qb, qp = args
        s = jnp.einsum('bqhcd,bkhcd->bhcqk', qb, k).astype(jnp.float32) * scale
        bucket = t5_bucket(qp[:, :, None], pos[:, None, :])
        bias = jnp.transpose(rel_bias[bucket], (0, 3, 1, 2)).astype(jnp.float32)
        s = s + bias[:, :, None]
        causal = qp[:, :, None] >= pos[:, None, :]
        s = jnp.where(causal[:, None, None], s, NEG_INF)
        p = jax.nn.softmax(s, axis=-1)
        a = (p[:, :, 0] - lam * p[:, :, 1]).astype(v.dtype)
        return jnp.einsum('bhqk,bkhe->bqhe', a, v)

    out = lax.map(block, (to_blocks(q), to_blocks(pos)))
    return from_blocks(out)

def clamped_swiglu(hcat):
    glu, lin = hcat[..., :D_EXPERT], hcat[..., D_EXPERT:]
    glu = jnp.minimum(glu, SWIGLU_LIMIT)
    lin = jnp.clip(lin, -SWIGLU_LIMIT, SWIGLU_LIMIT)
    return glu * jax.nn.sigmoid(SWIGLU_ALPHA * glu) * (lin + 1.0)

def moe_ffn(h, w_router, b_router, w1, b1, w2, b2):
    b, s, d = h.shape
    n = b * s
    t = h.reshape(n, d)
    logits = (t @ w_router + b_router).astype(jnp.float32)
    top_val, top_idx = lax.top_k(logits, TOP_K)
    top_w = jax.nn.softmax(top_val, axis=-1)
    nk = n * TOP_K
    flat_e = top_idx.reshape(nk)
    flat_tok = jnp.repeat(jnp.arange(n, dtype=jnp.int32), TOP_K)
    flat_w = top_w.reshape(nk)
    order = jnp.argsort(flat_e)
    se, stok, sw = flat_e[order], flat_tok[order], flat_w[order]
    counts = jnp.zeros((N_EXPERTS,), jnp.int32).at[flat_e].add(1)
    start = jnp.cumsum(counts) - counts
    padded = (counts + EXPERT_BLOCK - 1) // EXPERT_BLOCK * EXPERT_BLOCK
    pend = jnp.cumsum(padded)
    pstart = pend - padded
    dest = pstart[se] + (jnp.arange(nk, dtype=jnp.int32) - start[se])
    n_blocks = -(-nk // EXPERT_BLOCK) + N_EXPERTS
    rows = n_blocks * EXPERT_BLOCK
    row_tok = jnp.full((rows,), n, jnp.int32).at[dest].set(stok)
    row_w = jnp.zeros((rows,), jnp.float32).at[dest].set(sw)
    block_e = jnp.minimum(
        jnp.searchsorted(pend, jnp.arange(n_blocks, dtype=jnp.int32) * EXPERT_BLOCK, side='right'),
        N_EXPERTS - 1).astype(jnp.int32)
    t_pad = jnp.concatenate([t, jnp.zeros((1, d), t.dtype)], axis=0)
    xs = t_pad[row_tok].reshape(n_blocks, EXPERT_BLOCK, d)

    def expert_block(args):
        xb, e = args
        act = clamped_swiglu(xb @ w1[e] + b1[e])
        return act @ w2[e] + b2[e]

    ys = lax.map(expert_block, (xs, block_e)).reshape(rows, d)
    ys = ys * row_w[:, None].astype(ys.dtype)
    out = jax.ops.segment_sum(ys, row_tok, num_segments=n + 1)[:n]
    return out.reshape(b, s, d)

def hybrid_layer(x, pos, cos, sin, rel_bias, lambda_init, norm_mix, w_in, mla_q_norm, w_q_b,
                 mla_kv_norm, w_kv_b, diff_lambda, diff_subln, w_up_mla, w_up_diff, w_out,
                 norm_ffn, w_router, b_router, w1, b1, w2, b2):
    b, s, _ = x.shape
    h = rmsnorm(x, norm_mix)
    proj = h @ w_in
    q_a, kv_a, dq, dk, dv, gates = jnp.split(proj, IN_SPLITS, axis=-1)

    q = (rmsnorm(q_a, mla_q_norm) @ w_q_b).reshape(b, s, MLA_HEADS, MLA_NOPE + MLA_ROPE)
    q_nope, q_rope = q[..., :MLA_NOPE], q[..., MLA_NOPE:]
    c_kv, k_rope = kv_a[..., :MLA_KV_RANK], kv_a[..., MLA_KV_RANK:]
    kv = (rmsnorm(c_kv, mla_kv_norm) @ w_kv_b).reshape(b, s, MLA_HEADS, MLA_NOPE + MLA_V)
    k_nope, v_mla = kv[..., :MLA_NOPE], kv[..., MLA_NOPE:]
    q_rope = apply_rope(q_rope, cos[:, :, None], sin[:, :, None])
    k_rope = apply_rope(k_rope, cos, sin)
    y_mla = mla_attention(q_nope, q_rope, k_nope, k_rope, v_mla, pos).reshape(b, s, MLA_HEADS * MLA_V)

    q_d = dq.reshape(b, s, DIFF_HEADS, 2, DIFF_HEAD_DIM)
    k_d = dk.reshape(b, s, DIFF_HEADS, 2, DIFF_HEAD_DIM)
    v_d = dv.reshape(b, s, DIFF_HEADS, DIFF_V)
    lf = diff_lambda.astype(jnp.float32)
    lam = (jnp.exp(jnp.sum(lf[0] * lf[1])) - jnp.exp(jnp.sum(lf[2] * lf[3])) + lambda_init)
    y_diff = diff_attention(q_d, k_d, v_d, pos, rel_bias, lam)
    y_diff = (rmsnorm(y_diff, diff_subln) * (1.0 - lambda_init)).reshape(b, s, DIFF_HEADS * DIFF_V)

    g = jax.nn.sigmoid(gates.astype(jnp.float32)).astype(x.dtype)
    g_mla, g_diff = g[..., :D_MODEL], g[..., D_MODEL:]
    merged = g_mla * (y_mla @ w_up_mla) + g_diff * (y_diff @ w_up_diff)
    x = x + merged @ w_out

    x = x + moe_ffn(rmsnorm(x, norm_ffn), w_router, b_router, w1, b1, w2, b2)
    return x

def setup_inputs(seed: int = 0) -> dict:
    key = jax.random.key(seed)
    ks = jax.random.split(key, 24)
    f32 = jnp.float32

    def nrm(k, shape, scale):
        return jax.random.normal(k, shape, f32) * scale

    mla_q_out = MLA_HEADS * (MLA_NOPE + MLA_ROPE)
    mla_kv_out = MLA_HEADS * (MLA_NOPE + MLA_V)
    x = jax.random.normal(ks[0], (BATCH, SEQ, D_MODEL), f32)
    offset = jax.random.randint(ks[1], (BATCH, 1), 0, 4096, dtype=jnp.int32)
    positions = (offset + jnp.arange(SEQ, dtype=jnp.int32)[None, :]).astype(jnp.int32)
    return {
        "x": x,
        "positions": positions,
        "norm_mix": 1.0 + nrm(ks[2], (DEPTH, D_MODEL), 0.02),
        "w_in": nrm(ks[3], (DEPTH, D_MODEL, IN_TOTAL), D_MODEL ** -0.5),
        "mla_q_norm": 1.0 + nrm(ks[4], (DEPTH, MLA_Q_RANK), 0.02),
        "w_q_b": nrm(ks[5], (DEPTH, MLA_Q_RANK, mla_q_out), MLA_Q_RANK ** -0.5),
        "mla_kv_norm": 1.0 + nrm(ks[6], (DEPTH, MLA_KV_RANK), 0.02),
        "w_kv_b": nrm(ks[7], (DEPTH, MLA_KV_RANK, mla_kv_out), MLA_KV_RANK ** -0.5),
        "diff_lambda": nrm(ks[8], (DEPTH, 4, DIFF_HEAD_DIM), 0.1),
        "diff_subln": 1.0 + nrm(ks[9], (DEPTH, DIFF_V), 0.02),
        "rel_bias": nrm(ks[10], (T5_BUCKETS, DIFF_HEADS), 0.5),
        "w_up_mla": nrm(ks[11], (DEPTH, MLA_HEADS * MLA_V, D_MODEL), (MLA_HEADS * MLA_V) ** -0.5),
        "w_up_diff": nrm(ks[12], (DEPTH, DIFF_HEADS * DIFF_V, D_MODEL), (DIFF_HEADS * DIFF_V) ** -0.5),
        "w_out": nrm(ks[13], (DEPTH, D_MODEL, D_MODEL), D_MODEL ** -0.5),
        "norm_ffn": 1.0 + nrm(ks[14], (DEPTH, D_MODEL), 0.02),
        "w_router": nrm(ks[15], (DEPTH, D_MODEL, N_EXPERTS), D_MODEL ** -0.5),
        "b_router": nrm(ks[16], (DEPTH, N_EXPERTS), 0.01),
        "w1": nrm(ks[17], (DEPTH, N_EXPERTS, D_MODEL, 2 * D_EXPERT), D_MODEL ** -0.5),
        "b1": nrm(ks[18], (DEPTH, N_EXPERTS, 2 * D_EXPERT), 0.02),
        "w2": nrm(ks[19], (DEPTH, N_EXPERTS, D_EXPERT, D_MODEL), D_EXPERT ** -0.5),
        "b2": nrm(ks[20], (DEPTH, N_EXPERTS, D_MODEL), 0.02),
        "norm_final": 1.0 + nrm(ks[21], (D_MODEL,), 0.02),
    }

def reference(x, positions, norm_mix, w_in, mla_q_norm, w_q_b, mla_kv_norm, w_kv_b, diff_lambda,
              diff_subln, rel_bias, w_up_mla, w_up_diff, w_out, norm_ffn, w_router, b_router,
              w1, b1, w2, b2, norm_final):
    freqs = ROPE_THETA ** (-jnp.arange(0, MLA_ROPE, 2, dtype=jnp.float32) / MLA_ROPE)
    ang = positions.astype(jnp.float32)[..., None] * freqs
    cos, sin = jnp.cos(ang).astype(x.dtype), jnp.sin(ang).astype(x.dtype)
    for l in range(DEPTH):
        lambda_init = 0.8 - 0.6 * math.exp(-0.3 * l)
        x = hybrid_layer(x, positions, cos, sin, rel_bias, lambda_init, norm_mix[l], w_in[l],
                         mla_q_norm[l], w_q_b[l], mla_kv_norm[l], w_kv_b[l], diff_lambda[l],
                         diff_subln[l], w_up_mla[l], w_up_diff[l], w_out[l], norm_ffn[l],
                         w_router[l], b_router[l], w1[l], b1[l], w2[l], b2[l])
    return rmsnorm(x, norm_final)


_drawn_inputs = setup_inputs


def setup_inputs(seed=0):
    import zlib

    import numpy as np

    out = dict(_drawn_inputs(seed))
    spreads = {}
    factors = {'mla_q_norm': 4.626,
     'mla_kv_norm': 4.683,
     'b1': 16.43,
     'b2': 18.856,
     'norm_final': 20.755,
     'diff_subln': 16.491,
     'b_router': 3.928,
     'norm_ffn': 4.101}
    for name, (base, spread) in spreads.items():
        noise = np.random.default_rng([zlib.crc32(name.encode()), seed]).standard_normal(out[name].shape)
        drawn = base * np.exp(spread * noise) if base else spread * noise
        out[name] = __import__('jax').numpy.asarray(drawn.astype(out[name].dtype))
    for name, factor in factors.items():
        out[name] = (out[name] * factor).astype(out[name].dtype)
    return out
```

```python
from contextlib import ExitStack

import numpy as np
import concourse.bass as bass
from concourse import mybir

F32 = mybir.dt.float32
I32 = mybir.dt.int32
U32 = mybir.dt.uint32
ALU = mybir.AluOpType
ACT = mybir.ActivationFunctionType
AX = mybir.AxisListType.X

P = 128
SEQ = 1024
D = 1024
KT = D // P
TT = SEQ // P
HALF = 512
EPS = 1e-5
NEG = -1e30

MLA_HEADS, NOPE, ROPE, MLA_V = 8, 64, 32, 64
Q_RANK, KV_RANK = 256, 128
HEAD_QK = NOPE + ROPE
DIFF_HEADS, DIFF_DIM, DIFF_V = 4, 64, 128
LAMBDA_INIT = 0.8 - 0.6
BUCKETS, MAX_DIST = 32, 128
MLA_SCALE = float(HEAD_QK) ** -0.5
DIFF_SCALE = float(DIFF_DIM) ** -0.5
OFF_KV = Q_RANK
OFF_KR = OFF_KV + KV_RANK
OFF_DQ = OFF_KR + ROPE
OFF_DK = OFF_DQ + DIFF_HEADS * 2 * DIFF_DIM
OFF_DV = OFF_DK + DIFF_HEADS * 2 * DIFF_DIM
OFF_GATE = OFF_DV + DIFF_HEADS * DIFF_V

EXPERTS, TOP_K, D_EXP = 32, 4, 1024
FT = D_EXP // P
LIMIT, ALPHA = 7.0, 1.702
JOB = 256
JH = JOB // P
LIST = SEQ
EXTRA_JOBS = SEQ * TOP_K // JOB
JOBS = EXPERTS + EXTRA_JOBS
WIDTHS = (64, 96, 128, 160, 192, JOB)
DUMMY = SEQ
ROWS = SEQ + JOB

HT = 0
Y_MLA = 8192
Y_DIFF = 12288
R = 16384
RING_SLOT = 4096
RING_SLOTS = 6
X_IN, H_N, SQ, W_DV = R, R + 4096, R + 6144, R + 8192
BIAS_T = R + 9216
W_PAIR = R + 8192
V_MLA, V_DIFF = R + 12288, R + 16384
QK = R + 20480
PROB, PROB_T, ROT = R, R + 4096, R + 6144
QA, CKV, COS, SIN, KR, W_ST = 40960, 43008, 44032, 45056, 46080, 47104
ARENA = 51200
Y_T, MERGED, W_MERGE, GATE_T = R, R + 8192, R + 16384, R + 22528
W_OUT, X_RES, X2, H2, H2_T = 0, 8192, 10240, 12288, 14336
W_ROUTER, B_ROUTER, LOGITS = 40960, 41216, 41248
CHOSEN, PICKED, MEMBER, EARLIER, PLACE, EXPERT_ROW, ENTRY, FILL = 41504, 42528, 43552, 43808, 44096, 44352, 44800, 44864
TRI, B_IN = 45376, 46400
XG, B1_T, B2_T, XT, EG, ACT_T, YT, YG, ENT = 0, 2048, 2560, 4096, 6144, 8192, 12288, 40960, 43008


def rel_buckets():
    n = np.maximum(255 - np.arange(383), 0)
    exact = BUCKETS // 2
    nf = np.maximum(n, 1).astype(np.float32)
    large = exact + (np.log(nf / np.float32(exact)) / np.float32(np.log(MAX_DIST / exact)) * (BUCKETS - exact)).astype(np.int32)
    b = np.where(n < exact, n, np.minimum(large, BUCKETS - 1))
    return (np.arange(BUCKETS)[:, None] == b[None, :]).astype(np.float32)


def rope_rows():
    half = np.arange(0, ROPE, 2, dtype=np.float32) / np.float32(ROPE)
    f = np.tile(np.power(np.float32(10000.0), -half), 2 * P // ROPE)
    sign = np.tile(np.repeat(np.float32([-1.0, 1.0]), ROPE // 2), P // ROPE)
    return np.stack([f, sign], axis=1).astype(np.float32)


class Core:

    def __init__(self, nc):
        self.nc = nc


class Dram:

    def __init__(self, a):
        self.x, self.positions, self.norm_mix, self.w_in = a["x"], a["positions"], a["norm_mix"], a["w_in"]
        self.mla_q_norm, self.w_q_b, self.mla_kv_norm, self.w_kv_b = a["mla_q_norm"], a["w_q_b"], a["mla_kv_norm"], a["w_kv_b"]
        self.diff_lambda, self.diff_subln, self.rel_bias = a["diff_lambda"], a["diff_subln"], a["rel_bias"]
        self.w_up_mla, self.w_up_diff, self.w_out = a["w_up_mla"], a["w_up_diff"], a["w_out"]
        self.norm_ffn, self.w_router, self.b_router = a["norm_ffn"], a["w_router"], a["b_router"]
        self.w1, self.b1, self.w2, self.b2, self.norm_final = a["w1"], a["b1"], a["w2"], a["b2"], a["norm_final"]
        self.rope_rows, self.bucket_rows = a["rope_rows"], a["bucket_rows"]
        self.out, self.acc, self.h2, self.lists = a["out"], a["acc"], a["h2"], a["lists"]


class Chain:

    def __init__(self, eng, sem, base=0):
        self.eng, self.sem, self.n = eng, sem, base

    def step(self, ins):
        ins.then_inc(self.sem, 1)
        self.n += 1
        self.eng.wait_ge(self.sem, self.n)


def setup(nc, ctx):
    g = Core(nc)
    g.sb = lambda name, shape, dt=F32: ctx.enter_context(nc.sbuf_tensor(name, shape, dt))
    g.sem = lambda name: ctx.enter_context(nc.semaphore(name))
    g.arena = g.sb("arena", [P, ARENA])
    g.banks = ctx.enter_context(nc.psum_tensor("banks", [P, 8 * HALF], F32))
    g.ident = g.sb("ident", [P, P])
    g.ones = g.sb("ones", [P, P])
    g.flip = g.sb("flip", [P, P])
    g.before = g.sb("before", [P, P])
    g.causal = g.sb("causal", [P, P])
    g.gain_mix = g.sb("gain_mix", [P, KT])
    g.gain_q = g.sb("gain_q", [P, 2])
    g.gain_kv = g.sb("gain_kv", [P, 1])
    g.gain_sub = g.sb("gain_sub", [P, 2])
    g.gain_ffn = g.sb("gain_ffn", [P, KT])
    g.eps = g.sb("eps", [P, 1])
    g.stat = g.sb("stat", [P, 32])
    g.lam = g.sb("lam", [P, 8])
    g.den = g.sb("den", [P, 64])
    g.ssq = g.sb("ssq", [P, 32])
    g.best, g.best_at = g.sb("best", [P, 8 * TT]), g.sb("best_at", [P, 8 * TT], U32)
    g.total = g.sb("total", [P, 1], I32)
    g.job_expert, g.job_place, g.job_count = (g.sb(n, [P, JOBS + 2], I32) for n in ("job_expert", "job_place", "job_count"))
    g.w_in = [g.sem(f"w_in{s}") for s in range(RING_SLOTS)]
    return g


def at(g, off, n):
    return g.arena[:, off:off + n]


def tiled(g, off, a, n):
    return g.arena[:, off:off + a * n].rearrange("p (a n) -> p a n", a=a)


def bank(g, b, n=1):
    return g.banks[:, b * HALF:(b + n) * HALF]


def stage_norm(g, io):
    nc = g.nc
    x_in = [g.sem(f"x_in{s}") for s in range(4)]
    gains_in, squared, norm_known, inverted, h_ready, turned, ht_ready = (
        g.sem(n) for n in ("gains_in", "squared", "norm_known", "inverted", "h_ready", "turned", "ht_ready"))
    filled, shaped = g.sem("filled"), g.sem("shaped")
    ht = tiled(g, HT, KT, SEQ)
    xs, hs = tiled(g, X_IN, 4, D), tiled(g, H_N, 2, D)
    total, root, inv = g.stat[:, 0:8], g.stat[:, 8:16], g.stat[:, 16:24]

    with nc.Block() as block:

        @block.sync
        def _(sp):
            for t in range(TT):
                if t >= 4:
                    sp.wait_ge(h_ready, t - 3)
                sp.dma_start(xs[:, t % 4, :], io.x[0, t * P:(t + 1) * P, :]).then_inc(x_in[t % 4], 16)

        @block.gpsimd
        def _(pool):
            for m, v in ((g.ident, 0.0), (g.ones, 1.0), (g.flip, 0.0), (g.before, 1.0), (g.causal, 0.0), (g.eps, EPS)):
                pool.memset(m[:, :], v).then_inc(filled, 1)
            pool.wait_ge(filled, 6)
            for m, op, fill, base, step, mult in (
                    (g.ident, ALU.not_equal, 1.0, 0, -1, 1),
                    (g.flip, ALU.not_equal, 1.0, -(P - 1), 1, 1),
                    (g.before, ALU.is_gt, 0.0, 0, 1, -1),
                    (g.causal, ALU.is_ge, NEG, 0, -1, 1)):
                pool.affine_select(out=m[:, :], in_=m[:, :], compare_op=op, fill=fill, base=base,
                                   pattern=[[step, P]], channel_multiplier=mult).then_inc(shaped, 1)
            pool.wait_ge(shaped, 4)

        @block.scalar
        def _(act):
            for gain, src in ((g.gain_mix, io.norm_mix), (g.gain_q, io.mla_q_norm), (g.gain_kv, io.mla_kv_norm),
                              (g.gain_sub, io.diff_subln), (g.gain_ffn, io.norm_ffn)):
                act.dma_start(gain[:, 0:src.shape[1] // P], src.rearrange("a (k p) -> (a p) k", p=P)).then_inc(gains_in, 16)
            act.wait_ge(filled, 6)
            with act.Fori(0, 2) as i:
                for s in range(4):
                    act.wait_ge(x_in[s], 16 * i + 16)
                    nc.scalar.activation(bank(g, 4 + 2 * (s % 2), 2), xs[:, s, :], ACT.Square,
                                         accum_out=total[:, bass.ds(4 * i + s, 1)]).then_inc(squared, 1)
                    act.wait_ge(squared, 4 * i + s + 1)
                    nc.scalar.activation(root[:, bass.ds(4 * i + s, 1)], total[:, bass.ds(4 * i + s, 1)], ACT.Sqrt,
                                         scale=1.0 / D, bias=g.eps[:, 0:1]).then_inc(norm_known, 1)
            act.wait_ge(gains_in, 5 * 16)

        @block.tensor
        def _(pe):
            pe.wait_ge(shaped, 4)
            with pe.Fori(0, 2) as i:
                for s in range(4):
                    pe.wait_ge(h_ready, 4 * i + s + 1)
                    for k in range(KT):
                        last = nc.tensor.transpose(bank(g, 2 * (s % 2), 2)[:, k * P:(k + 1) * P],
                                                   hs[:, s % 2, k * P:(k + 1) * P], g.ident[:, :])
                    last.then_inc(turned, 1)

        @block.vector
        def _(dve):
            dve.wait_ge(gains_in, 5 * 16)
            with dve.Fori(0, 2) as i:
                for s in range(4):
                    dve.wait_ge(norm_known, 4 * i + s + 1)
                    nc.vector.reciprocal(inv[:, bass.ds(4 * i + s, 1)], root[:, bass.ds(4 * i + s, 1)]).then_inc(inverted, 1)
                    dve.wait_ge(inverted, 4 * i + s + 1)
                    nc.vector.tensor_scalar(hs[:, s % 2, :], xs[:, s, :], inv[:, bass.ds(4 * i + s, 1)], None,
                                            ALU.mult).then_inc(h_ready, 1)
                    dve.wait_ge(turned, 4 * i + s + 1)
                    nc.vector.tensor_tensor(ht[:, :, bass.ds((4 * i + s) * P, P)],
                                            bank(g, 2 * (s % 2), 2).rearrange("p (k t) -> p k t", k=KT),
                                            g.gain_mix[:, :].unsqueeze(2).broadcast_to([P, KT, P]), ALU.mult).then_inc(ht_ready, 1)
            dve.wait_ge(ht_ready, TT)


def stage_latents(g, io):
    nc = g.nc
    w_ready = [g.sem(f"w_latent{m}") for m in range(4)]
    rows_in, wdv_in, wkv_in = g.sem("rows_in"), g.sem("wdv_in"), g.sem("wkv_in")
    projected, lat_out, lat_sq, lat_sum, lat_root, lat_done = (
        g.sem(n) for n in ("projected", "lat_out", "lat_sq", "lat_sum", "lat_root", "lat_done"))
    row_made, row_out, row_stored, row_shifted, row_flipped, bias_made, bias_masked = (
        g.sem(n) for n in ("row_made", "row_out", "row_stored", "row_shifted", "row_flipped", "bias_made", "bias_masked"))
    value_made, value_out, angles, trig, steps = (
        g.sem(n) for n in ("value_made", "value_out", "angles", "trig", "latent_steps"))
    w_v = io.w_in.rearrange("(k p) n -> p k n", p=P)
    ht = tiled(g, HT, KT, SEQ)
    wst = g.arena[:, W_ST:W_ST + 4 * SEQ].rearrange("p (s k c) -> p s k c", s=4, k=KT)
    wdv = tiled(g, W_DV, KT, HALF)
    sq = tiled(g, SQ, 2, HALF)
    root = at(g, X_IN, 2 * SEQ)
    arg_sin, arg_cos = at(g, X_IN + 2048, SEQ), at(g, X_IN + 3072, SEQ)
    pos_i, posf, angle = at(g, KR, SEQ).bitcast(I32), at(g, COS, SEQ), at(g, SIN, SEQ)
    rows = g.sb("rope_rows_sb", [P, 2])
    bias_far = g.sb("bias_far", [P, DIFF_HEADS])
    rel = at(g, QK + 3072, DIFF_HEADS)[0:BUCKETS]
    onehot = at(g, QK, 383)[0:BUCKETS]
    by_distance = at(g, QK + 512, 383)[0:DIFF_HEADS]
    shifted = tiled(g, QK + 1024, DIFF_HEADS, 256)
    lamv, lamp = at(g, QK + 2048, 256), at(g, QK + 2304, 128)
    wv = at(g, QK + 2560, HALF)
    bias_t = tiled(g, BIAS_T, DIFF_HEADS, 256)
    kr, rot = at(g, KR, SEQ)[NOPE:HEAD_QK], at(g, SQ, SEQ)[NOPE:HEAD_QK]
    toeplitz = nc.dram_tensor("bias_by_distance", (DIFF_HEADS, 384), F32).ap()

    with nc.Block() as block:

        @block.sync
        def _(sp):
            for m, col in enumerate((0, P, OFF_KV)):
                sp.dma_start(wst[:, m], w_v[:, :, col:col + P]).then_inc(w_ready[m], 16)
            half = ROPE // 2
            for to, col, n in ((0, OFF_KR, ROPE), (ROPE, OFF_KR + half, half), (ROPE + half, OFF_KR, half)):
                sp.dma_start(wst[:, 3, :, to:to + n], w_v[:, :, col:col + n]).then_inc(w_ready[3], 16)
            sp.dma_start(wdv, w_v[:, :, OFF_DV:OFF_DV + HALF]).then_inc(wdv_in, 16)
            sp.wait_ge(row_out, 1)
            sp.dma_start(toeplitz[:, 0:383], by_distance).then_inc(row_stored, 16)
            sp.wait_ge(row_stored, 16)
            for h in range(DIFF_HEADS):
                src = bass.AP(tensor=toeplitz.tensor, offset=h * 384, ap=[[1, P], [1, 256]])
                sp.dma_start(shifted[:, h, :], src).then_inc(row_shifted, 16)
            sp.wait_ge(row_shifted, 16 * DIFF_HEADS)

        @block.gpsimd
        def _(pool):
            pool.wait_ge(bias_made, DIFF_HEADS)
            for h in range(DIFF_HEADS):
                pool.affine_select(out=bias_t[:, h, P:], in_=bias_t[:, h, P:], compare_op=ALU.is_ge, fill=NEG,
                                   base=0, pattern=[[-1, P]], channel_multiplier=1).then_inc(bias_masked, 1)
            pool.wait_ge(bias_masked, DIFF_HEADS)

        @block.scalar
        def _(act):
            for out, src in ((rel, io.rel_bias), (onehot, io.bucket_rows), (pos_i, io.positions.partition_broadcast(P)),
                             (rows[:, :], io.rope_rows), (bias_far[:, :], io.rel_bias[BUCKETS - 1:BUCKETS, :].partition_broadcast(P)),
                             (lamv, io.diff_lambda.rearrange("(o a) b -> o (a b)", o=1).partition_broadcast(P))):
                act.dma_start(out, src).then_inc(rows_in, 16)
            act.dma_start(wv.rearrange("p (h c) -> p h c", c=MLA_V),
                          io.w_kv_b.rearrange("p (h c) -> p h c", c=NOPE + MLA_V)[:, :, NOPE:]).then_inc(wkv_in, 16)
            for m in range(3):
                act.wait_ge(lat_out, m + 1)
                for h in range(2):
                    if m >= 1:
                        act.wait_ge(lat_sum, 2 * m + h - 1)
                    nc.scalar.activation(sq[:, h, :], bank(g, 4 + 2 * (m % 2) + h), ACT.Square).then_inc(lat_sq, 1)
            act.wait_ge(lat_sum, 6)
            nc.scalar.activation(root[:, 0:SEQ], bank(g, 0, 2), ACT.Sqrt, scale=1.0 / Q_RANK, bias=g.eps[:, 0:1]).then_inc(lat_root, 1)
            nc.scalar.activation(root[:, SEQ:], bank(g, 2, 2), ACT.Sqrt, scale=1.0 / KV_RANK, bias=g.eps[:, 0:1]).then_inc(lat_root, 1)
            act.wait_ge(angles, 1)
            nc.scalar.activation(at(g, SIN, SEQ), arg_sin, ACT.Sin, scale=rows[:, 1:2]).then_inc(trig, 1)
            nc.scalar.activation(at(g, COS, SEQ), arg_cos, ACT.Sin).then_inc(trig, 1)

        @block.tensor
        def _(pe):
            pe.wait_ge(rows_in, 6 * 16)
            nc.tensor.matmul(bank(g, 0)[0:DIFF_HEADS, 0:383], rel, onehot, start=True, stop=True).then_inc(row_made, 1)
            pe.wait_ge(row_out, 1)
            for m in range(3):
                pe.wait_ge(w_ready[m], 16)
                if m == 2:
                    pe.wait_ge(lat_sq, 2)
                for h in range(2):
                    for k in range(KT):
                        last = nc.tensor.matmul(bank(g, 4 + 2 * (m % 2) + h), wst[:, m, k, :], ht[:, k, h * HALF:(h + 1) * HALF],
                                                start=(k == 0), stop=(k == KT - 1))
                last.then_inc(projected, 1)
                for h in range(2):
                    pe.wait_ge(lat_sq, 2 * m + h + 1)
                    nc.tensor.matmul(bank(g, (0 if m < 2 else 2) + h), g.ones[:, :], sq[:, h, :],
                                     start=(m != 1), stop=(m != 0)).then_inc(lat_sum, 1)
            pe.wait_ge(w_ready[3], 48)
            for swapped, b in ((0, 6), (1, 4)):
                for h in range(2):
                    for k in range(KT):
                        last = nc.tensor.matmul(bank(g, b + h)[NOPE:HEAD_QK, :], wst[:, 3, k, swapped * ROPE:(swapped + 1) * ROPE],
                                                ht[:, k, h * HALF:(h + 1) * HALF], start=(k == 0), stop=(k == KT - 1))
            last.then_inc(projected, 1)
            pe.wait_ge(wdv_in, 16)
            pe.wait_ge(lat_root, 2)
            for t in range(TT):
                if t >= 4:
                    pe.wait_ge(value_out, t - 3)
                for k in range(KT):
                    last = nc.tensor.matmul(bank(g, t % 4), ht[:, k, t * P:(t + 1) * P], wdv[:, k, :],
                                            start=(k == 0), stop=(k == KT - 1))
                last.then_inc(value_made, 1)
            pe.wait_ge(wkv_in, 16)
            pe.wait_ge(lat_done, 3)
            for t in range(TT):
                pe.wait_ge(value_out, t + 5)
                nc.tensor.matmul(bank(g, t % 4), at(g, CKV, SEQ)[:, t * P:(t + 1) * P], wv,
                                 start=True, stop=True).then_inc(value_made, 1)
            pe.wait_ge(row_shifted, 16 * DIFF_HEADS)
            for h in range(DIFF_HEADS):
                nc.tensor.matmul(bank(g, 4 + h % 2)[:, (h // 2) * 256:(h // 2) * 256 + 256], g.flip[:, :], shifted[:, h, :],
                                 start=True, stop=True).then_inc(row_flipped, 1)

        @block.vector
        def _(dve):
            chain = Chain(dve, steps)
            dve.wait_ge(row_made, 1)
            nc.vector.tensor_copy(by_distance, bank(g, 0)[0:DIFF_HEADS, 0:383]).then_inc(row_out, 1)
            dve.wait_ge(rows_in, 6 * 16)
            turn = 2 * np.pi
            part1 = 6.28125
            part2 = round((turn - part1) * 2 ** 21) / 2 ** 21
            part3 = turn - part1 - part2
            limit = 3.1415925
            chain.step(nc.vector.tensor_copy(posf, pos_i))
            chain.step(nc.vector.tensor_scalar(angle, posf, rows[:, 0:1], None, ALU.mult))
            turns_i, turns = at(g, H_N, SEQ).bitcast(I32), at(g, H_N + 1024, SEQ)
            for quarter, out in ((0.0, arg_sin), (0.25, arg_cos)):
                chain.step(nc.vector.tensor_scalar(turns_i, angle, 1.0 / turn, quarter, ALU.mult, ALU.add))
                chain.step(nc.vector.tensor_copy(turns, turns_i))
                src = angle
                for part in (part1, part2, part3):
                    chain.step(nc.vector.scalar_tensor_tensor(out=out, in0=turns, scalar=-float(part), in1=src, op0=ALU.mult, op1=ALU.add))
                    src = out
                chain.step(nc.vector.tensor_scalar(out, out, quarter * turn, limit, ALU.add, ALU.min))
                last = nc.vector.tensor_scalar(out, out, -limit, None, ALU.max)
                if quarter == 0.0:
                    chain.step(last)
            last.then_inc(angles, 1)
            for j in range(2):
                chain.step(nc.vector.tensor_tensor(lamp[:, j * 64:(j + 1) * 64], lamv[:, 128 * j:128 * j + 64],
                                                   lamv[:, 128 * j + 64:128 * j + 128], ALU.mult))
                chain.step(nc.vector.reduce_sum(g.lam[:, j:j + 1], lamp[:, j * 64:(j + 1) * 64], AX))
            for m in range(3):
                dve.wait_ge(projected, m + 1)
                gain = g.gain_q[:, m:m + 1] if m < 2 else g.gain_kv[:, 0:1]
                nc.vector.tensor_scalar(at(g, QA + m * SEQ, SEQ), bank(g, 4 + 2 * (m % 2), 2), gain, None, ALU.mult).then_inc(lat_out, 1)
            dve.wait_ge(lat_root, 2)
            chain.step(nc.vector.reciprocal(root, root))
            dve.wait_ge(lat_out, 3)
            for m in range(3):
                r = root[:, 0:SEQ] if m < 2 else root[:, SEQ:]
                nc.vector.tensor_tensor(at(g, QA + m * SEQ, SEQ), at(g, QA + m * SEQ, SEQ), r, ALU.mult).then_inc(lat_done, 1)
            dve.wait_ge(trig, 2)
            dve.wait_ge(projected, 4)
            chain.step(nc.vector.tensor_tensor(kr, bank(g, 6, 2)[NOPE:HEAD_QK], at(g, COS, SEQ)[NOPE:HEAD_QK], ALU.mult))
            chain.step(nc.vector.tensor_tensor(rot, bank(g, 4, 2)[NOPE:HEAD_QK], at(g, SIN, SEQ)[NOPE:HEAD_QK], ALU.mult))
            chain.step(nc.vector.tensor_tensor(kr, kr, rot, ALU.add))
            chain.step(nc.vector.tensor_scalar(kr, kr, MLA_SCALE, None, ALU.mult))
            for t in range(2 * TT):
                dve.wait_ge(value_made, t + 1)
                out = at(g, (V_DIFF if t < TT else V_MLA) + (t % TT) * HALF, HALF)
                nc.vector.tensor_copy(out, bank(g, t % 4)).then_inc(value_out, 1)
            dve.wait_ge(row_flipped, DIFF_HEADS)
            for h in range(DIFF_HEADS):
                nc.vector.tensor_scalar(bias_t[:, h, :], bank(g, 4 + h % 2)[:, (h // 2) * 256:(h // 2) * 256 + 256],
                                        bias_far[:, h:h + 1], None, ALU.subtract).then_inc(bias_made, 1)


def stage_mla(g, io):
    nc = g.nc
    w_pair, projected, qk_copied, q_rotated, rot_steps = (
        g.sem(n) for n in ("w_pair", "pair_projected", "qk_copied", "q_rotated", "rot_steps"))
    scored, masked, max_known, exped, turned0, turned1, pt_act, pt_dve, applied, inverted, y_out = (
        g.sem("mla_" + n) for n in ("scored", "masked", "max_known", "exped", "turned0", "turned1", "pt_act", "pt_dve",
                                    "applied", "inverted", "y_out"))
    UNITS, LATE = 2 * TT, TT
    qa, ckv = tiled(g, QA, 2, SEQ), at(g, CKV, SEQ)
    wq = tiled(g, W_PAIR, 2, 256)
    wk = at(g, W_PAIR + 512, P)
    q_t = [at(g, QK + (2 * j) * SEQ, SEQ) for j in range(2)]
    k_t = [at(g, QK + (2 * j + 1) * SEQ, SEQ) for j in range(2)]
    prob, prob_t, rot = tiled(g, PROB, 2, SEQ), tiled(g, PROB_T, 2, SEQ), tiled(g, ROT, 2, SEQ)
    v, y = tiled(g, V_MLA, TT, HALF), tiled(g, Y_MLA, TT, HALF)
    neg_max, total, inv = g.den[:, 0:16], g.den[:, 16:32], g.den[:, 32:48]
    wq_v = io.w_q_b.rearrange("(k p) (h c) -> p k h c", p=P, c=HEAD_QK)
    wk_v = io.w_kv_b.rearrange("p (h c) -> p h c", c=NOPE + MLA_V)
    half = ROPE // 2
    PAIR_DMAS = 9

    with nc.Block() as block:

        @block.sync
        def _(sp):
            def load_pair(hp):
                for k in range(2):
                    for to, step, col, n in ((0, NOPE, 0, NOPE), (2 * NOPE, ROPE, NOPE, ROPE),
                                             (2 * NOPE + 2 * ROPE, ROPE, NOPE + half, half),
                                             (2 * NOPE + 2 * ROPE + half, ROPE, NOPE, half)):
                        dst = wq[:, k, (to // step) * step:(to // step + 2) * step].rearrange("p (j c) -> p j c", j=2)
                        sp.dma_start(dst[:, :, to % step:to % step + n],
                                     wq_v[:, k, bass.ds(2 * hp, 2), col:col + n]).then_inc(w_pair, 16)
                sp.dma_start(wk.rearrange("p (j c) -> p j c", j=2),
                             wk_v[:, bass.ds(2 * hp, 2), 0:NOPE]).then_inc(w_pair, 16)
            load_pair(0)
            with sp.Fori(1, MLA_HEADS // 2) as hp:
                sp.wait_ge(projected, 3 * hp)
                load_pair(hp)

        @block.tensor
        def _(pe):
            with pe.Fori(0, MLA_HEADS // 2) as hp:
                base = UNITS * hp
                pe.wait_ge(w_pair, 16 * PAIR_DMAS * hp + 16 * PAIR_DMAS)
                pe.wait_ge(y_out, base + 1)
                for b, lhs in ((0, lambda k: wq[:, k, 0:P]), (2, lambda k: wq[:, k, P:2 * P])):
                    for h in range(2):
                        for k in range(2):
                            last = nc.tensor.matmul(bank(g, b + h), lhs(k), qa[:, k, h * HALF:(h + 1) * HALF],
                                                    start=(k == 0), stop=(k == 1))
                    last.then_inc(projected, 1)
                for h in range(2):
                    last = nc.tensor.matmul(bank(g, 4 + h), wk, ckv[:, h * HALF:(h + 1) * HALF], start=True, stop=True)
                last.then_inc(projected, 1)
                pe.wait_ge(qk_copied, 4 * hp + 4)
                pe.wait_ge(q_rotated, 2 * hp + 3)

                def score(u):
                    j, i = divmod(u, TT)
                    if u >= 2:
                        pe.wait_ge(exped, base + u - 1)
                    keys = (i + 1) * P
                    for c in range(0, keys, HALF):
                        n = min(HALF, keys - c)
                        last = nc.tensor.matmul(bank(g, 2 * (u % 2) + c // HALF)[:, 0:n], q_t[j][0:HEAD_QK, i * P:(i + 1) * P],
                                                k_t[j][0:HEAD_QK, c:c + n], start=True, stop=True)
                    last.then_inc(scored, 1)

                def turn(u):
                    j, i = divmod(u, TT)
                    pe.wait_ge(exped, base + u + 1)
                    for grp in range(1 + i // 4):
                        if grp == 0 and u >= 1:
                            pe.wait_ge(pt_act, base + u)
                        if grp == 1 and (j or i > 4):
                            pe.wait_ge(pt_dve, LATE * hp + 4 * j + i - 4)
                        for kt in range(4 * grp, min(4 * grp + 4, i + 1)):
                            last = nc.tensor.transpose(bank(g, 4 + grp)[:, (kt % 4) * P:(kt % 4 + 1) * P],
                                                       prob[:, u % 2, kt * P:(kt + 1) * P], g.ident[:, :])
                        last.then_inc((turned0, turned1)[grp], 1)

                def apply(u):
                    j, i = divmod(u, TT)
                    pe.wait_ge(pt_act, base + u + 1)
                    if i >= 4:
                        pe.wait_ge(pt_dve, LATE * hp + 4 * j + i - 3)
                    if u >= 2:
                        pe.wait_ge(y_out, base + u)
                    for kt in range(i + 1):
                        last = nc.tensor.matmul(bank(g, 6 + u % 2)[:, 0:MLA_V], prob_t[:, u % 2, kt * P:(kt + 1) * P],
                                                v[:, kt, bass.ds((2 * hp + j) * MLA_V, MLA_V)], start=(kt == 0), stop=(kt == i))
                    last.then_inc(applied, 1)

                score(0)
                for u in range(UNITS):
                    if u + 1 < UNITS:
                        score(u + 1)
                    turn(u)
                    if u >= 1:
                        apply(u - 1)
                apply(UNITS - 1)

        @block.vector
        def _(dve):
            nc.vector.tensor_copy(k_t[0][NOPE:HEAD_QK, :], at(g, KR, SEQ)[NOPE:HEAD_QK]).then_inc(q_rotated, 1)
            nc.vector.tensor_copy(k_t[1][NOPE:HEAD_QK, :], at(g, KR, SEQ)[NOPE:HEAD_QK]).then_inc(y_out, 1)
            with dve.Fori(0, MLA_HEADS // 2) as hp:
                base = UNITS * hp
                dve.wait_ge(projected, 3 * hp + 2)
                nc.vector.tensor_tensor(rot[0:NOPE, 0, :], bank(g, 2, 2)[0:NOPE], at(g, COS, SEQ)[0:NOPE], ALU.mult).then_inc(rot_steps, 1)
                nc.vector.tensor_tensor(rot[0:NOPE, 1, :], bank(g, 2, 2)[NOPE:P], at(g, SIN, SEQ)[NOPE:P], ALU.mult).then_inc(rot_steps, 1)
                dve.wait_ge(rot_steps, 2 * hp + 2)
                for j in range(2):
                    nc.vector.tensor_tensor(q_t[j][NOPE:HEAD_QK, :], rot[j * ROPE:(j + 1) * ROPE, 0, :],
                                            rot[j * ROPE:(j + 1) * ROPE, 1, :], ALU.add).then_inc(q_rotated, 1)

                def row_max(u):
                    i = u % TT
                    dve.wait_ge(scored, base + u + 1)
                    s = bank(g, 2 * (u % 2), 2)
                    nc.vector.tensor_tensor(s[:, i * P:(i + 1) * P], s[:, i * P:(i + 1) * P], g.causal[:, :], ALU.add).then_inc(masked, 1)
                    dve.wait_ge(masked, base + u + 1)
                    nc.vector.reduce_max(neg_max[:, u:u + 1], s[:, 0:(i + 1) * P], AX, negate=True).then_inc(max_known, 1)

                def copy_late(u):
                    j, i = divmod(u, TT)
                    if i < 4:
                        return
                    dve.wait_ge(turned1, LATE * hp + 4 * j + i - 3)
                    nc.vector.tensor_copy(prob_t[:, u % 2, HALF:(i + 1) * P], bank(g, 5)[:, 0:(i - 3) * P]).then_inc(pt_dve, 1)

                def store_y(u):
                    j, i = divmod(u, TT)
                    dve.wait_ge(applied, base + u + 1)
                    nc.vector.reciprocal(inv[:, u:u + 1], total[:, u:u + 1]).then_inc(inverted, 1)
                    dve.wait_ge(inverted, base + u + 1)
                    nc.vector.tensor_scalar(y[:, i, bass.ds((2 * hp + j) * MLA_V, MLA_V)], bank(g, 6 + u % 2)[:, 0:MLA_V],
                                            inv[:, u:u + 1], None, ALU.mult).then_inc(y_out, 1)

                row_max(0)
                for u in range(UNITS):
                    if u + 1 < UNITS:
                        row_max(u + 1)
                    copy_late(u)
                    if u >= 1:
                        store_y(u - 1)
                store_y(UNITS - 1)
            dve.wait_ge(y_out, UNITS * MLA_HEADS // 2 + 1)

        @block.scalar
        def _(act):
            with act.Fori(0, MLA_HEADS // 2) as hp:
                base = UNITS * hp
                act.wait_ge(projected, 3 * hp + 1)
                for j in range(2):
                    nc.scalar.activation(q_t[j][0:NOPE, :], bank(g, 0, 2)[j * NOPE:(j + 1) * NOPE], ACT.Copy).then_inc(qk_copied, 1)
                act.wait_ge(projected, 3 * hp + 3)
                for j in range(2):
                    nc.scalar.activation(k_t[j][0:NOPE, :], bank(g, 4, 2)[j * NOPE:(j + 1) * NOPE], ACT.Copy,
                                         scale=MLA_SCALE).then_inc(qk_copied, 1)

                def exp(u):
                    keys = (u % TT + 1) * P
                    act.wait_ge(max_known, base + u + 1)
                    nc.scalar.activation(prob[:, u % 2, 0:keys], bank(g, 2 * (u % 2), 2)[:, 0:keys], ACT.Exp,
                                         bias=neg_max[:, u:u + 1], accum_out=total[:, u:u + 1]).then_inc(exped, 1)

                def copy_early(u):
                    keys = min(HALF, (u % TT + 1) * P)
                    act.wait_ge(turned0, base + u + 1)
                    nc.scalar.activation(prob_t[:, u % 2, 0:keys], bank(g, 4)[:, 0:keys], ACT.Copy).then_inc(pt_act, 1)

                exp(0)
                for u in range(UNITS):
                    if u + 1 < UNITS:
                        exp(u + 1)
                    copy_early(u)


def stage_diff(g, io):
    nc = g.nc
    w_q, w_k, projected, q_copied, k_copied, lam_exp, lam_steps = (
        g.sem("diff_" + n) for n in ("w_q", "w_k", "projected", "q_copied", "k_copied", "lam_exp", "lam_steps"))
    scored, biased, max_known, exped, weighed, combined, turned0, turned1, pt_act, pt_dve, applied, y_out = (
        g.sem("diff_" + n) for n in ("scored", "biased", "max_known", "exped", "weighed", "combined", "turned0", "turned1",
                                     "pt_act", "pt_dve", "applied", "y_out"))
    HALVES, LATE = 2 * TT, TT // 2
    ht = tiled(g, HT, KT, SEQ)
    wst = g.arena[:, W_ST:W_ST + 2 * SEQ].rearrange("p (s k c) -> p s k c", s=2, k=KT)
    q_t, k_t = at(g, QK, SEQ), at(g, QK + SEQ, SEQ)
    prob, prob_t = tiled(g, PROB, 4, SEQ), tiled(g, PROB_T, 2, SEQ)
    v, y = tiled(g, V_DIFF, TT, HALF), tiled(g, Y_DIFF, TT, HALF)
    bias_t = tiled(g, BIAS_T, DIFF_HEADS, 256)
    neg_max, total, inv, share = g.den[:, 0:16], g.den[:, 16:32], g.den[:, 32:48], g.den[:, 48:56]
    w_v = io.w_in.rearrange("(k p) n -> p k n", p=P)

    with nc.Block() as block:

        @block.sync
        def _(sp):
            def load_head(h):
                sp.dma_start(wst[:, 0], w_v[:, :, bass.ds(OFF_DQ + P * h, P)]).then_inc(w_q, 16)
                sp.dma_start(wst[:, 1], w_v[:, :, bass.ds(OFF_DK + P * h, P)]).then_inc(w_k, 16)
            load_head(0)
            with sp.Fori(1, DIFF_HEADS) as h:
                sp.wait_ge(projected, 2 * h)
                load_head(h)

        @block.tensor
        def _(pe):
            with pe.Fori(0, DIFF_HEADS) as h:
                base, ub = HALVES * h, TT * h
                pe.wait_ge(y_out, ub + 1)
                for s, w in ((0, w_q), (1, w_k)):
                    pe.wait_ge(w, 16 * h + 16)
                    for c in range(2):
                        for k in range(KT):
                            last = nc.tensor.matmul(bank(g, 2 * s + c), wst[:, s, k, :], ht[:, k, c * HALF:(c + 1) * HALF],
                                                    start=(k == 0), stop=(k == KT - 1))
                    last.then_inc(projected, 1)
                pe.wait_ge(q_copied, h + 1)
                pe.wait_ge(k_copied, h + 1)

                def score(i):
                    keys = (i + 1) * P
                    for c in range(2):
                        s = 2 * i + c
                        if s >= 2:
                            pe.wait_ge(exped, base + s - 1)
                        rows = slice(c * DIFF_DIM, (c + 1) * DIFF_DIM)
                        for a in range(0, keys, HALF):
                            n = min(HALF, keys - a)
                            last = nc.tensor.matmul(bank(g, 2 * c + a // HALF)[:, 0:n], q_t[rows, i * P:(i + 1) * P],
                                                    k_t[rows, a:a + n], start=True, stop=True)
                        last.then_inc(scored, 1)

                def turn(i):
                    pe.wait_ge(combined, ub + i + 1)
                    for grp in range(1 + i // 4):
                        if grp == 0 and i >= 1:
                            pe.wait_ge(pt_act, ub + i)
                        if grp == 1 and i > 4:
                            pe.wait_ge(pt_dve, LATE * h + i - 4)
                        for kt in range(4 * grp, min(4 * grp + 4, i + 1)):
                            last = nc.tensor.transpose(bank(g, 4 + grp)[:, (kt % 4) * P:(kt % 4 + 1) * P],
                                                       prob[:, 2 * (i % 2), kt * P:(kt + 1) * P], g.ident[:, :])
                        last.then_inc((turned0, turned1)[grp], 1)

                def apply(i):
                    pe.wait_ge(pt_act, ub + i + 1)
                    if i >= 4:
                        pe.wait_ge(pt_dve, LATE * h + i - 3)
                    if i >= 2:
                        pe.wait_ge(y_out, ub + i)
                    for kt in range(i + 1):
                        last = nc.tensor.matmul(bank(g, 6 + i % 2)[:, 0:DIFF_V], prob_t[:, i % 2, kt * P:(kt + 1) * P],
                                                v[:, kt, bass.ds(h * DIFF_V, DIFF_V)], start=(kt == 0), stop=(kt == i))
                    last.then_inc(applied, 1)

                score(0)
                for i in range(TT):
                    if i + 1 < TT:
                        score(i + 1)
                    turn(i)
                    if i >= 1:
                        apply(i - 1)
                apply(TT - 1)

        @block.vector
        def _(dve):
            dve.wait_ge(lam_exp, 1)
            nc.vector.tensor_tensor(g.lam[:, 4:5], g.lam[:, 3:4], g.lam[:, 2:3], ALU.subtract).then_inc(lam_steps, 1)
            dve.wait_ge(lam_steps, 1)
            nc.vector.tensor_scalar(g.lam[:, 5:6], g.lam[:, 4:5], -LAMBDA_INIT, None, ALU.add).then_inc(lam_steps, 1)
            dve.wait_ge(lam_steps, 2)
            nc.vector.tensor_copy(g.lam[:, 6:7], g.lam[:, 5:6]).then_inc(y_out, 1)
            with dve.Fori(0, DIFF_HEADS) as h:
                base, ub = HALVES * h, TT * h
                dve.wait_ge(projected, 2 * h + 2)
                nc.vector.tensor_copy(k_t, bank(g, 2, 2)).then_inc(k_copied, 1)

                def row_max(i):
                    keys, near = (i + 1) * P, max(0, i - 1) * P
                    for c in range(2):
                        s = 2 * i + c
                        dve.wait_ge(scored, base + s + 1)
                        sc = bank(g, 2 * c, 2)
                        nc.vector.tensor_tensor(sc[:, near:keys], sc[:, near:keys],
                                                bias_t[:, bass.ds(h, 1), 2 * P - (keys - near):2 * P], ALU.add).then_inc(biased, 1)
                        dve.wait_ge(biased, base + s + 1)
                        nc.vector.reduce_max(neg_max[:, s:s + 1], sc[:, 0:keys], AX, negate=True).then_inc(max_known, 1)

                def combine(i):
                    dve.wait_ge(exped, base + 2 * i + 2)
                    nc.vector.reciprocal(inv[:, 2 * i:2 * i + 2], total[:, 2 * i:2 * i + 2]).then_inc(weighed, 1)
                    dve.wait_ge(weighed, 2 * (ub + i) + 1)
                    nc.vector.scalar_tensor_tensor(out=share[:, i:i + 1], in0=total[:, 2 * i:2 * i + 1], scalar=g.lam[:, 5:6],
                                                   in1=inv[:, 2 * i + 1:2 * i + 2], op0=ALU.mult, op1=ALU.mult).then_inc(weighed, 1)
                    dve.wait_ge(weighed, 2 * (ub + i) + 2)
                    keys, s = (i + 1) * P, 2 * (i % 2)
                    nc.vector.scalar_tensor_tensor(out=prob[:, s, 0:keys], in0=prob[:, s + 1, 0:keys], scalar=share[:, i:i + 1],
                                                   in1=prob[:, s, 0:keys], op0=ALU.mult, op1=ALU.add).then_inc(combined, 1)

                def copy_late(i):
                    if i < 4:
                        return
                    dve.wait_ge(turned1, LATE * h + i - 3)
                    nc.vector.tensor_copy(prob_t[:, i % 2, HALF:(i + 1) * P], bank(g, 5)[:, 0:(i - 3) * P]).then_inc(pt_dve, 1)

                def store_y(i):
                    dve.wait_ge(applied, ub + i + 1)
                    nc.vector.tensor_scalar(y[:, i, bass.ds(h * DIFF_V, DIFF_V)], bank(g, 6 + i % 2)[:, 0:DIFF_V],
                                            inv[:, 2 * i:2 * i + 1], None, ALU.mult).then_inc(y_out, 1)

                row_max(0)
                combine(0)
                for i in range(TT):
                    if i + 1 < TT:
                        row_max(i + 1)
                    copy_late(i)
                    if i + 1 < TT:
                        combine(i + 1)
                    if i >= 1:
                        store_y(i - 1)
                store_y(TT - 1)
            dve.wait_ge(y_out, TT * DIFF_HEADS + 1)

        @block.scalar
        def _(act):
            nc.scalar.activation(g.lam[:, 2:4], g.lam[:, 0:2], ACT.Exp).then_inc(lam_exp, 1)
            with act.Fori(0, DIFF_HEADS) as h:
                base, ub = HALVES * h, TT * h
                act.wait_ge(projected, 2 * h + 1)
                nc.scalar.activation(q_t, bank(g, 0, 2), ACT.Copy, scale=DIFF_SCALE).then_inc(q_copied, 1)

                def exp(i):
                    keys = (i + 1) * P
                    for c in range(2):
                        s = 2 * i + c
                        act.wait_ge(max_known, base + s + 1)
                        nc.scalar.activation(prob[:, s % 4, 0:keys], bank(g, 2 * c, 2)[:, 0:keys], ACT.Exp,
                                             bias=neg_max[:, s:s + 1], accum_out=total[:, s:s + 1]).then_inc(exped, 1)

                def copy_early(i):
                    keys = min(HALF, (i + 1) * P)
                    act.wait_ge(turned0, ub + i + 1)
                    nc.scalar.activation(prob_t[:, i % 2, 0:keys], bank(g, 4)[:, 0:keys], ACT.Copy).then_inc(pt_act, 1)

                exp(0)
                for i in range(TT):
                    if i + 1 < TT:
                        exp(i + 1)
                    copy_early(i)


def stage_merge(g, io):
    nc = g.nc
    squared, summed, rooted, inverted, normed = (g.sem("sub_" + n) for n in ("squared", "summed", "rooted", "inverted", "normed"))
    turned, copied_a, copied_d = g.sem("y_turned"), g.sem("y_copied_act"), g.sem("y_copied_dve")
    w_tile = [g.sem(f"w_merge{s}") for s in range(2)]
    made, gated, scaled, merged = (g.sem("merge_" + n) for n in ("made", "gated", "scaled", "merged"))
    ht, yt = tiled(g, HT, KT, SEQ), tiled(g, Y_T, KT, SEQ)
    y_m, y_d = tiled(g, Y_MLA, TT, HALF), tiled(g, Y_DIFF, TT, HALF)
    sq = at(g, MERGED, TT * HALF)
    out = tiled(g, MERGED, KT, SEQ)
    gate = tiled(g, GATE_T, 4, HALF)
    w = [[tiled(g, W_MERGE + 3072 * s + o, n, P) for o, n in ((0, KT), (1024, KT), (2048, 4), (2560, 4))] for s in range(2)]
    w_in = io.w_in.rearrange("(k p) n -> p k n", p=P)
    w_um, w_ud = (a.rearrange("(k p) n -> p k n", p=P) for a in (io.w_up_mla, io.w_up_diff))

    with nc.Block() as block:

        @block.sync
        def _(sp):
            def load(f, s):
                for dst, src, col in zip(w[s], (w_in, w_in, w_um, w_ud), (OFF_GATE, OFF_GATE + D, 0, 0)):
                    sp.dma_start(dst, src[:, :, bass.ds(f * P + col, P)]).then_inc(w_tile[s], 16)
            load(0, 0)
            load(1, 1)
            with sp.Fori(1, KT // 2) as i:
                for s in range(2):
                    sp.wait_ge(made, 4 * i + 2 * s - 2)
                    load(2 * i + s, s)

        @block.tensor
        def _(pe):
            for n in range(16):
                a, h = divmod(n, 2)
                src = y_m if a < 4 else y_d
                if n == 8:
                    pe.wait_ge(normed, 1)
                if n >= 8:
                    pe.wait_ge(copied_a if n % 2 == 0 else copied_d, (n - 8) // 2 + 1)
                for t in range(4):
                    last = nc.tensor.transpose(bank(g, n % 8)[:, t * P:(t + 1) * P], src[:, 4 * h + t, (a % 4) * P:(a % 4 + 1) * P], g.ident[:, :])
                last.then_inc(turned, 1)
            pe.wait_ge(copied_a, 8)
            pe.wait_ge(copied_d, 8)
            with pe.Fori(0, KT // 2) as i:
                for s in range(2):
                    pe.wait_ge(w_tile[s], 64 * i + 64)
                    for h in range(2):
                        n = 4 * i + 2 * s + h
                        pe.wait_ge(merged, n + 1)
                        cols = slice(h * HALF, (h + 1) * HALF)
                        for b, (rhs, k0, kn) in enumerate(((ht, 0, KT), (ht, 0, KT), (yt, 0, 4), (yt, 4, 4))):
                            for k in range(kn):
                                last = nc.tensor.matmul(bank(g, 4 * h + b), w[s][b][:, k, :], rhs[:, k0 + k, cols],
                                                        start=(k == 0), stop=(k == kn - 1))
                        last.then_inc(made, 1)

        @block.scalar
        def _(act):
            act.wait_ge(summed, 1)
            nc.scalar.activation(g.ssq[:, :], g.ssq[:, :], ACT.Sqrt, scale=1.0 / DIFF_V, bias=g.eps[:, 0:1]).then_inc(rooted, 1)
            for n in range(0, 16, 2):
                act.wait_ge(turned, n + 1)
                if n < 8:
                    last = nc.scalar.activation(yt[:, n // 2, 0:HALF], bank(g, n % 8), ACT.Copy)
                else:
                    last = nc.scalar.activation(yt[:, n // 2, 0:HALF], bank(g, n % 8), ACT.Copy, scale=g.gain_sub[:, 1:2])
                last.then_inc(copied_a, 1)
            with act.Fori(0, KT // 2) as i:
                for u in range(4):
                    act.wait_ge(made, 4 * i + u + 1)
                    for b in range(2):
                        nc.scalar.activation(gate[:, 2 * (u % 2) + b, :], bank(g, 4 * (u % 2) + b), ACT.Sigmoid).then_inc(gated, 1)

        @block.vector
        def _(dve):
            dve.sem_inc(merged, 2)
            nc.vector.tensor_tensor(sq, at(g, Y_DIFF, TT * HALF), at(g, Y_DIFF, TT * HALF), ALU.mult).then_inc(squared, 1)
            nc.vector.tensor_scalar(g.gain_sub[:, 1:2], g.gain_sub[:, 0:1], 1.0 - LAMBDA_INIT, None, ALU.mult).then_inc(squared, 1)
            dve.wait_ge(squared, 2)
            nc.vector.reduce_sum(g.ssq[:, :], sq.rearrange("p (a n) -> p a n", n=DIFF_V), AX).then_inc(summed, 1)
            dve.wait_ge(rooted, 1)
            nc.vector.reciprocal(g.ssq[:, :], g.ssq[:, :]).then_inc(inverted, 1)
            dve.wait_ge(inverted, 1)
            yv = at(g, Y_DIFF, TT * HALF).rearrange("p (a n) -> p a n", n=DIFF_V)
            nc.vector.tensor_tensor(yv, yv, g.ssq[:, :].unsqueeze(2).broadcast_to([P, 32, DIFF_V]), ALU.mult).then_inc(normed, 1)
            for n in range(1, 16, 2):
                dve.wait_ge(turned, n + 1)
                if n < 8:
                    last = nc.vector.tensor_copy(yt[:, n // 2, HALF:], bank(g, n % 8))
                else:
                    last = nc.vector.tensor_scalar(yt[:, n // 2, HALF:], bank(g, n % 8), g.gain_sub[:, 1:2], None, ALU.mult)
                last.then_inc(copied_d, 1)
            with dve.Fori(0, KT // 2) as i:
                for s in range(2):
                    for h in range(2):
                        n = 4 * i + 2 * s + h
                        for b in range(2):
                            dve.wait_ge(gated, 2 * n + b + 1)
                            nc.vector.tensor_tensor(gate[:, 2 * h + b, :], bank(g, 4 * h + 2 + b), gate[:, 2 * h + b, :], ALU.mult).then_inc(scaled, 1)
                        dve.wait_ge(scaled, 2 * n + 2)
                        nc.vector.tensor_tensor(out[:, bass.ds(2 * i + s, 1), h * HALF:(h + 1) * HALF], gate[:, 2 * h, :],
                                                gate[:, 2 * h + 1, :], ALU.add).then_inc(merged, 1)
            dve.wait_ge(merged, 2 * KT + 2)


def stage_out(g, io):
    nc = g.nc
    w_out_in, x_in = g.sem("w_out_in"), [g.sem(f"x_res{s}") for s in range(2)]
    router_in = g.sem("router_in")
    x2_out, h2_out = [g.sem(f"x2_out{s}") for s in range(2)], [g.sem(f"h2_out{s}") for s in range(2)]
    made, added, squared, rooted, inverted, normed, turned, h2t_ready, scored, biased, best, chosen = (
        g.sem("out_" + n) for n in ("made", "added", "squared", "rooted", "inverted", "normed", "turned", "h2t_ready",
                                    "scored", "biased", "best", "chosen"))
    w_out, merged = tiled(g, W_OUT, KT, D), tiled(g, MERGED, KT, SEQ)
    x, x2, h2 = tiled(g, X_RES, 2, D), tiled(g, X2, 2, D), tiled(g, H2, 2, D)
    h2t = g.arena[:, H2_T:H2_T + 2 * D].rearrange("p (s k t) -> p s k t", s=2, k=KT)
    w_r = tiled(g, W_ROUTER, KT, EXPERTS)
    b_r = at(g, B_ROUTER, EXPERTS)
    logits = tiled(g, LOGITS, TT, EXPERTS)
    junk = bank(g, 6, 2)
    total, root, inv = g.stat[:, 0:8], g.stat[:, 8:16], g.stat[:, 16:24]

    with nc.Block() as block:

        @block.sync
        def _(sp):
            sp.dma_start(w_out, io.w_out.rearrange("(k p) n -> p k n", p=P)).then_inc(w_out_in, 16)
            sp.dma_start(w_r, io.w_router.rearrange("(k p) n -> p k n", p=P)).then_inc(router_in, 16)
            sp.dma_start(b_r, io.b_router.partition_broadcast(P)).then_inc(router_in, 16)
            for t in range(TT):
                if t >= 2:
                    sp.wait_ge(added, t - 1)
                sp.dma_start(x[:, t % 2, :], io.x[0, t * P:(t + 1) * P, :]).then_inc(x_in[t % 2], 16)

        @block.gpsimd
        def _(pool):
            for t in range(TT):
                rows = slice(t * P, (t + 1) * P)
                pool.wait_ge(added, t + 1)
                pool.dma_start(io.acc[rows, :], x2[:, t % 2, :]).then_inc(x2_out[t % 2], 16)
                pool.wait_ge(normed, t + 1)
                pool.dma_start(io.h2[rows, :], h2[:, t % 2, :]).then_inc(h2_out[t % 2], 16)
            for s in range(2):
                pool.wait_ge(x2_out[s], 16 * TT // 2)
                pool.wait_ge(h2_out[s], 16 * TT // 2)

        @block.tensor
        def _(pe):
            pe.wait_ge(w_out_in, 16)
            pe.wait_ge(router_in, 32)

            def project(t):
                if t >= 2:
                    pe.wait_ge(added, t - 1)
                for h in range(2):
                    for k in range(KT):
                        last = nc.tensor.matmul(bank(g, 2 * (t % 2) + h), merged[:, k, t * P:(t + 1) * P], w_out[:, k, h * HALF:(h + 1) * HALF],
                                                start=(k == 0), stop=(k == KT - 1))
                last.then_inc(made, 1)

            def turn(t):
                pe.wait_ge(normed, t + 1)
                if t >= 1:
                    pe.wait_ge(h2t_ready, t)
                for k in range(KT):
                    last = nc.tensor.transpose(bank(g, 4, 2)[:, k * P:(k + 1) * P], h2[:, t % 2, k * P:(k + 1) * P], g.ident[:, :])
                last.then_inc(turned, 1)

            def route(t):
                pe.wait_ge(h2t_ready, t + 1)
                if t >= 1:
                    pe.wait_ge(biased, t)
                for k in range(KT):
                    last = nc.tensor.matmul(bank(g, 6)[:, 0:EXPERTS], h2t[:, t % 2, k, :], w_r[:, k, :], start=(k == 0), stop=(k == KT - 1))
                last.then_inc(scored, 1)

            project(0)
            for t in range(TT):
                if t + 1 < TT:
                    project(t + 1)
                turn(t)
                if t >= 1:
                    route(t - 1)
            route(TT - 1)

        @block.scalar
        def _(act):
            for t in range(TT):
                act.wait_ge(added, t + 1)
                nc.scalar.activation(h2[:, t % 2, :], x2[:, t % 2, :], ACT.Square, accum_out=total[:, t:t + 1]).then_inc(squared, 1)
                act.wait_ge(squared, t + 1)
                nc.scalar.activation(root[:, t:t + 1], total[:, t:t + 1], ACT.Sqrt, scale=1.0 / D, bias=g.eps[:, 0:1]).then_inc(rooted, 1)

        @block.vector
        def _(dve):
            def add(t):
                s = t % 2
                if t >= 2:
                    dve.wait_ge(x2_out[s], 16 * (t // 2))
                    dve.wait_ge(h2_out[s], 16 * (t // 2))
                    dve.wait_ge(turned, t - 1)
                dve.wait_ge(made, t + 1)
                dve.wait_ge(x_in[s], 16 * (t // 2) + 16)
                nc.vector.tensor_tensor(x2[:, s, :], bank(g, 2 * s, 2), x[:, s, :], ALU.add).then_inc(added, 1)

            def norm(t):
                dve.wait_ge(rooted, t + 1)
                nc.vector.reciprocal(inv[:, t:t + 1], root[:, t:t + 1]).then_inc(inverted, 1)
                dve.wait_ge(inverted, t + 1)
                nc.vector.tensor_scalar(h2[:, t % 2, :], x2[:, t % 2, :], inv[:, t:t + 1], None, ALU.mult).then_inc(normed, 1)

            def copy(t):
                dve.wait_ge(turned, t + 1)
                nc.vector.tensor_tensor(h2t[:, t % 2], bank(g, 4, 2).rearrange("p (k t) -> p k t", k=KT),
                                        g.gain_ffn[:, :].unsqueeze(2).broadcast_to([P, KT, P]), ALU.mult).then_inc(h2t_ready, 1)

            def choose(t):
                dve.wait_ge(scored, t + 1)
                nc.vector.tensor_tensor(logits[:, t, :], bank(g, 6)[:, 0:EXPERTS], b_r, ALU.add).then_inc(biased, 1)
                dve.wait_ge(biased, t + 1)
                nc.vector.max(g.best[:, 8 * t:8 * t + 8], logits[:, t, :]).then_inc(best, 1)
                dve.wait_ge(best, t + 1)
                nc.vector.max_index(g.best_at[:, 8 * t:8 * t + 8], g.best[:, 8 * t:8 * t + 8], logits[:, t, :]).then_inc(chosen, 1)

            dve.wait_ge(router_in, 32)
            add(0)
            for t in range(TT):
                norm(t)
                if t + 1 < TT:
                    add(t + 1)
                copy(t)
                if t >= 1:
                    choose(t - 1)
            choose(TT - 1)
            dve.wait_ge(chosen, TT)


def stage_route(g, io):
    nc = g.nc
    chain_s, ids, fill_out, exps, placed, counted, data_ready, listed = (
        g.sem("route_" + n) for n in ("chain", "ids", "fill_out", "exps", "placed", "counted", "data_ready", "listed"))
    shifted, m_ready, bias_in, bias_turned, zeros = (
        g.sem("route_" + n) for n in ("shifted", "m_ready", "bias_in", "bias_turned", "zeros"))
    TK = TT * TOP_K
    chosen = tiled(g, CHOSEN, TK, EXPERTS)
    picked = tiled(g, PICKED, TK, EXPERTS)
    member = tiled(g, MEMBER, TT, EXPERTS)
    earlier = tiled(g, EARLIER, TT + 1, EXPERTS)
    place = tiled(g, PLACE, TT, EXPERTS)
    expert_row, expert_i = at(g, EXPERT_ROW, EXPERTS), at(g, EXPERT_ROW + 32, EXPERTS).bitcast(I32)
    start_row = at(g, EXPERT_ROW + 64, EXPERTS)
    best_f, dest, wts = at(g, EXPERT_ROW + 96, TK), at(g, EXPERT_ROW + 128, TK), at(g, EXPERT_ROW + 160, TK)
    dest_i, sums = at(g, EXPERT_ROW + 192, TK).bitcast(I32), at(g, EXPERT_ROW + 224, TT)
    cnt, more, upto = (at(g, EXPERT_ROW + 256 + 32 * n, EXPERTS) for n in range(3))
    entry = at(g, ENTRY, 2 * TK)
    fill = at(g, FILL, 512)
    tri = tiled(g, TRI, EXPERTS, EXPERTS)
    tri2, past = tiled(g, CHOSEN, EXPERTS, EXPERTS), tiled(g, PICKED, EXTRA_JOBS, EXPERTS)
    past2 = tiled(g, PICKED + 512, EXTRA_JOBS, EXPERTS)
    job_no, job_e, job_d = (at(g, EXPERT_ROW + 352 + 16 * n, EXTRA_JOBS) for n in range(3))
    b1_in, b2_in = at(g, B_IN, 2 * D_EXP)[0:EXPERTS], at(g, B_IN + 2 * D_EXP, D)[0:EXPERTS]
    b1_t, b2_t = tiled(g, B1_T, EXPERTS, 2 * FT), tiled(g, B2_T, EXPERTS, KT)
    zero = at(g, H2_T, D)

    with nc.Block() as block:

        @block.gpsimd
        def _(pool):
            pool.iota(expert_i, pattern=[[1, EXPERTS]], base=0, channel_multiplier=0).then_inc(ids, 1)
            pool.iota(entry.bitcast(I32).rearrange("p (n c) -> p n c", c=2)[:, :, 0:1].rearrange("p (t k) c -> p t (k c)", t=TT),
                      pattern=[[P, TT], [0, TOP_K]], base=0, channel_multiplier=1).then_inc(ids, 1)
            pool.memset(fill, 0.0).then_inc(ids, 1)
            pool.memset(tri, 1.0).then_inc(ids, 1)
            pool.memset(zero, 0.0).then_inc(ids, 1)
            pool.iota(job_no.bitcast(I32), pattern=[[1, EXTRA_JOBS]], base=0, channel_multiplier=0).then_inc(ids, 1)
            pool.wait_ge(ids, 6)
            pool.iota(fill.bitcast(I32).rearrange("p (n c) -> p n c", c=2)[:, :, 0], pattern=[[1, 256]],
                      base=DUMMY, channel_multiplier=0).then_inc(ids, 1)
            pool.affine_select(out=tri, in_=tri, compare_op=ALU.is_ge, fill=0.0, base=0,
                               pattern=[[1, EXPERTS], [-1, EXPERTS]], channel_multiplier=0).then_inc(ids, 1)
            pool.wait_ge(ids, 8)
            pool.dma_start(io.lists.rearrange("(p n) c -> p (n c)", p=P), fill).then_inc(fill_out, 16)
            for r in range(DUMMY, ROWS, P):
                pool.dma_start(io.h2[r:r + P, :], zero).then_inc(zeros, 16)
                pool.dma_start(io.acc[r:r + P, :], zero).then_inc(zeros, 16)
            pool.wait_ge(fill_out, 16)
            pool.wait_ge(data_ready, 1)
            for n in range(TK):
                pool.indirect_dma_start(out=io.lists, out_offset=bass.IndirectOffsetOnAxis(ap=dest_i[:, n:n + 1], axis=0),
                                        in_=entry[:, 2 * n:2 * n + 2], in_offset=None,
                                        bounds_check=EXPERTS * LIST - 1, oob_is_err=True).then_inc(listed, 16)
            pool.wait_ge(listed, 16 * TK)
            pool.wait_ge(zeros, 16 * 2 * JH)

        @block.sync
        def _(sp):
            sp.dma_start(b1_in, io.b1).then_inc(bias_in, 16)
            sp.dma_start(b2_in, io.b2).then_inc(bias_in, 16)
            for slot in range(6):
                load_weights(g, io, sp, 0, slot)

        @block.tensor
        def _(pe):
            pe.wait_ge(bias_in, 32)
            for f in range(3 * FT):
                src = b1_in[:, f * P:(f + 1) * P] if f < 2 * FT else b2_in[:, (f - 2 * FT) * P:(f - 2 * FT + 1) * P]
                last = nc.tensor.transpose(bank(g, 2 + f // 16)[:, (f % 16) * EXPERTS:(f % 16 + 1) * EXPERTS], src, g.ident[0:EXPERTS, 0:EXPERTS])
            last.then_inc(bias_turned, 1)
            pe.wait_ge(m_ready, 1)
            for t in range(TT):
                nc.tensor.matmul(bank(g, 0)[:, t * EXPERTS:(t + 1) * EXPERTS], g.before[:, :], member[:, t, :], start=True, stop=False)
                last = nc.tensor.matmul(bank(g, 0)[:, t * EXPERTS:(t + 1) * EXPERTS], g.ones[:, :], earlier[:, t, :], start=False, stop=True)
            last.then_inc(placed, 1)
            nc.tensor.matmul(bank(g, 1)[:, 0:EXPERTS], g.ones[:, :], earlier[:, TT, :], start=True, stop=True).then_inc(counted, 1)

        @block.scalar
        def _(act):
            act.wait_ge(shifted, 1)
            nc.scalar.activation(wts, wts, ACT.Exp).then_inc(exps, 1)

        @block.vector
        def _(dve):
            chain = Chain(dve, chain_s)
            best = g.best[:, :].rearrange("p (t k) -> p t k", t=TT)
            best_at = g.best_at[:, :].rearrange("p (t k) -> p t k", t=TT)
            wv = wts.rearrange("p (t k) -> p t k", t=TT)
            nc.vector.tensor_tensor(wv, best[:, :, 0:TOP_K], best[:, :, 0:1].broadcast_to([P, TT, TOP_K]), ALU.subtract).then_inc(shifted, 1)
            dve.wait_ge(ids, 8)
            chain.step(nc.vector.tensor_copy(expert_row, expert_i))
            chain.step(nc.vector.tensor_copy(best_f.rearrange("p (t k) -> p t k", t=TT), best_at[:, :, 0:TOP_K]))
            chain.step(nc.vector.tensor_scalar(start_row, expert_row, float(LIST), None, ALU.mult))
            chain.step(nc.vector.tensor_tensor(chosen, expert_row.unsqueeze(1).broadcast_to([P, TK, EXPERTS]),
                                               best_f.unsqueeze(2).broadcast_to([P, TK, EXPERTS]), ALU.is_equal))
            chain.step(nc.vector.reduce_sum(member, chosen.rearrange("p (t k) e -> p t e k", t=TT), AX))
            chain.step(nc.vector.memset(earlier[:, 0, :], 0.0))
            for t in range(TT):
                chain.step(nc.vector.tensor_tensor(earlier[:, t + 1, :], earlier[:, t, :], member[:, t, :], ALU.add))
            nc.vector.tensor_copy(g.stat[:, 0:1], g.eps[:, :]).then_inc(m_ready, 1)
            dve.wait_ge(exps, 1)
            chain.step(nc.vector.reduce_sum(sums, wv, AX))
            chain.step(nc.vector.reciprocal(sums, sums))
            chain.step(nc.vector.tensor_tensor(entry.rearrange("p (t k c) -> p t k c", t=TT, c=2)[:, :, :, 1], wv,
                                               sums.unsqueeze(2).broadcast_to([P, TT, TOP_K]), ALU.mult))
            dve.wait_ge(placed, 1)
            chain.step(nc.vector.tensor_tensor(place, bank(g, 0)[:, 0:TT * EXPERTS].rearrange("p (t e) -> p t e", t=TT),
                                               start_row.unsqueeze(1).broadcast_to([P, TT, EXPERTS]), ALU.add))
            for k in range(TOP_K):
                view = lambda a: a.rearrange("p (t k) e -> p t k e", t=TT)[:, :, k, :]
                chain.step(nc.vector.tensor_tensor(view(picked), view(chosen), place, ALU.mult))
            chain.step(nc.vector.reduce_sum(dest, picked, AX))
            nc.vector.tensor_copy(dest_i, dest).then_inc(data_ready, 1)
            dve.wait_ge(counted, 1)
            chain.step(nc.vector.tensor_copy(cnt, bank(g, 1)[:, 0:EXPERTS]))
            chain.step(nc.vector.tensor_copy(g.job_count[:, 0:EXPERTS], cnt))
            chain.step(nc.vector.memset(g.job_count[:, EXPERTS:], JOB))
            chain.step(nc.vector.tensor_scalar(more, cnt, float(JOB), None, ALU.is_gt))
            for j in range(2, LIST // JOB):
                chain.step(nc.vector.scalar_tensor_tensor(out=more, in0=cnt, scalar=float(JOB * j), in1=more, op0=ALU.is_gt, op1=ALU.add))
            chain.step(nc.vector.tensor_tensor(tri2, tri, more.unsqueeze(1).broadcast_to([P, EXPERTS, EXPERTS]), ALU.mult))
            chain.step(nc.vector.reduce_sum(upto, tri2, AX))
            chain.step(nc.vector.tensor_scalar(g.total[:, 0:1], upto[:, EXPERTS - 1:EXPERTS], float(EXPERTS), None, ALU.add))
            chain.step(nc.vector.tensor_copy(job_e, job_no.bitcast(I32)))
            chain.step(nc.vector.tensor_tensor(past, job_e.unsqueeze(2).broadcast_to([P, EXTRA_JOBS, EXPERTS]),
                                               upto.unsqueeze(1).broadcast_to([P, EXTRA_JOBS, EXPERTS]), ALU.is_ge))
            chain.step(nc.vector.tensor_tensor(past2, past, more.unsqueeze(1).broadcast_to([P, EXTRA_JOBS, EXPERTS]), ALU.mult))
            chain.step(nc.vector.reduce_sum(job_d, past2, AX))
            chain.step(nc.vector.tensor_tensor(job_d, job_e, job_d, ALU.subtract))
            chain.step(nc.vector.tensor_scalar(job_d, job_d, 1.0, None, ALU.add))
            chain.step(nc.vector.reduce_sum(job_e, past, AX))
            chain.step(nc.vector.tensor_scalar(job_e, job_e, float(EXPERTS - 1), None, ALU.min))
            chain.step(nc.vector.tensor_copy(g.job_expert[:, 0:EXPERTS], expert_row))
            chain.step(nc.vector.tensor_copy(g.job_expert[:, EXPERTS:JOBS], job_e))
            chain.step(nc.vector.scalar_tensor_tensor(out=job_d, in0=job_e, scalar=float(LIST // JOB), in1=job_d, op0=ALU.mult, op1=ALU.add))
            chain.step(nc.vector.tensor_scalar(g.job_place[:, EXPERTS:JOBS], job_d, float(EXPERTS * LIST // JOB - 1), None, ALU.min))
            chain.step(nc.vector.tensor_scalar(g.job_place[:, 0:EXPERTS], expert_row, float(LIST // JOB), None, ALU.mult))
            chain.step(nc.vector.memset(g.job_place[:, JOBS:], 0))
            dve.wait_ge(bias_turned, 1)
            src = bank(g, 2)[:, :].rearrange("p (f e) -> p e f", e=EXPERTS)
            chain.step(nc.vector.tensor_copy(b1_t[:, :, 0:FT], src[:, :, 0:FT]))
            chain.step(nc.vector.tensor_scalar(b1_t[:, :, FT:], src[:, :, FT:], 1.0, None, ALU.add))
            chain.step(nc.vector.tensor_copy(b2_t, bank(g, 3)[:, 0:KT * EXPERTS].rearrange("p (f e) -> p e f", e=EXPERTS)))
            chain.step(nc.vector.memset(bank(g, 0, 8), 0.0))


def weight_slots(g):
    return ([g.arena[:, R + c * RING_SLOT:R + (c + 1) * RING_SLOT].rearrange("p (s k n) -> p s k n", s=2, k=KT) for c in range(4)],
            [tiled(g, R + (4 + c) * RING_SLOT, FT, HALF) for c in range(2)])


def load_weights(g, io, eng, expert, slot):
    w1, w2 = weight_slots(g)
    if slot < 4:
        src = io.w1.rearrange("e (k p) n -> p e k n", p=P)
        for s in range(2):
            col = s * D_EXP + slot * 2 * P
            eng.dma_start(w1[slot][:, s].unsqueeze(1), src[:, bass.ds(expert, 1), :, col:col + 2 * P]).then_inc(g.w_in[slot], 16)
    else:
        src = io.w2.rearrange("e (k p) n -> p e k n", p=P)
        col = (slot - 4) * HALF
        eng.dma_start(w2[slot - 4].unsqueeze(1), src[:, bass.ds(expert, 1), :, col:col + HALF]).then_inc(g.w_in[slot], 16)


def stage_experts(g, io):
    nc = g.nc
    ent_in, gathered, scattered, x_turned, xt_dve, xt_act = (
        g.sem("moe_" + n) for n in ("ent_in", "gathered", "scattered", "x_turned", "xt_dve", "xt_act"))
    rows_known, yg_free, issued = g.sem("moe_rows_known"), g.sem("moe_yg_free"), g.sem("moe_issued")
    made, g_ready, l_ready, s_ready, gs_ready, act_ready = (
        g.sem("moe_" + n) for n in ("made", "g_ready", "l_ready", "s_ready", "gs_ready", "act_ready"))
    y_made, y_biased, y_turned, yg_dve, yg_act = (g.sem("moe_" + n) for n in ("y_made", "y_biased", "y_turned", "yg_dve", "yg_act"))
    w1, w2 = weight_slots(g)
    xg, yg = tiled(g, XG, JH, D), tiled(g, YG, JH, D)
    xt, act_t, yt = tiled(g, XT, KT, JOB), tiled(g, ACT_T, FT, JOB), tiled(g, YT, KT, JOB)
    glu, sig, lin = at(g, EG, HALF), at(g, EG + HALF, HALF), at(g, EG + 2 * HALF, HALF)
    ent = g.arena[:, ENT:ENT + (JOBS + 2) * 2 * JH].rearrange("p (n h c) -> p n h c", h=JH, c=2)
    b1_t, b2_t = tiled(g, B1_T, EXPERTS, 2 * FT), tiled(g, B2_T, EXPERTS, KT)
    rows_in, rows_out = (at(g, ENT + (JOBS + 2) * 2 * JH + JH * s, JH).bitcast(I32) for s in range(2))
    weight = lambda n, h: g.arena[:, bass.ds(2 * JH * n + (ENT + 2 * h + 1), 1)]
    entries = io.lists.rearrange("(n h p) c -> p n h c", p=P, h=JH)

    with nc.Block() as block:

        @block.sync
        def _(sp):
            total = sp.value_load(g.total[0:1, 0:1], min_val=EXPERTS, max_val=JOBS)
            with sp.Fori(1, JOBS) as n:
                with sp.If(total > n):
                    expert = sp.value_load(g.job_expert[0:1, bass.ds(n, 1)], min_val=0, max_val=EXPERTS - 1)
                    for c in range(6):
                        if c < 4:
                            sp.wait_ge(made, 8 * n + (2 * c - 6))
                        else:
                            sp.wait_ge(y_made, 4 * n + (2 * c - 10))
                        load_weights(g, io, sp, expert, c)
                with sp.Else():
                    sp.nop()

        @block.gpsimd
        def _(pool):
            def load_entries(n):
                place = pool.value_load(g.job_place[0:1, bass.ds(n, 1)], min_val=0, max_val=EXPERTS * LIST // JOB - 1)
                pool.dma_start(ent[:, bass.ds(n, 1)], entries[:, bass.ds(place, 1)]).then_inc(ent_in, 16)

            def gather(n, seen):
                nc.gpsimd.tensor_copy(rows_in, ent.bitcast(I32)[:, bass.ds(n, 1), :, 0]).then_inc(rows_known, 1)
                pool.wait_ge(rows_known, seen)
                pool.sem_inc(issued, 1)
                for h in range(JH):
                    pool.indirect_dma_start(out=xg[:, h, :], out_offset=None, in_=io.h2,
                                            in_offset=bass.IndirectOffsetOnAxis(ap=rows_in[:, h:h + 1], axis=0),
                                            bounds_check=ROWS - 1, oob_is_err=True).then_inc(gathered, 16)

            pool.sem_inc(yg_free, 1)
            load_entries(0)
            pool.wait_ge(ent_in, 16)
            gather(0, 1)
            load_entries(1)
            total = pool.value_load(g.total[0:1, 0:1], min_val=EXPERTS, max_val=JOBS)
            with pool.Fori(0, JOBS) as n:
                with pool.If(total > n):
                    pool.wait_ge(ent_in, 16 * n + 32)
                    pool.wait_ge(x_turned, 4 * n + 4)
                    gather(n + 1, 2 * n + 2)
                    load_entries(n + 2)
                    pool.wait_ge(yg_dve, n + 2)
                    pool.wait_ge(yg_act, n + 2)
                    nc.gpsimd.tensor_copy(rows_out, ent.bitcast(I32)[:, bass.ds(n, 1), :, 0]).then_inc(rows_known, 1)
                    pool.wait_ge(rows_known, 2 * n + 3)
                    pool.sem_inc(issued, 1)
                    for h in range(JH):
                        pool.indirect_dma_start(out=io.acc, out_offset=bass.IndirectOffsetOnAxis(ap=rows_out[:, h:h + 1], axis=0),
                                                in_=yg[:, h, :], in_offset=None, compute_op=ALU.add,
                                                bounds_check=ROWS - 1, oob_is_err=True).then_inc(scattered, 16)
                    pool.wait_ge(scattered, 32 * n + 32)
                    pool.sem_inc(yg_free, 1)
                with pool.Else():
                    pool.nop()
            pool.wait_ge(ent_in, 16 * total + 32)

        @block.tensor
        def _(pe):
            def turn_x(halves):
                for k in range(KT):
                    for h in range(halves):
                        last = nc.tensor.transpose(bank(g, 4 + k // 2)[:, (k % 2) * JOB + h * P:(k % 2) * JOB + (h + 1) * P],
                                                   xg[:, h, k * P:(k + 1) * P], g.ident[:, :])
                    if k % 2 == 1:
                        last.then_inc(x_turned, 1)

            def job(n, width, next_count):
                pe.wait_ge(xt_dve, 2 * n + 2)
                pe.wait_ge(xt_act, 4 * n + 4)
                for c in range(4):
                    pe.wait_ge(g.w_in[c], 32 * n + 32)
                    if c >= 2:
                        pe.wait_ge(act_ready, 4 * n + (c - 1))
                    for s in range(2):
                        for a in range(2):
                            for k in range(KT):
                                last = nc.tensor.matmul(bank(g, 2 * (c % 2) + s)[:, a * JOB:a * JOB + width], w1[c][:, s, k, a * P:(a + 1) * P],
                                                        xt[:, k, 0:width], start=(k == 0), stop=(k == KT - 1))
                        last.then_inc(made, 1)
                pe.wait_ge(gathered, 32 * n + 64)
                pe.wait_ge(yg_dve, n + 1)
                pe.wait_ge(yg_act, n + 1)
                with pe.If(next_count > P):
                    turn_x(2)
                with pe.Else():
                    turn_x(1)

                def second(d, fs):
                    for f in fs:
                        last = nc.tensor.matmul(bank(g, d // 2)[:, (d % 2) * JOB:(d % 2) * JOB + width], w2[d // 4][:, f, (d % 4) * P:(d % 4 + 1) * P],
                                                act_t[:, f, 0:width], start=(f == 0), stop=(f == FT - 1))
                    return last
                pe.wait_ge(act_ready, 4 * n + 3)
                pe.wait_ge(g.w_in[4], 16 * n + 16)
                for d in (0, 2):
                    second(d, range(6))
                pe.wait_ge(act_ready, 4 * n + 4)
                for d in (0, 2):
                    last = second(d, range(6, FT))
                    last = second(d + 1, range(FT))
                    last.then_inc(y_made, 1)
                pe.wait_ge(g.w_in[5], 16 * n + 16)
                for d in range(4, KT):
                    last = second(d, range(FT))
                    if d % 2 == 1:
                        last.then_inc(y_made, 1)
                pe.wait_ge(xt_dve, 2 * n + 4)
                pe.wait_ge(xt_act, 4 * n + 8)
                for b in range(4):
                    pe.wait_ge(y_biased, 4 * n + b + 1)
                    for d in (2 * b, 2 * b + 1):
                        for h in range(1 if width <= P else 2):
                            last = nc.tensor.transpose(bank(g, 4 + 2 * h, 2)[:, d * P:(d + 1) * P], yt[:, d, h * P:(h + 1) * P], g.ident[:, :])
                last.then_inc(y_turned, 1)

            def by_count(n, widths, count, next_count):
                if len(widths) == 1:
                    job(n, widths[0], next_count)
                    return
                with pe.If(count > widths[0]):
                    by_count(n, widths[1:], count, next_count)
                with pe.Else():
                    job(n, widths[0], next_count)

            pe.wait_ge(gathered, 32)
            turn_x(2)
            total = pe.value_load(g.total[0:1, 0:1], min_val=EXPERTS, max_val=JOBS)
            with pe.Fori(0, JOBS) as n:
                with pe.If(total > n):
                    count = pe.value_load(g.job_count[0:1, bass.ds(n, 1)], min_val=0, max_val=SEQ)
                    next_count = pe.value_load(g.job_count[0:1, bass.ds(n + 1, 1)], min_val=0, max_val=SEQ)
                    by_count(n, WIDTHS, count, next_count)
                with pe.Else():
                    pe.nop()

        @block.scalar
        def _(act):
            def take_x(n):
                for k in range(KT // 2, KT):
                    if k % 2 == 0:
                        act.wait_ge(x_turned, 4 * n + k // 2 + 1)
                    nc.scalar.activation(xt[:, k, :], bank(g, 4 + k // 2)[:, (k % 2) * JOB:(k % 2 + 1) * JOB], ACT.Copy,
                                         scale=g.gain_ffn[:, k:k + 1]).then_inc(xt_act, 1)

            act.sem_inc(yg_act, 1)
            take_x(0)
            total = act.value_load(g.total[0:1, 0:1], min_val=EXPERTS, max_val=JOBS)
            with act.Fori(0, JOBS) as n:
                with act.If(total > n):
                    for c in range(4):
                        act.wait_ge(g_ready, 8 * n + 2 * c + 2)
                        nc.scalar.activation(sig, glu, ACT.Sigmoid, scale=ALPHA).then_inc(s_ready, 1)
                    take_x(n + 1)
                    act.wait_ge(y_turned, n + 1)
                    act.wait_ge(yg_free, n + 1)
                    nc.scalar.activation(yg[:, 1, :], bank(g, 6, 2), ACT.Copy, scale=weight(n, 1)).then_inc(yg_act, 1)
                with act.Else():
                    act.nop()

        @block.vector
        def _(dve):
            def take_x(n):
                for b in range(2):
                    dve.wait_ge(x_turned, 4 * n + b + 1)
                    nc.vector.tensor_tensor(xt[:, 2 * b:2 * b + 2, :], bank(g, 4 + b).rearrange("p (k t) -> p k t", k=2),
                                            g.gain_ffn[:, 2 * b:2 * b + 2].unsqueeze(2).broadcast_to([P, 2, JOB]), ALU.mult).then_inc(xt_dve, 1)

            dve.sem_inc(yg_dve, 1)
            take_x(0)
            total = dve.value_load(g.total[0:1, 0:1], min_val=EXPERTS, max_val=JOBS)
            with dve.Fori(0, JOBS) as n:
                with dve.If(total > n):
                    expert = dve.value_load(g.job_expert[0:1, bass.ds(n, 1)], min_val=0, max_val=EXPERTS - 1)
                    for c in range(4):
                        for s, (dst, ready, limit) in enumerate(((glu, g_ready, LIMIT), (lin, l_ready, LIMIT + 1.0))):
                            dve.wait_ge(made, 8 * n + 2 * c + s + 1)
                            for a in range(2):
                                nc.vector.tensor_scalar(dst[:, a * JOB:(a + 1) * JOB], bank(g, 2 * (c % 2) + s)[:, a * JOB:(a + 1) * JOB],
                                                        b1_t[:, bass.ds(expert, 1), s * FT + 2 * c + a], limit, ALU.add, ALU.min).then_inc(ready, 1)
                        dve.wait_ge(s_ready, 4 * n + c + 1)
                        dve.wait_ge(g_ready, 8 * n + 2 * c + 2)
                        nc.vector.tensor_tensor(sig, glu, sig, ALU.mult).then_inc(gs_ready, 1)
                        dve.wait_ge(gs_ready, 4 * n + c + 1)
                        dve.wait_ge(l_ready, 8 * n + 2 * c + 2)
                        nc.vector.scalar_tensor_tensor(out=at(g, ACT_T + 2 * c * JOB, 2 * JOB), in0=lin, scalar=1.0 - LIMIT, in1=sig,
                                                       op0=ALU.max, op1=ALU.mult).then_inc(act_ready, 1)
                        dve.wait_ge(act_ready, 4 * n + c + 1)
                    take_x(n + 1)
                    for b in range(4):
                        dve.wait_ge(y_made, 4 * n + b + 1)
                        nc.vector.tensor_tensor(yt[:, 2 * b:2 * b + 2, :], bank(g, b).rearrange("p (k t) -> p k t", k=2),
                                                b2_t[:, bass.ds(expert, 1), 2 * b:2 * b + 2].rearrange("p o k -> p (o k)").unsqueeze(2).broadcast_to([P, 2, JOB]),
                                                ALU.add).then_inc(y_biased, 1)
                    dve.wait_ge(y_turned, n + 1)
                    dve.wait_ge(yg_free, n + 1)
                    nc.vector.tensor_scalar(yg[:, 0, :], bank(g, 4, 2), weight(n, 0), None, ALU.mult).then_inc(yg_dve, 1)
                with dve.Else():
                    dve.nop()


def stage_final(g, io):
    nc = g.nc
    gain_in, rows_in = g.sem("final_gain_in"), [g.sem(f"final_in{s}") for s in range(TT // 2)]
    squared, rooted, inverted, normed, stored = (g.sem("final_" + n) for n in ("squared", "rooted", "inverted", "normed", "stored"))
    x, gain, y = tiled(g, 0, TT, D), at(g, TT * D, D), tiled(g, (TT + 1) * D, TT, D)
    total, root, inv = g.stat[:, 0:8], g.stat[:, 8:16], g.stat[:, 16:24]

    with nc.Block() as block:

        @block.sync
        def _(sp):
            sp.dma_start(gain, io.norm_final.partition_broadcast(P)).then_inc(gain_in, 16)
            for s in range(TT // 2):
                sp.dma_start(x[:, 2 * s:2 * s + 2, :], io.acc[2 * s * P:(2 * s + 2) * P, :].rearrange("(t p) d -> p t d", p=P)).then_inc(rows_in[s], 16)

        @block.gpsimd
        def _(pool):
            for t in range(TT):
                pool.wait_ge(normed, t + 1)
                pool.dma_start(io.out[0, t * P:(t + 1) * P, :], y[:, t, :]).then_inc(stored, 16)
            pool.wait_ge(stored, 16 * TT)

        @block.scalar
        def _(act):
            for t in range(TT):
                act.wait_ge(rows_in[t // 2], 16)
                nc.scalar.activation(y[:, t, :], x[:, t, :], ACT.Square, accum_out=total[:, t:t + 1]).then_inc(squared, 1)
                act.wait_ge(squared, t + 1)
                nc.scalar.activation(root[:, t:t + 1], total[:, t:t + 1], ACT.Sqrt, scale=1.0 / D, bias=g.eps[:, 0:1]).then_inc(rooted, 1)

        @block.vector
        def _(dve):
            dve.wait_ge(gain_in, 16)
            for t in range(TT):
                dve.wait_ge(rooted, t + 1)
                nc.vector.reciprocal(inv[:, t:t + 1], root[:, t:t + 1]).then_inc(inverted, 1)
                dve.wait_ge(inverted, t + 1)
                nc.vector.scalar_tensor_tensor(out=y[:, t, :], in0=x[:, t, :], scalar=inv[:, t:t + 1], in1=gain,
                                               op0=ALU.mult, op1=ALU.mult).then_inc(normed, 1)


STAGES = [stage_norm, stage_latents, stage_mla, stage_diff, stage_merge, stage_out, stage_route, stage_experts, stage_final]


def program(nc, io):
    ctx = ExitStack()
    with ctx, nc.allow_non_contiguous_dma(reason="columns of gains and biases: a few KiB"):
        g = setup(nc, ctx)
        for stage in STAGES:
            stage(g, io)


_INS = ['x', 'positions', 'norm_mix', 'w_in', 'mla_q_norm', 'w_q_b', 'mla_kv_norm', 'w_kv_b', 'diff_lambda', 'diff_subln',
        'rel_bias', 'w_up_mla', 'w_up_diff', 'w_out', 'norm_ffn', 'w_router', 'b_router', 'w1', 'b1', 'w2', 'b2', 'norm_final']


def kernel(**inputs):
    import numpy as _np
    import concourse.bacc as _bacc
    from concourse import mybir as _mybir
    from concourse.bass_utils import run_bass_kernel_spmd as _run

    nc = _bacc.Bacc("TRN2", target_bir_lowering=False, num_devices=1)
    arrays, dram = {}, {}
    given = {name: inputs[name] for name in _INS} | {"rope_rows": rope_rows(), "bucket_rows": rel_buckets()}
    for name, a in given.items():
        a = _np.ascontiguousarray(a)
        if a.ndim > 1 and a.shape[0] == 1 and name not in ("x", "positions"):
            a = a.reshape(a.shape[1:])
        if a.ndim == 1:
            a = a.reshape(1, -1)
        arrays[f"in_{name}"] = a
        dram[name] = nc.dram_tensor(f"in_{name}", a.shape, _mybir.dt.from_np(a.dtype), kind="ExternalInput").ap()
    dram['out'] = nc.dram_tensor("out_0", (1, SEQ, D), _mybir.dt.float32, kind="ExternalOutput").ap()
    dram['acc'] = nc.dram_tensor("acc_rows", (ROWS, D), F32).ap()
    dram['h2'] = nc.dram_tensor("h2_rows", (ROWS, D), F32).ap()
    dram['lists'] = nc.dram_tensor("lists", (EXPERTS * LIST, 2), F32).ap()
    program(nc, Dram(dram))
    r = _run(nc, [arrays], core_ids=[0])
    return r.results[0]["out_0"]
```

```python
from contextlib import ExitStack

import numpy as np
import concourse.bass as bass
from concourse import mybir

F32 = mybir.dt.float32
I32 = mybir.dt.int32
U32 = mybir.dt.uint32
ALU = mybir.AluOpType
ACT = mybir.ActivationFunctionType
AX = mybir.AxisListType.X

P = 128
SEQ = 1024
D = 1024
KT = D // P
TT = SEQ // P
HALF = 512
EPS = 1e-5
NEG = -1e30

MLA_HEADS, NOPE, ROPE, MLA_V = 8, 64, 32, 64
Q_RANK, KV_RANK = 256, 128
HEAD_QK = NOPE + ROPE
DIFF_HEADS, DIFF_DIM, DIFF_V = 4, 64, 128
LAMBDA_INIT = 0.8 - 0.6
BUCKETS, MAX_DIST = 32, 128
MLA_SCALE = float(HEAD_QK) ** -0.5
DIFF_SCALE = float(DIFF_DIM) ** -0.5
OFF_KV = Q_RANK
OFF_KR = OFF_KV + KV_RANK
OFF_DQ = OFF_KR + ROPE
OFF_DK = OFF_DQ + DIFF_HEADS * 2 * DIFF_DIM
OFF_DV = OFF_DK + DIFF_HEADS * 2 * DIFF_DIM
OFF_GATE = OFF_DV + DIFF_HEADS * DIFF_V

EXPERTS, TOP_K, D_EXP = 32, 4, 1024
FT = D_EXP // P
LIMIT, ALPHA = 7.0, 1.702
JOB = 256
JH = JOB // P
LIST = SEQ
EXTRA_JOBS = SEQ * TOP_K // JOB
JOBS = EXPERTS + EXTRA_JOBS
TK = TT * TOP_K
WIDTHS = tuple(range(P, JOB + 1, 16))
DUMMY = SEQ
ROWS = SEQ + JOB

HT = 0
Y_MLA = 8192
Y_DIFF = 12288
R = 16384
RING_SLOT = 4096
RING_SLOTS = 6
X_IN, H_N, SQ, W_DV = R, R + 4096, R + 6144, R + 8192
BIAS_T = R + 9216
W_PAIR = R + 8192
V_MLA, V_DIFF = R + 12288, R + 16384
QK = R + 20480
PROB, PROB_T, ROT = R, R + 4096, R + 6144
QA, CKV, COS, SIN, KR, W_ST = 40960, 43008, 44032, 45056, 46080, 47104
ARENA = 51200
Y_T, MERGED, W_MERGE, GATE_T = R, R + 8192, R + 16384, R + 22528
W_OUT, X_RES, H2, H2_T, X2 = 0, 8192, 12288, 14336, R + 16384
W_ROUTER, B_ROUTER, LOGITS = 40960, 41216, 41248
CHOSEN, PICKED, MEMBER, EARLIER, PLACE, EXPERT_ROW, ENTRY, FILL = 41504, 42528, 43552, 43808, 44096, 44352, 44800, 44864
TRI, B_IN, ZERO = 45376, 46400, 49472
GATES, WEIGHTED = 50496, 50752
XG, B1_T, XT, EG, ACT_T, YG, ENT = 0, 2048, 4096, 6144, 8192, 40960, 43008


def rel_buckets():
    n = np.maximum(255 - np.arange(383), 0)
    exact = BUCKETS // 2
    nf = np.maximum(n, 1).astype(np.float32)
    large = exact + (np.log(nf / np.float32(exact)) / np.float32(np.log(MAX_DIST / exact)) * (BUCKETS - exact)).astype(np.int32)
    b = np.where(n < exact, n, np.minimum(large, BUCKETS - 1))
    return (np.arange(BUCKETS)[:, None] == b[None, :]).astype(np.float32)


def rope_rows():
    half = np.arange(0, ROPE, 2, dtype=np.float32) / np.float32(ROPE)
    f = np.tile(np.power(np.float32(10000.0), -half), 2 * P // ROPE)
    sign = np.tile(np.repeat(np.float32([-1.0, 1.0]), ROPE // 2), P // ROPE)
    return np.stack([f, sign], axis=1).astype(np.float32)


class Core:

    def __init__(self, nc):
        self.nc = nc


class Dram:

    def __init__(self, a):
        self.x, self.positions, self.norm_mix, self.w_in = a["x"], a["positions"], a["norm_mix"], a["w_in"]
        self.mla_q_norm, self.w_q_b, self.mla_kv_norm, self.w_kv_b = a["mla_q_norm"], a["w_q_b"], a["mla_kv_norm"], a["w_kv_b"]
        self.diff_lambda, self.diff_subln, self.rel_bias = a["diff_lambda"], a["diff_subln"], a["rel_bias"]
        self.w_up_mla, self.w_up_diff, self.w_out = a["w_up_mla"], a["w_up_diff"], a["w_out"]
        self.norm_ffn, self.w_router, self.b_router = a["norm_ffn"], a["w_router"], a["b_router"]
        self.w1, self.b1, self.w2, self.b2, self.norm_final = a["w1"], a["b1"], a["w2"], a["b2"], a["norm_final"]
        self.rope_rows, self.bucket_rows = a["rope_rows"], a["bucket_rows"]
        self.out, self.acc, self.h2, self.lists = a["out"], a["acc"], a["h2"], a["lists"]


class Chain:

    def __init__(self, eng, sem, base=0):
        self.eng, self.sem, self.n = eng, sem, base

    def step(self, ins):
        ins.then_inc(self.sem, 1)
        self.n += 1
        self.eng.wait_ge(self.sem, self.n)


def setup(nc, ctx):
    g = Core(nc)
    g.sb = lambda name, shape, dt=F32: ctx.enter_context(nc.sbuf_tensor(name, shape, dt))
    g.sem = lambda name: ctx.enter_context(nc.semaphore(name))
    g.arena = g.sb("arena", [P, ARENA])
    g.banks = ctx.enter_context(nc.psum_tensor("banks", [P, 8 * HALF], F32))
    g.ident = g.sb("ident", [P, P])
    g.ones = g.sb("ones", [P, P])
    g.flip = g.sb("flip", [P, P])
    g.before = g.sb("before", [P, P])
    g.causal = g.sb("causal", [P, P])
    g.gain_mix = g.sb("gain_mix", [P, KT])
    g.gain_q = g.sb("gain_q", [P, 2])
    g.gain_kv = g.sb("gain_kv", [P, 1])
    g.gain_sub = g.sb("gain_sub", [P, 2])
    g.gain_ffn = g.sb("gain_ffn", [P, KT])
    g.eps = g.sb("eps", [P, 1])
    g.stat = g.sb("stat", [P, 32])
    g.lam = g.sb("lam", [P, 8])
    g.den = g.sb("den", [P, 64])
    g.ssq = g.sb("ssq", [P, 32])
    g.best, g.best_at = g.sb("best", [P, 8 * TT]), g.sb("best_at", [P, 8 * TT], U32)
    g.total = g.sb("total", [P, 1], I32)
    g.job_expert, g.job_place, g.job_count = (g.sb(n, [P, JOBS + 2], I32) for n in ("job_expert", "job_place", "job_count"))
    g.w_in = [g.sem(f"w_in{s}") for s in range(RING_SLOTS)]
    g.listed, g.zeros, g.acc_out = g.sem("listed"), g.sem("zeros"), g.sem("acc_out")
    return g


def at(g, off, n):
    return g.arena[:, off:off + n]


def tiled(g, off, a, n):
    return g.arena[:, off:off + a * n].rearrange("p (a n) -> p a n", a=a)


def bank(g, b, n=1):
    return g.banks[:, b * HALF:(b + n) * HALF]


def stage_norm(g, io):
    nc = g.nc
    x_in = [g.sem(f"x_in{s}") for s in range(4)]
    gains_in, squared, norm_known, inverted, h_ready, turned, ht_ready = (
        g.sem(n) for n in ("gains_in", "squared", "norm_known", "inverted", "h_ready", "turned", "ht_ready"))
    filled, shaped = g.sem("filled"), g.sem("shaped")
    ht = tiled(g, HT, KT, SEQ)
    xs, hs = tiled(g, X_IN, 4, D), tiled(g, H_N, 2, D)
    total, root, inv = g.stat[:, 0:8], g.stat[:, 8:16], g.stat[:, 16:24]

    with nc.Block() as block:

        @block.sync
        def _(sp):
            for t in range(TT):
                if t >= 4:
                    sp.wait_ge(h_ready, t - 3)
                sp.dma_start(xs[:, t % 4, :], io.x[0, t * P:(t + 1) * P, :]).then_inc(x_in[t % 4], 16)

        @block.gpsimd
        def _(pool):
            for m, v in ((g.ident, 0.0), (g.ones, 1.0), (g.flip, 0.0), (g.before, 1.0), (g.causal, 0.0), (g.eps, EPS)):
                pool.memset(m[:, :], v).then_inc(filled, 1)
            pool.wait_ge(filled, 6)
            for m, op, fill, base, step, mult in (
                    (g.ident, ALU.not_equal, 1.0, 0, -1, 1),
                    (g.flip, ALU.not_equal, 1.0, -(P - 1), 1, 1),
                    (g.before, ALU.is_gt, 0.0, 0, 1, -1),
                    (g.causal, ALU.is_ge, NEG, 0, -1, 1)):
                pool.affine_select(out=m[:, :], in_=m[:, :], compare_op=op, fill=fill, base=base,
                                   pattern=[[step, P]], channel_multiplier=mult).then_inc(shaped, 1)
            pool.wait_ge(shaped, 4)

        @block.scalar
        def _(act):
            for gain, src in ((g.gain_mix, io.norm_mix), (g.gain_q, io.mla_q_norm), (g.gain_kv, io.mla_kv_norm),
                              (g.gain_sub, io.diff_subln), (g.gain_ffn, io.norm_ffn)):
                act.dma_start(gain[:, 0:src.shape[1] // P], src.rearrange("a (k p) -> (a p) k", p=P)).then_inc(gains_in, 16)
            act.wait_ge(filled, 6)
            with act.Fori(0, 2) as i:
                for s in range(4):
                    act.wait_ge(x_in[s], 16 * i + 16)
                    nc.scalar.activation(bank(g, 4 + 2 * (s % 2), 2), xs[:, s, :], ACT.Square,
                                         accum_out=total[:, bass.ds(4 * i + s, 1)]).then_inc(squared, 1)
                    act.wait_ge(squared, 4 * i + s + 1)
                    nc.scalar.activation(root[:, bass.ds(4 * i + s, 1)], total[:, bass.ds(4 * i + s, 1)], ACT.Sqrt,
                                         scale=1.0 / D, bias=g.eps[:, 0:1]).then_inc(norm_known, 1)
            act.wait_ge(gains_in, 5 * 16)

        @block.tensor
        def _(pe):
            pe.wait_ge(shaped, 4)
            with pe.Fori(0, 2) as i:
                for s in range(4):
                    pe.wait_ge(h_ready, 4 * i + s + 1)
                    for k in range(KT):
                        last = nc.tensor.transpose(bank(g, 2 * (s % 2), 2)[:, k * P:(k + 1) * P],
                                                   hs[:, s % 2, k * P:(k + 1) * P], g.ident[:, :])
                    last.then_inc(turned, 1)

        @block.vector
        def _(dve):
            dve.wait_ge(gains_in, 5 * 16)
            with dve.Fori(0, 2) as i:
                for s in range(4):
                    dve.wait_ge(norm_known, 4 * i + s + 1)
                    nc.vector.reciprocal(inv[:, bass.ds(4 * i + s, 1)], root[:, bass.ds(4 * i + s, 1)]).then_inc(inverted, 1)
                    dve.wait_ge(inverted, 4 * i + s + 1)
                    nc.vector.tensor_scalar(hs[:, s % 2, :], xs[:, s, :], inv[:, bass.ds(4 * i + s, 1)], None,
                                            ALU.mult).then_inc(h_ready, 1)
                    dve.wait_ge(turned, 4 * i + s + 1)
                    nc.vector.tensor_tensor(ht[:, :, bass.ds((4 * i + s) * P, P)],
                                            bank(g, 2 * (s % 2), 2).rearrange("p (k t) -> p k t", k=KT),
                                            g.gain_mix[:, :].unsqueeze(2).broadcast_to([P, KT, P]), ALU.mult).then_inc(ht_ready, 1)
            dve.wait_ge(ht_ready, TT)


def stage_latents(g, io):
    nc = g.nc
    w_ready = [g.sem(f"w_latent{m}") for m in range(4)]
    rows_in, wdv_in, wkv_in = g.sem("rows_in"), g.sem("wdv_in"), g.sem("wkv_in")
    projected, lat_out, lat_sq, lat_sum, lat_root, lat_done = (
        g.sem(n) for n in ("projected", "lat_out", "lat_sq", "lat_sum", "lat_root", "lat_done"))
    row_made, row_out, row_stored, row_shifted, row_flipped, bias_made, bias_masked = (
        g.sem(n) for n in ("row_made", "row_out", "row_stored", "row_shifted", "row_flipped", "bias_made", "bias_masked"))
    value_made, value_out, angles, trig, steps = (
        g.sem(n) for n in ("value_made", "value_out", "angles", "trig", "latent_steps"))
    w_v = io.w_in.rearrange("(k p) n -> p k n", p=P)
    ht = tiled(g, HT, KT, SEQ)
    wst = g.arena[:, W_ST:W_ST + 4 * SEQ].rearrange("p (s k c) -> p s k c", s=4, k=KT)
    wdv = tiled(g, W_DV, KT, HALF)
    sq = tiled(g, SQ, 2, HALF)
    root = at(g, X_IN, 2 * SEQ)
    arg_sin, arg_cos = at(g, X_IN + 2048, SEQ), at(g, X_IN + 3072, SEQ)
    pos_i, posf, angle = at(g, KR, SEQ).bitcast(I32), at(g, COS, SEQ), at(g, SIN, SEQ)
    rows = g.sb("rope_rows_sb", [P, 2])
    bias_far = g.sb("bias_far", [P, DIFF_HEADS])
    rel = at(g, QK + 3072, DIFF_HEADS)[0:BUCKETS]
    onehot = at(g, QK, 383)[0:BUCKETS]
    by_distance = at(g, QK + 512, 383)[0:DIFF_HEADS]
    shifted = tiled(g, QK + 1024, DIFF_HEADS, 256)
    lamv, lamp = at(g, QK + 2048, 256), at(g, QK + 2304, 128)
    wv = at(g, QK + 2560, HALF)
    bias_t = tiled(g, BIAS_T, DIFF_HEADS, 256)
    kr, rot = at(g, KR, SEQ)[NOPE:HEAD_QK], at(g, SQ, SEQ)[NOPE:HEAD_QK]
    toeplitz = nc.dram_tensor("bias_by_distance", (DIFF_HEADS, 384), F32).ap()

    with nc.Block() as block:

        @block.sync
        def _(sp):
            for m, col in enumerate((0, P, OFF_KV)):
                sp.dma_start(wst[:, m], w_v[:, :, col:col + P]).then_inc(w_ready[m], 16)
            half = ROPE // 2
            for to, col, n in ((0, OFF_KR, ROPE), (ROPE, OFF_KR + half, half), (ROPE + half, OFF_KR, half)):
                sp.dma_start(wst[:, 3, :, to:to + n], w_v[:, :, col:col + n]).then_inc(w_ready[3], 16)
            sp.dma_start(wdv, w_v[:, :, OFF_DV:OFF_DV + HALF]).then_inc(wdv_in, 16)
            sp.wait_ge(row_out, 1)
            sp.dma_start(toeplitz[:, 0:383], by_distance).then_inc(row_stored, 16)
            sp.wait_ge(row_stored, 16)
            for h in range(DIFF_HEADS):
                src = bass.AP(tensor=toeplitz.tensor, offset=h * 384, ap=[[1, P], [1, 256]])
                sp.dma_start(shifted[:, h, :], src).then_inc(row_shifted, 16)
            sp.wait_ge(row_shifted, 16 * DIFF_HEADS)

        @block.gpsimd
        def _(pool):
            pool.wait_ge(bias_made, DIFF_HEADS)
            for h in range(DIFF_HEADS):
                pool.affine_select(out=bias_t[:, h, P:], in_=bias_t[:, h, P:], compare_op=ALU.is_ge, fill=NEG,
                                   base=0, pattern=[[-1, P]], channel_multiplier=1).then_inc(bias_masked, 1)
            pool.wait_ge(bias_masked, DIFF_HEADS)

        @block.scalar
        def _(act):
            for out, src in ((rel, io.rel_bias), (onehot, io.bucket_rows), (pos_i, io.positions.partition_broadcast(P)),
                             (rows[:, :], io.rope_rows), (bias_far[:, :], io.rel_bias[BUCKETS - 1:BUCKETS, :].partition_broadcast(P)),
                             (lamv, io.diff_lambda.rearrange("(o a) b -> o (a b)", o=1).partition_broadcast(P))):
                act.dma_start(out, src).then_inc(rows_in, 16)
            act.dma_start(wv.rearrange("p (h c) -> p h c", c=MLA_V),
                          io.w_kv_b.rearrange("p (h c) -> p h c", c=NOPE + MLA_V)[:, :, NOPE:]).then_inc(wkv_in, 16)
            for m in range(3):
                act.wait_ge(lat_out, m + 1)
                for h in range(2):
                    if m >= 1:
                        act.wait_ge(lat_sum, 2 * m + h - 1)
                    nc.scalar.activation(sq[:, h, :], bank(g, 4 + 2 * (m % 2) + h), ACT.Square).then_inc(lat_sq, 1)
            act.wait_ge(lat_sum, 6)
            nc.scalar.activation(root[:, 0:SEQ], bank(g, 0, 2), ACT.Sqrt, scale=1.0 / Q_RANK, bias=g.eps[:, 0:1]).then_inc(lat_root, 1)
            nc.scalar.activation(root[:, SEQ:], bank(g, 2, 2), ACT.Sqrt, scale=1.0 / KV_RANK, bias=g.eps[:, 0:1]).then_inc(lat_root, 1)
            act.wait_ge(angles, 1)
            nc.scalar.activation(at(g, SIN, SEQ), arg_sin, ACT.Sin, scale=rows[:, 1:2]).then_inc(trig, 1)
            nc.scalar.activation(at(g, COS, SEQ), arg_cos, ACT.Sin).then_inc(trig, 1)

        @block.tensor
        def _(pe):
            pe.wait_ge(rows_in, 6 * 16)
            nc.tensor.matmul(bank(g, 0)[0:DIFF_HEADS, 0:383], rel, onehot, start=True, stop=True).then_inc(row_made, 1)
            pe.wait_ge(row_out, 1)
            for m in range(3):
                pe.wait_ge(w_ready[m], 16)
                if m == 2:
                    pe.wait_ge(lat_sq, 2)
                for h in range(2):
                    for k in range(KT):
                        last = nc.tensor.matmul(bank(g, 4 + 2 * (m % 2) + h), wst[:, m, k, :], ht[:, k, h * HALF:(h + 1) * HALF],
                                                start=(k == 0), stop=(k == KT - 1))
                last.then_inc(projected, 1)
                for h in range(2):
                    pe.wait_ge(lat_sq, 2 * m + h + 1)
                    nc.tensor.matmul(bank(g, (0 if m < 2 else 2) + h), g.ones[:, :], sq[:, h, :],
                                     start=(m != 1), stop=(m != 0)).then_inc(lat_sum, 1)
            pe.wait_ge(w_ready[3], 48)
            for swapped, b in ((0, 6), (1, 4)):
                for h in range(2):
                    for k in range(KT):
                        last = nc.tensor.matmul(bank(g, b + h)[NOPE:HEAD_QK, :], wst[:, 3, k, swapped * ROPE:(swapped + 1) * ROPE],
                                                ht[:, k, h * HALF:(h + 1) * HALF], start=(k == 0), stop=(k == KT - 1))
            last.then_inc(projected, 1)
            pe.wait_ge(wdv_in, 16)
            pe.wait_ge(lat_root, 2)
            for t in range(TT):
                if t >= 4:
                    pe.wait_ge(value_out, t - 3)
                for k in range(KT):
                    last = nc.tensor.matmul(bank(g, t % 4), ht[:, k, t * P:(t + 1) * P], wdv[:, k, :],
                                            start=(k == 0), stop=(k == KT - 1))
                last.then_inc(value_made, 1)
            pe.wait_ge(wkv_in, 16)
            pe.wait_ge(lat_done, 3)
            for t in range(TT):
                pe.wait_ge(value_out, t + 5)
                nc.tensor.matmul(bank(g, t % 4), at(g, CKV, SEQ)[:, t * P:(t + 1) * P], wv,
                                 start=True, stop=True).then_inc(value_made, 1)
            pe.wait_ge(row_shifted, 16 * DIFF_HEADS)
            for h in range(DIFF_HEADS):
                nc.tensor.matmul(bank(g, 4 + h % 2)[:, (h // 2) * 256:(h // 2) * 256 + 256], g.flip[:, :], shifted[:, h, :],
                                 start=True, stop=True).then_inc(row_flipped, 1)

        @block.vector
        def _(dve):
            chain = Chain(dve, steps)
            dve.wait_ge(row_made, 1)
            nc.vector.tensor_copy(by_distance, bank(g, 0)[0:DIFF_HEADS, 0:383]).then_inc(row_out, 1)
            dve.wait_ge(rows_in, 6 * 16)
            turn = 2 * np.pi
            part1 = 6.28125
            part2 = round((turn - part1) * 2 ** 21) / 2 ** 21
            part3 = turn - part1 - part2
            limit = 3.1415925
            chain.step(nc.vector.tensor_copy(posf, pos_i))
            chain.step(nc.vector.tensor_scalar(angle, posf, rows[:, 0:1], None, ALU.mult))
            turns_i, turns = at(g, H_N, SEQ).bitcast(I32), at(g, H_N + 1024, SEQ)
            for quarter, out in ((0.0, arg_sin), (0.25, arg_cos)):
                chain.step(nc.vector.tensor_scalar(turns_i, angle, 1.0 / turn, quarter, ALU.mult, ALU.add))
                chain.step(nc.vector.tensor_copy(turns, turns_i))
                src = angle
                for part in (part1, part2, part3):
                    chain.step(nc.vector.scalar_tensor_tensor(out=out, in0=turns, scalar=-float(part), in1=src, op0=ALU.mult, op1=ALU.add))
                    src = out
                chain.step(nc.vector.tensor_scalar(out, out, quarter * turn, limit, ALU.add, ALU.min))
                last = nc.vector.tensor_scalar(out, out, -limit, None, ALU.max)
                if quarter == 0.0:
                    chain.step(last)
            last.then_inc(angles, 1)
            for j in range(2):
                chain.step(nc.vector.tensor_tensor(lamp[:, j * 64:(j + 1) * 64], lamv[:, 128 * j:128 * j + 64],
                                                   lamv[:, 128 * j + 64:128 * j + 128], ALU.mult))
                chain.step(nc.vector.reduce_sum(g.lam[:, j:j + 1], lamp[:, j * 64:(j + 1) * 64], AX))
            for m in range(3):
                dve.wait_ge(projected, m + 1)
                gain = g.gain_q[:, m:m + 1] if m < 2 else g.gain_kv[:, 0:1]
                nc.vector.tensor_scalar(at(g, QA + m * SEQ, SEQ), bank(g, 4 + 2 * (m % 2), 2), gain, None, ALU.mult).then_inc(lat_out, 1)
            dve.wait_ge(lat_root, 2)
            chain.step(nc.vector.reciprocal(root, root))
            dve.wait_ge(lat_out, 3)
            for m in range(3):
                r = root[:, 0:SEQ] if m < 2 else root[:, SEQ:]
                nc.vector.tensor_tensor(at(g, QA + m * SEQ, SEQ), at(g, QA + m * SEQ, SEQ), r, ALU.mult).then_inc(lat_done, 1)
            dve.wait_ge(trig, 2)
            dve.wait_ge(projected, 4)
            chain.step(nc.vector.tensor_tensor(kr, bank(g, 6, 2)[NOPE:HEAD_QK], at(g, COS, SEQ)[NOPE:HEAD_QK], ALU.mult))
            chain.step(nc.vector.tensor_tensor(rot, bank(g, 4, 2)[NOPE:HEAD_QK], at(g, SIN, SEQ)[NOPE:HEAD_QK], ALU.mult))
            chain.step(nc.vector.tensor_tensor(kr, kr, rot, ALU.add))
            chain.step(nc.vector.tensor_scalar(kr, kr, MLA_SCALE, None, ALU.mult))
            for t in range(2 * TT):
                dve.wait_ge(value_made, t + 1)
                out = at(g, (V_DIFF if t < TT else V_MLA) + (t % TT) * HALF, HALF)
                nc.vector.tensor_copy(out, bank(g, t % 4)).then_inc(value_out, 1)
            dve.wait_ge(row_flipped, DIFF_HEADS)
            for h in range(DIFF_HEADS):
                nc.vector.tensor_scalar(bias_t[:, h, :], bank(g, 4 + h % 2)[:, (h // 2) * 256:(h // 2) * 256 + 256],
                                        bias_far[:, h:h + 1], None, ALU.subtract).then_inc(bias_made, 1)


def stage_mla(g, io):
    nc = g.nc
    w_pair, projected, qk_copied, q_rotated, rot_steps = (
        g.sem(n) for n in ("w_pair", "pair_projected", "qk_copied", "q_rotated", "rot_steps"))
    scored, masked, max_known, exped, turned0, turned1, pt_act, pt_dve, applied, inverted, y_out = (
        g.sem("mla_" + n) for n in ("scored", "masked", "max_known", "exped", "turned0", "turned1", "pt_act", "pt_dve",
                                    "applied", "inverted", "y_out"))
    UNITS, LATE = 2 * TT, TT
    qa, ckv = tiled(g, QA, 2, SEQ), at(g, CKV, SEQ)
    wq = tiled(g, W_PAIR, 2, 256)
    wk = at(g, W_PAIR + 512, P)
    q_t = [at(g, QK + (2 * j) * SEQ, SEQ) for j in range(2)]
    k_t = [at(g, QK + (2 * j + 1) * SEQ, SEQ) for j in range(2)]
    prob, prob_t, rot = tiled(g, PROB, 2, SEQ), tiled(g, PROB_T, 2, SEQ), tiled(g, ROT, 2, SEQ)
    v, y = tiled(g, V_MLA, TT, HALF), tiled(g, Y_MLA, TT, HALF)
    neg_max, total, inv = g.den[:, 0:16], g.den[:, 16:32], g.den[:, 32:48]
    wq_v = io.w_q_b.rearrange("(k p) (h c) -> p k h c", p=P, c=HEAD_QK)
    wk_v = io.w_kv_b.rearrange("p (h c) -> p h c", c=NOPE + MLA_V)
    half = ROPE // 2
    PAIR_DMAS = 9

    with nc.Block() as block:

        @block.sync
        def _(sp):
            def load_pair(hp):
                for k in range(2):
                    for to, step, col, n in ((0, NOPE, 0, NOPE), (2 * NOPE, ROPE, NOPE, ROPE),
                                             (2 * NOPE + 2 * ROPE, ROPE, NOPE + half, half),
                                             (2 * NOPE + 2 * ROPE + half, ROPE, NOPE, half)):
                        dst = wq[:, k, (to // step) * step:(to // step + 2) * step].rearrange("p (j c) -> p j c", j=2)
                        sp.dma_start(dst[:, :, to % step:to % step + n],
                                     wq_v[:, k, bass.ds(2 * hp, 2), col:col + n]).then_inc(w_pair, 16)
                sp.dma_start(wk.rearrange("p (j c) -> p j c", j=2),
                             wk_v[:, bass.ds(2 * hp, 2), 0:NOPE]).then_inc(w_pair, 16)
            load_pair(0)
            with sp.Fori(1, MLA_HEADS // 2) as hp:
                sp.wait_ge(projected, 3 * hp)
                load_pair(hp)

        @block.tensor
        def _(pe):
            with pe.Fori(0, MLA_HEADS // 2) as hp:
                base = UNITS * hp
                pe.wait_ge(w_pair, 16 * PAIR_DMAS * hp + 16 * PAIR_DMAS)
                pe.wait_ge(y_out, base + 1)
                for b, lhs in ((0, lambda k: wq[:, k, 0:P]), (2, lambda k: wq[:, k, P:2 * P])):
                    for h in range(2):
                        for k in range(2):
                            last = nc.tensor.matmul(bank(g, b + h), lhs(k), qa[:, k, h * HALF:(h + 1) * HALF],
                                                    start=(k == 0), stop=(k == 1))
                    last.then_inc(projected, 1)
                for h in range(2):
                    last = nc.tensor.matmul(bank(g, 4 + h), wk, ckv[:, h * HALF:(h + 1) * HALF], start=True, stop=True)
                last.then_inc(projected, 1)
                pe.wait_ge(qk_copied, 4 * hp + 4)
                pe.wait_ge(q_rotated, 2 * hp + 3)

                def score(u):
                    j, i = divmod(u, TT)
                    if u >= 2:
                        pe.wait_ge(exped, base + u - 1)
                    keys = (i + 1) * P
                    for c in range(0, keys, HALF):
                        n = min(HALF, keys - c)
                        last = nc.tensor.matmul(bank(g, 2 * (u % 2) + c // HALF)[:, 0:n], q_t[j][0:HEAD_QK, i * P:(i + 1) * P],
                                                k_t[j][0:HEAD_QK, c:c + n], start=True, stop=True)
                    last.then_inc(scored, 1)

                def turn(u):
                    j, i = divmod(u, TT)
                    pe.wait_ge(exped, base + u + 1)
                    for grp in range(1 + i // 4):
                        if grp == 0 and u >= 1:
                            pe.wait_ge(pt_act, base + u)
                        if grp == 1 and (j or i > 4):
                            pe.wait_ge(pt_dve, LATE * hp + 4 * j + i - 4)
                        for kt in range(4 * grp, min(4 * grp + 4, i + 1)):
                            last = nc.tensor.transpose(bank(g, 4 + grp)[:, (kt % 4) * P:(kt % 4 + 1) * P],
                                                       prob[:, u % 2, kt * P:(kt + 1) * P], g.ident[:, :])
                        last.then_inc((turned0, turned1)[grp], 1)

                def apply(u):
                    j, i = divmod(u, TT)
                    pe.wait_ge(pt_act, base + u + 1)
                    if i >= 4:
                        pe.wait_ge(pt_dve, LATE * hp + 4 * j + i - 3)
                    if u >= 2:
                        pe.wait_ge(y_out, base + u)
                    for kt in range(i + 1):
                        last = nc.tensor.matmul(bank(g, 6 + u % 2)[:, 0:MLA_V], prob_t[:, u % 2, kt * P:(kt + 1) * P],
                                                v[:, kt, bass.ds((2 * hp + j) * MLA_V, MLA_V)], start=(kt == 0), stop=(kt == i))
                    last.then_inc(applied, 1)

                score(0)
                for u in range(UNITS):
                    if u + 1 < UNITS:
                        score(u + 1)
                    turn(u)
                    if u >= 1:
                        apply(u - 1)
                apply(UNITS - 1)

        @block.vector
        def _(dve):
            nc.vector.tensor_copy(k_t[0][NOPE:HEAD_QK, :], at(g, KR, SEQ)[NOPE:HEAD_QK]).then_inc(q_rotated, 1)
            nc.vector.tensor_copy(k_t[1][NOPE:HEAD_QK, :], at(g, KR, SEQ)[NOPE:HEAD_QK]).then_inc(y_out, 1)
            with dve.Fori(0, MLA_HEADS // 2) as hp:
                base = UNITS * hp
                dve.wait_ge(projected, 3 * hp + 2)
                nc.vector.tensor_tensor(rot[0:NOPE, 0, :], bank(g, 2, 2)[0:NOPE], at(g, COS, SEQ)[0:NOPE], ALU.mult).then_inc(rot_steps, 1)
                nc.vector.tensor_tensor(rot[0:NOPE, 1, :], bank(g, 2, 2)[NOPE:P], at(g, SIN, SEQ)[NOPE:P], ALU.mult).then_inc(rot_steps, 1)
                dve.wait_ge(rot_steps, 2 * hp + 2)
                for j in range(2):
                    nc.vector.tensor_tensor(q_t[j][NOPE:HEAD_QK, :], rot[j * ROPE:(j + 1) * ROPE, 0, :],
                                            rot[j * ROPE:(j + 1) * ROPE, 1, :], ALU.add).then_inc(q_rotated, 1)

                def row_max(u):
                    i = u % TT
                    dve.wait_ge(scored, base + u + 1)
                    s = bank(g, 2 * (u % 2), 2)
                    nc.vector.tensor_tensor(s[:, i * P:(i + 1) * P], s[:, i * P:(i + 1) * P], g.causal[:, :], ALU.add).then_inc(masked, 1)
                    dve.wait_ge(masked, base + u + 1)
                    nc.vector.reduce_max(neg_max[:, u:u + 1], s[:, 0:(i + 1) * P], AX, negate=True).then_inc(max_known, 1)

                def copy_late(u):
                    j, i = divmod(u, TT)
                    if i < 4:
                        return
                    dve.wait_ge(turned1, LATE * hp + 4 * j + i - 3)
                    nc.vector.tensor_copy(prob_t[:, u % 2, HALF:(i + 1) * P], bank(g, 5)[:, 0:(i - 3) * P]).then_inc(pt_dve, 1)

                def store_y(u):
                    j, i = divmod(u, TT)
                    dve.wait_ge(applied, base + u + 1)
                    nc.vector.reciprocal(inv[:, u:u + 1], total[:, u:u + 1]).then_inc(inverted, 1)
                    dve.wait_ge(inverted, base + u + 1)
                    nc.vector.tensor_scalar(y[:, i, bass.ds((2 * hp + j) * MLA_V, MLA_V)], bank(g, 6 + u % 2)[:, 0:MLA_V],
                                            inv[:, u:u + 1], None, ALU.mult).then_inc(y_out, 1)

                row_max(0)
                for u in range(UNITS):
                    if u + 1 < UNITS:
                        row_max(u + 1)
                    copy_late(u)
                    if u >= 1:
                        store_y(u - 1)
                store_y(UNITS - 1)
            dve.wait_ge(y_out, UNITS * MLA_HEADS // 2 + 1)

        @block.scalar
        def _(act):
            with act.Fori(0, MLA_HEADS // 2) as hp:
                base = UNITS * hp
                act.wait_ge(projected, 3 * hp + 1)
                for j in range(2):
                    nc.scalar.activation(q_t[j][0:NOPE, :], bank(g, 0, 2)[j * NOPE:(j + 1) * NOPE], ACT.Copy).then_inc(qk_copied, 1)
                act.wait_ge(projected, 3 * hp + 3)
                for j in range(2):
                    nc.scalar.activation(k_t[j][0:NOPE, :], bank(g, 4, 2)[j * NOPE:(j + 1) * NOPE], ACT.Copy,
                                         scale=MLA_SCALE).then_inc(qk_copied, 1)

                def exp(u):
                    keys = (u % TT + 1) * P
                    act.wait_ge(max_known, base + u + 1)
                    nc.scalar.activation(prob[:, u % 2, 0:keys], bank(g, 2 * (u % 2), 2)[:, 0:keys], ACT.Exp,
                                         bias=neg_max[:, u:u + 1], accum_out=total[:, u:u + 1]).then_inc(exped, 1)

                def copy_early(u):
                    keys = min(HALF, (u % TT + 1) * P)
                    act.wait_ge(turned0, base + u + 1)
                    nc.scalar.activation(prob_t[:, u % 2, 0:keys], bank(g, 4)[:, 0:keys], ACT.Copy).then_inc(pt_act, 1)

                exp(0)
                for u in range(UNITS):
                    if u + 1 < UNITS:
                        exp(u + 1)
                    copy_early(u)


def stage_diff(g, io):
    nc = g.nc
    w_q, w_k, projected, q_copied, k_copied, lam_exp, lam_steps = (
        g.sem("diff_" + n) for n in ("w_q", "w_k", "projected", "q_copied", "k_copied", "lam_exp", "lam_steps"))
    scored, biased, max_known, exped, weighed, combined, turned0, turned1, pt_act, pt_dve, applied, y_out = (
        g.sem("diff_" + n) for n in ("scored", "biased", "max_known", "exped", "weighed", "combined", "turned0", "turned1",
                                     "pt_act", "pt_dve", "applied", "y_out"))
    HALVES, LATE = 2 * TT, TT // 2
    ht = tiled(g, HT, KT, SEQ)
    wst = g.arena[:, W_ST:W_ST + 2 * SEQ].rearrange("p (s k c) -> p s k c", s=2, k=KT)
    q_t, k_t = at(g, QK, SEQ), at(g, QK + SEQ, SEQ)
    prob, prob_t = tiled(g, PROB, 4, SEQ), tiled(g, PROB_T, 2, SEQ)
    v, y = tiled(g, V_DIFF, TT, HALF), tiled(g, Y_DIFF, TT, HALF)
    bias_t = tiled(g, BIAS_T, DIFF_HEADS, 256)
    neg_max, total, inv, share = g.den[:, 0:16], g.den[:, 16:32], g.den[:, 32:48], g.den[:, 48:56]
    w_v = io.w_in.rearrange("(k p) n -> p k n", p=P)

    with nc.Block() as block:

        @block.sync
        def _(sp):
            def load_head(h):
                sp.dma_start(wst[:, 0], w_v[:, :, bass.ds(OFF_DQ + P * h, P)]).then_inc(w_q, 16)
                sp.dma_start(wst[:, 1], w_v[:, :, bass.ds(OFF_DK + P * h, P)]).then_inc(w_k, 16)
            load_head(0)
            with sp.Fori(1, DIFF_HEADS) as h:
                sp.wait_ge(projected, 2 * h)
                load_head(h)

        @block.tensor
        def _(pe):
            with pe.Fori(0, DIFF_HEADS) as h:
                base, ub = HALVES * h, TT * h
                pe.wait_ge(y_out, ub + 1)
                for s, w in ((0, w_q), (1, w_k)):
                    pe.wait_ge(w, 16 * h + 16)
                    for c in range(2):
                        for k in range(KT):
                            last = nc.tensor.matmul(bank(g, 2 * s + c), wst[:, s, k, :], ht[:, k, c * HALF:(c + 1) * HALF],
                                                    start=(k == 0), stop=(k == KT - 1))
                    last.then_inc(projected, 1)
                pe.wait_ge(q_copied, h + 1)
                pe.wait_ge(k_copied, h + 1)

                def score(i):
                    keys = (i + 1) * P
                    for c in range(2):
                        s = 2 * i + c
                        if s >= 2:
                            pe.wait_ge(exped, base + s - 1)
                        rows = slice(c * DIFF_DIM, (c + 1) * DIFF_DIM)
                        for a in range(0, keys, HALF):
                            n = min(HALF, keys - a)
                            last = nc.tensor.matmul(bank(g, 2 * c + a // HALF)[:, 0:n], q_t[rows, i * P:(i + 1) * P],
                                                    k_t[rows, a:a + n], start=True, stop=True)
                        last.then_inc(scored, 1)

                def turn(i):
                    pe.wait_ge(combined, ub + i + 1)
                    for grp in range(1 + i // 4):
                        if grp == 0 and i >= 1:
                            pe.wait_ge(pt_act, ub + i)
                        if grp == 1 and i > 4:
                            pe.wait_ge(pt_dve, LATE * h + i - 4)
                        for kt in range(4 * grp, min(4 * grp + 4, i + 1)):
                            last = nc.tensor.transpose(bank(g, 4 + grp)[:, (kt % 4) * P:(kt % 4 + 1) * P],
                                                       prob[:, 2 * (i % 2), kt * P:(kt + 1) * P], g.ident[:, :])
                        last.then_inc((turned0, turned1)[grp], 1)

                def apply(i):
                    pe.wait_ge(pt_act, ub + i + 1)
                    if i >= 4:
                        pe.wait_ge(pt_dve, LATE * h + i - 3)
                    if i >= 2:
                        pe.wait_ge(y_out, ub + i)
                    for kt in range(i + 1):
                        last = nc.tensor.matmul(bank(g, 6 + i % 2)[:, 0:DIFF_V], prob_t[:, i % 2, kt * P:(kt + 1) * P],
                                                v[:, kt, bass.ds(h * DIFF_V, DIFF_V)], start=(kt == 0), stop=(kt == i))
                    last.then_inc(applied, 1)

                score(0)
                for i in range(TT):
                    if i + 1 < TT:
                        score(i + 1)
                    turn(i)
                    if i >= 1:
                        apply(i - 1)
                apply(TT - 1)

        @block.vector
        def _(dve):
            dve.wait_ge(lam_exp, 1)
            nc.vector.tensor_tensor(g.lam[:, 4:5], g.lam[:, 3:4], g.lam[:, 2:3], ALU.subtract).then_inc(lam_steps, 1)
            dve.wait_ge(lam_steps, 1)
            nc.vector.tensor_scalar(g.lam[:, 5:6], g.lam[:, 4:5], -LAMBDA_INIT, None, ALU.add).then_inc(lam_steps, 1)
            dve.wait_ge(lam_steps, 2)
            nc.vector.tensor_copy(g.lam[:, 6:7], g.lam[:, 5:6]).then_inc(y_out, 1)
            with dve.Fori(0, DIFF_HEADS) as h:
                base, ub = HALVES * h, TT * h
                dve.wait_ge(projected, 2 * h + 2)
                nc.vector.tensor_copy(k_t, bank(g, 2, 2)).then_inc(k_copied, 1)

                def row_max(i):
                    keys, near = (i + 1) * P, max(0, i - 1) * P
                    for c in range(2):
                        s = 2 * i + c
                        dve.wait_ge(scored, base + s + 1)
                        sc = bank(g, 2 * c, 2)
                        nc.vector.tensor_tensor(sc[:, near:keys], sc[:, near:keys],
                                                bias_t[:, bass.ds(h, 1), 2 * P - (keys - near):2 * P], ALU.add).then_inc(biased, 1)
                        dve.wait_ge(biased, base + s + 1)
                        nc.vector.reduce_max(neg_max[:, s:s + 1], sc[:, 0:keys], AX, negate=True).then_inc(max_known, 1)

                def combine(i):
                    dve.wait_ge(exped, base + 2 * i + 2)
                    nc.vector.reciprocal(inv[:, 2 * i:2 * i + 2], total[:, 2 * i:2 * i + 2]).then_inc(weighed, 1)
                    dve.wait_ge(weighed, 2 * (ub + i) + 1)
                    nc.vector.scalar_tensor_tensor(out=share[:, i:i + 1], in0=total[:, 2 * i:2 * i + 1], scalar=g.lam[:, 5:6],
                                                   in1=inv[:, 2 * i + 1:2 * i + 2], op0=ALU.mult, op1=ALU.mult).then_inc(weighed, 1)
                    dve.wait_ge(weighed, 2 * (ub + i) + 2)
                    keys, s = (i + 1) * P, 2 * (i % 2)
                    nc.vector.scalar_tensor_tensor(out=prob[:, s, 0:keys], in0=prob[:, s + 1, 0:keys], scalar=share[:, i:i + 1],
                                                   in1=prob[:, s, 0:keys], op0=ALU.mult, op1=ALU.add).then_inc(combined, 1)

                def copy_late(i):
                    if i < 4:
                        return
                    dve.wait_ge(turned1, LATE * h + i - 3)
                    nc.vector.tensor_copy(prob_t[:, i % 2, HALF:(i + 1) * P], bank(g, 5)[:, 0:(i - 3) * P]).then_inc(pt_dve, 1)

                def store_y(i):
                    dve.wait_ge(applied, ub + i + 1)
                    nc.vector.tensor_scalar(y[:, i, bass.ds(h * DIFF_V, DIFF_V)], bank(g, 6 + i % 2)[:, 0:DIFF_V],
                                            inv[:, 2 * i:2 * i + 1], None, ALU.mult).then_inc(y_out, 1)

                row_max(0)
                combine(0)
                for i in range(TT):
                    if i + 1 < TT:
                        row_max(i + 1)
                    copy_late(i)
                    if i + 1 < TT:
                        combine(i + 1)
                    if i >= 1:
                        store_y(i - 1)
                store_y(TT - 1)
            dve.wait_ge(y_out, TT * DIFF_HEADS + 1)

        @block.scalar
        def _(act):
            nc.scalar.activation(g.lam[:, 2:4], g.lam[:, 0:2], ACT.Exp).then_inc(lam_exp, 1)
            with act.Fori(0, DIFF_HEADS) as h:
                base, ub = HALVES * h, TT * h
                act.wait_ge(projected, 2 * h + 1)
                nc.scalar.activation(q_t, bank(g, 0, 2), ACT.Copy, scale=DIFF_SCALE).then_inc(q_copied, 1)

                def exp(i):
                    keys = (i + 1) * P
                    for c in range(2):
                        s = 2 * i + c
                        act.wait_ge(max_known, base + s + 1)
                        nc.scalar.activation(prob[:, s % 4, 0:keys], bank(g, 2 * c, 2)[:, 0:keys], ACT.Exp,
                                             bias=neg_max[:, s:s + 1], accum_out=total[:, s:s + 1]).then_inc(exped, 1)

                def copy_early(i):
                    keys = min(HALF, (i + 1) * P)
                    act.wait_ge(turned0, ub + i + 1)
                    nc.scalar.activation(prob_t[:, i % 2, 0:keys], bank(g, 4)[:, 0:keys], ACT.Copy).then_inc(pt_act, 1)

                exp(0)
                for i in range(TT):
                    if i + 1 < TT:
                        exp(i + 1)
                    copy_early(i)


def stage_merge(g, io):
    nc = g.nc
    squared, summed, rooted, inverted, normed = (g.sem("sub_" + n) for n in ("squared", "summed", "rooted", "inverted", "normed"))
    turned, copied_a, copied_d = g.sem("y_turned"), g.sem("y_copied_act"), g.sem("y_copied_dve")
    w_tile = [g.sem(f"w_merge{s}") for s in range(2)]
    made, gated, scaled, merged = (g.sem("merge_" + n) for n in ("made", "gated", "scaled", "merged"))
    ht, yt = tiled(g, HT, KT, SEQ), tiled(g, Y_T, KT, SEQ)
    y_m, y_d = tiled(g, Y_MLA, TT, HALF), tiled(g, Y_DIFF, TT, HALF)
    sq = at(g, MERGED, TT * HALF)
    out = tiled(g, MERGED, KT, SEQ)
    gate = tiled(g, GATE_T, 4, HALF)
    w = [[tiled(g, W_MERGE + 3072 * s + o, n, P) for o, n in ((0, KT), (1024, KT), (2048, 4), (2560, 4))] for s in range(2)]
    w_in = io.w_in.rearrange("(k p) n -> p k n", p=P)
    w_um, w_ud = (a.rearrange("(k p) n -> p k n", p=P) for a in (io.w_up_mla, io.w_up_diff))

    with nc.Block() as block:

        @block.sync
        def _(sp):
            def load(f, s):
                for dst, src, col in zip(w[s], (w_in, w_in, w_um, w_ud), (OFF_GATE, OFF_GATE + D, 0, 0)):
                    sp.dma_start(dst, src[:, :, bass.ds(f * P + col, P)]).then_inc(w_tile[s], 16)
            load(0, 0)
            load(1, 1)
            with sp.Fori(1, KT // 2) as i:
                for s in range(2):
                    sp.wait_ge(made, 4 * i + 2 * s - 2)
                    load(2 * i + s, s)

        @block.tensor
        def _(pe):
            for n in range(16):
                a, h = divmod(n, 2)
                src = y_m if a < 4 else y_d
                if n == 8:
                    pe.wait_ge(normed, 1)
                if n >= 8:
                    pe.wait_ge(copied_a if n % 2 == 0 else copied_d, (n - 8) // 2 + 1)
                for t in range(4):
                    last = nc.tensor.transpose(bank(g, n % 8)[:, t * P:(t + 1) * P], src[:, 4 * h + t, (a % 4) * P:(a % 4 + 1) * P], g.ident[:, :])
                last.then_inc(turned, 1)
            pe.wait_ge(copied_a, 8)
            pe.wait_ge(copied_d, 8)
            with pe.Fori(0, KT // 2) as i:
                for s in range(2):
                    pe.wait_ge(w_tile[s], 64 * i + 64)
                    for h in range(2):
                        n = 4 * i + 2 * s + h
                        pe.wait_ge(merged, n + 1)
                        cols = slice(h * HALF, (h + 1) * HALF)
                        for b, (rhs, k0, kn) in enumerate(((ht, 0, KT), (ht, 0, KT), (yt, 0, 4), (yt, 4, 4))):
                            for k in range(kn):
                                last = nc.tensor.matmul(bank(g, 4 * h + b), w[s][b][:, k, :], rhs[:, k0 + k, cols],
                                                        start=(k == 0), stop=(k == kn - 1))
                        last.then_inc(made, 1)

        @block.scalar
        def _(act):
            act.wait_ge(summed, 1)
            nc.scalar.activation(g.ssq[:, :], g.ssq[:, :], ACT.Sqrt, scale=1.0 / DIFF_V, bias=g.eps[:, 0:1]).then_inc(rooted, 1)
            for n in range(0, 16, 2):
                act.wait_ge(turned, n + 1)
                if n < 8:
                    last = nc.scalar.activation(yt[:, n // 2, 0:HALF], bank(g, n % 8), ACT.Copy)
                else:
                    last = nc.scalar.activation(yt[:, n // 2, 0:HALF], bank(g, n % 8), ACT.Copy, scale=g.gain_sub[:, 1:2])
                last.then_inc(copied_a, 1)
            with act.Fori(0, KT // 2) as i:
                for u in range(4):
                    act.wait_ge(made, 4 * i + u + 1)
                    for b in range(2):
                        nc.scalar.activation(gate[:, 2 * (u % 2) + b, :], bank(g, 4 * (u % 2) + b), ACT.Sigmoid).then_inc(gated, 1)

        @block.vector
        def _(dve):
            dve.sem_inc(merged, 2)
            nc.vector.tensor_tensor(sq, at(g, Y_DIFF, TT * HALF), at(g, Y_DIFF, TT * HALF), ALU.mult).then_inc(squared, 1)
            nc.vector.tensor_scalar(g.gain_sub[:, 1:2], g.gain_sub[:, 0:1], 1.0 - LAMBDA_INIT, None, ALU.mult).then_inc(squared, 1)
            dve.wait_ge(squared, 2)
            nc.vector.reduce_sum(g.ssq[:, :], sq.rearrange("p (a n) -> p a n", n=DIFF_V), AX).then_inc(summed, 1)
            dve.wait_ge(rooted, 1)
            nc.vector.reciprocal(g.ssq[:, :], g.ssq[:, :]).then_inc(inverted, 1)
            dve.wait_ge(inverted, 1)
            yv = at(g, Y_DIFF, TT * HALF).rearrange("p (a n) -> p a n", n=DIFF_V)
            nc.vector.tensor_tensor(yv, yv, g.ssq[:, :].unsqueeze(2).broadcast_to([P, 32, DIFF_V]), ALU.mult).then_inc(normed, 1)
            for n in range(1, 16, 2):
                dve.wait_ge(turned, n + 1)
                if n < 8:
                    last = nc.vector.tensor_copy(yt[:, n // 2, HALF:], bank(g, n % 8))
                else:
                    last = nc.vector.tensor_scalar(yt[:, n // 2, HALF:], bank(g, n % 8), g.gain_sub[:, 1:2], None, ALU.mult)
                last.then_inc(copied_d, 1)
            with dve.Fori(0, KT // 2) as i:
                for s in range(2):
                    for h in range(2):
                        n = 4 * i + 2 * s + h
                        for b in range(2):
                            dve.wait_ge(gated, 2 * n + b + 1)
                            nc.vector.tensor_tensor(gate[:, 2 * h + b, :], bank(g, 4 * h + 2 + b), gate[:, 2 * h + b, :], ALU.mult).then_inc(scaled, 1)
                        dve.wait_ge(scaled, 2 * n + 2)
                        nc.vector.tensor_tensor(out[:, bass.ds(2 * i + s, 1), h * HALF:(h + 1) * HALF], gate[:, 2 * h, :],
                                                gate[:, 2 * h + 1, :], ALU.add).then_inc(merged, 1)
            dve.wait_ge(merged, 2 * KT + 2)


def routing_views(g):
    v = Core(g.nc)
    v.chosen = tiled(g, CHOSEN, TK, EXPERTS)
    v.earlier = tiled(g, EARLIER, TT + 1, EXPERTS)
    v.gates = tiled(g, GATES, TT, EXPERTS)
    v.expert_row = at(g, EXPERT_ROW, EXPERTS)
    v.tri = tiled(g, TRI, EXPERTS, EXPERTS)
    v.job_no = at(g, EXPERT_ROW + 352, EXTRA_JOBS).bitcast(I32)
    v.x2 = tiled(g, X2, TT, D)
    return v


def stage_out(g, io):
    nc = g.nc
    w_out_in, x_in = g.sem("w_out_in"), [g.sem(f"x_res{s}") for s in range(2)]
    router_in = g.sem("router_in")
    h2_out = [g.sem(f"h2_out{s}") for s in range(2)]
    ids, fill_out, shifted, exps, ranked, placed, data_ready, chain_s = (
        g.sem("route_" + n) for n in ("ids", "fill_out", "shifted", "exps", "ranked", "placed", "data_ready", "chain"))
    made, added, squared, rooted, normed, turned, h2t_ready, scored, biased, chosen = (
        g.sem("out_" + n) for n in ("made", "added", "squared", "rooted", "normed", "turned", "h2t_ready", "scored", "biased", "chosen"))
    w_out, merged = tiled(g, W_OUT, KT, D), tiled(g, MERGED, KT, SEQ)
    x, h2 = tiled(g, X_RES, 2, D), tiled(g, H2, 2, D)
    h2t = g.arena[:, H2_T:H2_T + 2 * D].rearrange("p (s k t) -> p s k t", s=2, k=KT)
    w_r = tiled(g, W_ROUTER, KT, EXPERTS)
    b_r = at(g, B_ROUTER, EXPERTS)
    logits = tiled(g, LOGITS, TT, EXPERTS)
    v = routing_views(g)
    x2, chosen_by, earlier = v.x2, v.chosen, v.earlier
    picked, weighted = tiled(g, PICKED, TK, EXPERTS), tiled(g, WEIGHTED, TOP_K, EXPERTS)
    member, place = tiled(g, MEMBER, TT, EXPERTS), tiled(g, PLACE, TT, EXPERTS)
    expert_i, start_row = at(g, EXPERT_ROW + 32, EXPERTS).bitcast(I32), at(g, EXPERT_ROW + 64, EXPERTS)
    best_f, dest, wts = at(g, EXPERT_ROW + 96, TK), at(g, EXPERT_ROW + 128, TK), at(g, EXPERT_ROW + 160, TK)
    dest_i, sums = at(g, EXPERT_ROW + 192, TK).bitcast(I32), at(g, EXPERT_ROW + 224, TT)
    entry, fill, zero = at(g, ENTRY, 2 * TK), at(g, FILL, 512), at(g, ZERO, D)
    total, root, inv = g.stat[:, 0:8], g.stat[:, 8:16], g.stat[:, 16:24]

    with nc.Block() as block:

        @block.sync
        def _(sp):
            sp.dma_start(w_out, io.w_out.rearrange("(k p) n -> p k n", p=P)).then_inc(w_out_in, 16)
            sp.dma_start(w_r, io.w_router.rearrange("(k p) n -> p k n", p=P)).then_inc(router_in, 16)
            sp.dma_start(b_r, io.b_router.partition_broadcast(P)).then_inc(router_in, 16)
            for slot in (0, 1):
                load_weights(g, io, sp, 0, slot)
            for t in range(TT):
                if t >= 2:
                    sp.wait_ge(added, t - 1)
                sp.dma_start(x[:, t % 2, :], io.x[0, t * P:(t + 1) * P, :]).then_inc(x_in[t % 2], 16)

        @block.gpsimd
        def _(pool):
            pool.iota(expert_i, pattern=[[1, EXPERTS]], base=0, channel_multiplier=0).then_inc(ids, 1)
            pool.iota(entry.bitcast(I32).rearrange("p (n c) -> p n c", c=2)[:, :, 0:1].rearrange("p (t k) c -> p t (k c)", t=TT),
                      pattern=[[P, TT], [0, TOP_K]], base=0, channel_multiplier=1).then_inc(ids, 1)
            pool.memset(fill, 0.0).then_inc(ids, 1)
            pool.memset(v.tri, 1.0).then_inc(ids, 1)
            pool.memset(zero, 0.0).then_inc(ids, 1)
            pool.iota(v.job_no, pattern=[[1, EXTRA_JOBS]], base=0, channel_multiplier=0).then_inc(ids, 1)
            pool.wait_ge(ids, 6)
            pool.iota(fill.bitcast(I32).rearrange("p (n c) -> p n c", c=2)[:, :, 0], pattern=[[1, 256]],
                      base=DUMMY, channel_multiplier=0).then_inc(ids, 1)
            pool.affine_select(out=v.tri, in_=v.tri, compare_op=ALU.is_ge, fill=0.0, base=0,
                               pattern=[[1, EXPERTS], [-1, EXPERTS]], channel_multiplier=0).then_inc(ids, 1)
            pool.wait_ge(ids, 8)
            pool.dma_start(io.lists.rearrange("(p n) c -> p (n c)", p=P), fill).then_inc(fill_out, 16)
            for r in range(DUMMY, ROWS, P):
                pool.dma_start(io.h2[r:r + P, :], zero).then_inc(g.zeros, 16)
                pool.dma_start(io.acc[r:r + P, :], zero).then_inc(g.zeros, 16)
            pool.wait_ge(fill_out, 16)

            def to_lists(t):
                pool.wait_ge(data_ready, t + 1)
                for n in range(t * TOP_K, (t + 1) * TOP_K):
                    pool.indirect_dma_start(out=io.lists, out_offset=bass.IndirectOffsetOnAxis(ap=dest_i[:, n:n + 1], axis=0),
                                            in_=entry[:, 2 * n:2 * n + 2], in_offset=None,
                                            bounds_check=EXPERTS * LIST - 1, oob_is_err=True).then_inc(g.listed, 16)

            for t in range(TT):
                pool.wait_ge(normed, t + 1)
                pool.dma_start(io.h2[t * P:(t + 1) * P, :], h2[:, t % 2, :]).then_inc(h2_out[t % 2], 16)
                if t >= 2:
                    to_lists(t - 2)
            for s in range(2):
                pool.wait_ge(h2_out[s], 16 * TT // 2)
            to_lists(TT - 2)
            to_lists(TT - 1)

        @block.tensor
        def _(pe):
            pe.wait_ge(w_out_in, 16)
            pe.wait_ge(router_in, 32)

            def project(t):
                if t >= 2:
                    pe.wait_ge(added, t - 1)
                for h in range(2):
                    for k in range(KT):
                        last = nc.tensor.matmul(bank(g, 2 * (t % 2) + h), merged[:, k, t * P:(t + 1) * P], w_out[:, k, h * HALF:(h + 1) * HALF],
                                                start=(k == 0), stop=(k == KT - 1))
                last.then_inc(made, 1)

            def turn(t):
                pe.wait_ge(normed, t + 1)
                if t >= 1:
                    pe.wait_ge(h2t_ready, t)
                for k in range(KT):
                    last = nc.tensor.transpose(bank(g, 4, 2)[:, k * P:(k + 1) * P], h2[:, t % 2, k * P:(k + 1) * P], g.ident[:, :])
                last.then_inc(turned, 1)

            def route(t):
                pe.wait_ge(h2t_ready, t + 1)
                if t >= 1:
                    pe.wait_ge(biased, t)
                for k in range(KT):
                    last = nc.tensor.matmul(bank(g, 6)[:, 0:EXPERTS], h2t[:, t % 2, k, :], w_r[:, k, :], start=(k == 0), stop=(k == KT - 1))
                last.then_inc(scored, 1)

            def rank(t):
                pe.wait_ge(ranked, t + 1)
                if t >= 1:
                    pe.wait_ge(data_ready, t)
                cols = bank(g, 7)[:, t * EXPERTS:(t + 1) * EXPERTS]
                nc.tensor.matmul(cols, g.before[:, :], member[:, t, :], start=True, stop=False)
                nc.tensor.matmul(cols, g.ones[:, :], earlier[:, t, :], start=False, stop=True).then_inc(placed, 1)

            project(0)
            for t in range(TT):
                if t + 1 < TT:
                    project(t + 1)
                turn(t)
                if t >= 1:
                    route(t - 1)
                if t >= 2:
                    rank(t - 2)
            route(TT - 1)
            rank(TT - 2)
            rank(TT - 1)

        @block.scalar
        def _(act):
            def exp(t):
                act.wait_ge(shifted, t + 1)
                tile = wts[:, t * TOP_K:(t + 1) * TOP_K]
                nc.scalar.activation(tile, tile, ACT.Exp).then_inc(exps, 1)

            for t in range(TT):
                act.wait_ge(added, t + 1)
                nc.scalar.activation(h2[:, t % 2, :], x2[:, t, :], ACT.Square, accum_out=total[:, t:t + 1]).then_inc(squared, 1)
                act.wait_ge(squared, t + 1)
                nc.scalar.activation(root[:, t:t + 1], total[:, t:t + 1], ACT.Sqrt, scale=1.0 / D, bias=g.eps[:, 0:1]).then_inc(rooted, 1)
                if t >= 2:
                    exp(t - 2)
            exp(TT - 2)
            exp(TT - 1)

        @block.vector
        def _(dve):
            chain = Chain(dve, chain_s)

            def add(t):
                s = t % 2
                if t >= 2:
                    dve.wait_ge(h2_out[s], 16 * (t // 2))
                    dve.wait_ge(turned, t - 1)
                dve.wait_ge(made, t + 1)
                dve.wait_ge(x_in[s], 16 * (t // 2) + 16)
                nc.vector.tensor_tensor(x2[:, t, :], bank(g, 2 * s, 2), x[:, s, :], ALU.add).then_inc(added, 1)

            def norm(t):
                dve.wait_ge(rooted, t + 1)
                chain.step(nc.vector.reciprocal(inv[:, t:t + 1], root[:, t:t + 1]))
                nc.vector.tensor_scalar(h2[:, t % 2, :], x2[:, t, :], inv[:, t:t + 1], None, ALU.mult).then_inc(normed, 1)

            def copy(t):
                dve.wait_ge(turned, t + 1)
                nc.vector.tensor_tensor(h2t[:, t % 2], bank(g, 4, 2).rearrange("p (k t) -> p k t", k=KT),
                                        g.gain_ffn[:, :].unsqueeze(2).broadcast_to([P, KT, P]), ALU.mult).then_inc(h2t_ready, 1)

            def choose(t):
                dve.wait_ge(scored, t + 1)
                nc.vector.tensor_tensor(logits[:, t, :], bank(g, 6)[:, 0:EXPERTS], b_r, ALU.add).then_inc(biased, 1)
                dve.wait_ge(biased, t + 1)
                chain.step(nc.vector.max(g.best[:, 8 * t:8 * t + 8], logits[:, t, :]))
                nc.vector.max_index(g.best_at[:, 8 * t:8 * t + 8], g.best[:, 8 * t:8 * t + 8], logits[:, t, :]).then_inc(chosen, 1)

            best_at = g.best_at[:, :].rearrange("p (t k) -> p t k", t=TT)
            best_v = g.best[:, :].rearrange("p (t k) -> p t k", t=TT)

            def member_of(t):
                ranks = slice(t * TOP_K, (t + 1) * TOP_K)
                dve.wait_ge(chosen, t + 1)
                nc.vector.tensor_tensor(wts[:, ranks], best_v[:, t, 0:TOP_K], best_v[:, t, 0:1].broadcast_to([P, TOP_K]),
                                        ALU.subtract).then_inc(shifted, 1)
                chain.step(nc.vector.tensor_copy(best_f[:, ranks], best_at[:, t, 0:TOP_K]))
                chain.step(nc.vector.tensor_tensor(chosen_by[:, ranks, :], v.expert_row.unsqueeze(1).broadcast_to([P, TOP_K, EXPERTS]),
                                                   best_f[:, ranks].unsqueeze(2).broadcast_to([P, TOP_K, EXPERTS]), ALU.is_equal))
                chain.step(nc.vector.reduce_sum(member[:, t, :], chosen_by[:, ranks, :].rearrange("p k e -> p e k"), AX))
                nc.vector.tensor_tensor(earlier[:, t + 1, :], earlier[:, t, :], member[:, t, :], ALU.add).then_inc(ranked, 1)
                dve.wait_ge(ranked, t + 1)

            def place_of(t):
                ranks = slice(t * TOP_K, (t + 1) * TOP_K)
                dve.wait_ge(exps, t + 1)
                chain.step(nc.vector.reduce_sum(sums[:, t:t + 1], wts[:, ranks], AX))
                chain.step(nc.vector.reciprocal(sums[:, t:t + 1], sums[:, t:t + 1]))
                chain.step(nc.vector.tensor_scalar(wts[:, ranks], wts[:, ranks], sums[:, t:t + 1], None, ALU.mult))
                chain.step(nc.vector.tensor_copy(entry.rearrange("p (n c) -> p n c", c=2)[:, ranks, 1], wts[:, ranks]))
                chain.step(nc.vector.tensor_tensor(weighted, chosen_by[:, ranks, :], wts[:, ranks].unsqueeze(2).broadcast_to([P, TOP_K, EXPERTS]), ALU.mult))
                chain.step(nc.vector.reduce_sum(v.gates[:, t, :], weighted.rearrange("p k e -> p e k"), AX))
                dve.wait_ge(placed, t + 1)
                chain.step(nc.vector.tensor_tensor(place[:, t, :], bank(g, 7)[:, t * EXPERTS:(t + 1) * EXPERTS], start_row, ALU.add))
                chain.step(nc.vector.tensor_tensor(picked[:, ranks, :], chosen_by[:, ranks, :], place[:, t:t + 1, :].broadcast_to([P, TOP_K, EXPERTS]), ALU.mult))
                chain.step(nc.vector.reduce_sum(dest[:, ranks], picked[:, ranks, :], AX))
                nc.vector.tensor_copy(dest_i[:, ranks], dest[:, ranks]).then_inc(data_ready, 1)

            dve.wait_ge(ids, 8)
            chain.step(nc.vector.tensor_copy(v.expert_row, expert_i))
            chain.step(nc.vector.tensor_scalar(start_row, v.expert_row, float(LIST), None, ALU.mult))
            chain.step(nc.vector.memset(earlier[:, 0, :], 0.0))
            dve.wait_ge(router_in, 32)
            add(0)
            for t in range(TT):
                norm(t)
                if t + 1 < TT:
                    add(t + 1)
                copy(t)
                if t >= 1:
                    choose(t - 1)
                    member_of(t - 1)
                if t >= 2:
                    place_of(t - 2)
            choose(TT - 1)
            member_of(TT - 1)
            place_of(TT - 2)
            place_of(TT - 1)
            dve.wait_ge(data_ready, TT)


def stage_route(g, io):
    nc = g.nc
    chain_s, counted, gates_turned, gates_out, bias_made, based = (
        g.sem("table_" + n) for n in ("chain", "counted", "gates_turned", "gates_out", "bias_made", "based"))
    bias_in, bias_turned = g.sem("table_bias_in"), g.sem("table_bias_turned")
    v = routing_views(g)
    cnt, more, upto = (at(g, EXPERT_ROW + 256 + 32 * n, EXPERTS) for n in range(3))
    tri2, past = tiled(g, CHOSEN, EXPERTS, EXPERTS), tiled(g, PICKED, EXTRA_JOBS, EXPERTS)
    past2 = tiled(g, PICKED + 512, EXTRA_JOBS, EXPERTS)
    job_e, job_d, job_n, job_w = (at(g, EXPERT_ROW + 368 + 16 * n, EXTRA_JOBS) for n in range(4))
    b1_in, b2_in = at(g, B_IN, 2 * D_EXP)[0:EXPERTS], at(g, B_IN + 2 * D_EXP, D)[0:EXPERTS]
    b1_t = tiled(g, B1_T, EXPERTS, 2 * FT)
    gates_t = at(g, ZERO, SEQ)[0:EXPERTS]

    with nc.Block() as block:

        @block.gpsimd
        def _(pool):
            pool.wait_ge(g.listed, 16 * TK)
            pool.wait_ge(g.zeros, 16 * 2 * JH)

        @block.sync
        def _(sp):
            sp.dma_start(b2_in, io.b2).then_inc(bias_in, 16)
            sp.dma_start(b1_in, io.b1).then_inc(bias_in, 16)
            for t in range(TT):
                sp.wait_ge(based, t + 1)
                sp.dma_start(io.acc[t * P:(t + 1) * P, :], v.x2[:, t, :]).then_inc(g.acc_out, 16)
            for slot in (2, 3):
                load_weights(g, io, sp, 0, slot)

        @block.tensor
        def _(pe):
            nc.tensor.matmul(bank(g, 1)[:, 0:EXPERTS], g.ones[:, :], v.earlier[:, TT, :], start=True, stop=True).then_inc(counted, 1)
            for t in range(TT):
                last = nc.tensor.transpose(bank(g, 4, 2)[0:EXPERTS, t * P:(t + 1) * P], v.gates[:, t, :], g.ident[:, :])
            last.then_inc(gates_turned, 1)
            pe.wait_ge(bias_in, 32)
            for f in range(2 * FT):
                last = nc.tensor.transpose(bank(g, 2)[:, f * EXPERTS:(f + 1) * EXPERTS], b1_in[:, f * P:(f + 1) * P], g.ident[0:EXPERTS, 0:EXPERTS])
            last.then_inc(bias_turned, 1)
            pe.wait_ge(gates_out, 1)
            for t in range(TT):
                if t >= 2:
                    pe.wait_ge(based, t - 1)
                for h in range(2):
                    last = nc.tensor.matmul(bank(g, 4 + 2 * (t % 2) + h), gates_t[:, t * P:(t + 1) * P], b2_in[:, h * HALF:(h + 1) * HALF],
                                            start=True, stop=True)
                last.then_inc(bias_made, 1)

        @block.scalar
        def _(act):
            act.wait_ge(gates_turned, 1)
            nc.scalar.activation(gates_t, bank(g, 4, 2)[0:EXPERTS], ACT.Copy).then_inc(gates_out, 1)

        @block.vector
        def _(dve):
            chain = Chain(dve, chain_s)
            for t in range(TT):
                dve.wait_ge(bias_made, t + 1)
                nc.vector.tensor_tensor(v.x2[:, t, :], v.x2[:, t, :], bank(g, 4 + 2 * (t % 2), 2), ALU.add).then_inc(based, 1)
            dve.wait_ge(counted, 1)
            chain.step(nc.vector.tensor_copy(cnt, bank(g, 1)[:, 0:EXPERTS]))
            chain.step(nc.vector.tensor_copy(g.job_count[:, 0:EXPERTS], cnt))
            chain.step(nc.vector.tensor_scalar(more, cnt, float(JOB), None, ALU.is_gt))
            for j in range(2, LIST // JOB):
                chain.step(nc.vector.scalar_tensor_tensor(out=more, in0=cnt, scalar=float(JOB * j), in1=more, op0=ALU.is_gt, op1=ALU.add))
            chain.step(nc.vector.tensor_tensor(tri2, v.tri, more.unsqueeze(1).broadcast_to([P, EXPERTS, EXPERTS]), ALU.mult))
            chain.step(nc.vector.reduce_sum(upto, tri2, AX))
            chain.step(nc.vector.tensor_scalar(g.total[:, 0:1], upto[:, EXPERTS - 1:EXPERTS], float(EXPERTS), None, ALU.add))
            chain.step(nc.vector.tensor_copy(job_e, v.job_no))
            chain.step(nc.vector.tensor_tensor(past, job_e.unsqueeze(2).broadcast_to([P, EXTRA_JOBS, EXPERTS]),
                                               upto.unsqueeze(1).broadcast_to([P, EXTRA_JOBS, EXPERTS]), ALU.is_ge))
            chain.step(nc.vector.tensor_tensor(past2, past, more.unsqueeze(1).broadcast_to([P, EXTRA_JOBS, EXPERTS]), ALU.mult))
            chain.step(nc.vector.reduce_sum(job_d, past2, AX))
            chain.step(nc.vector.tensor_tensor(job_d, job_e, job_d, ALU.subtract))
            chain.step(nc.vector.tensor_scalar(job_d, job_d, 1.0, None, ALU.add))
            chain.step(nc.vector.reduce_sum(job_e, past, AX))
            chain.step(nc.vector.tensor_scalar(job_e, job_e, float(EXPERTS - 1), None, ALU.min))
            chain.step(nc.vector.tensor_copy(g.job_expert[:, 0:EXPERTS], v.expert_row))
            chain.step(nc.vector.tensor_copy(g.job_expert[:, EXPERTS:JOBS], job_e))
            chain.step(nc.vector.tensor_copy(job_w, job_d))
            chain.step(nc.vector.scalar_tensor_tensor(out=job_d, in0=job_e, scalar=float(LIST // JOB), in1=job_d, op0=ALU.mult, op1=ALU.add))
            chain.step(nc.vector.tensor_scalar(g.job_place[:, EXPERTS:JOBS], job_d, float(EXPERTS * LIST // JOB - 1), None, ALU.min))
            chain.step(nc.vector.tensor_scalar(g.job_place[:, 0:EXPERTS], v.expert_row, float(LIST // JOB), None, ALU.mult))
            chain.step(nc.vector.memset(g.job_place[:, JOBS:], 0))
            chain.step(nc.vector.tensor_tensor(past, v.expert_row.unsqueeze(1).broadcast_to([P, EXTRA_JOBS, EXPERTS]),
                                               job_e.unsqueeze(2).broadcast_to([P, EXTRA_JOBS, EXPERTS]), ALU.is_equal))
            chain.step(nc.vector.tensor_tensor(past2, past, cnt.unsqueeze(1).broadcast_to([P, EXTRA_JOBS, EXPERTS]), ALU.mult))
            chain.step(nc.vector.reduce_sum(job_n, past2, AX))
            chain.step(nc.vector.scalar_tensor_tensor(out=job_n, in0=job_w, scalar=-float(JOB), in1=job_n, op0=ALU.mult, op1=ALU.add))
            chain.step(nc.vector.tensor_scalar(g.job_count[:, EXPERTS:JOBS], job_n, 0.0, None, ALU.max))
            chain.step(nc.vector.memset(g.job_count[:, JOBS:], 0))
            dve.wait_ge(bias_turned, 1)
            src = bank(g, 2)[:, :].rearrange("p (f e) -> p e f", e=EXPERTS)
            chain.step(nc.vector.tensor_copy(b1_t[:, :, 0:FT], src[:, :, 0:FT]))
            chain.step(nc.vector.tensor_scalar(b1_t[:, :, FT:], src[:, :, FT:], 1.0, None, ALU.add))


def weight_slots(g):
    return ([g.arena[:, R + c * RING_SLOT:R + (c + 1) * RING_SLOT].rearrange("p (s k n) -> p s k n", s=2, k=KT) for c in range(4)],
            [tiled(g, R + (4 + c) * RING_SLOT, FT, HALF) for c in range(2)])


def load_weights(g, io, eng, expert, slot):
    w1, w2 = weight_slots(g)
    if slot < 4:
        src = io.w1.rearrange("e (k p) n -> p e k n", p=P)
        for s in range(2):
            col = s * D_EXP + slot * 2 * P
            eng.dma_start(w1[slot][:, s].unsqueeze(1), src[:, bass.ds(expert, 1), :, col:col + 2 * P]).then_inc(g.w_in[slot], 16)
    else:
        src = io.w2.rearrange("e (k p) n -> p e k n", p=P)
        col = (slot - 4) * HALF
        eng.dma_start(w2[slot - 4].unsqueeze(1), src[:, bass.ds(expert, 1), :, col:col + HALF]).then_inc(g.w_in[slot], 16)


def stage_experts(g, io):
    nc = g.nc
    ent_in, gathered, scattered, x_turned, xt_dve, xt_act = (
        g.sem("moe_" + n) for n in ("ent_in", "gathered", "scattered", "x_turned", "xt_dve", "xt_act"))
    rows_known, yg_free, issued = g.sem("moe_rows_known"), g.sem("moe_yg_free"), g.sem("moe_issued")
    made, g_ready, l_ready, s_ready, gs_ready, act_ready = (
        g.sem("moe_" + n) for n in ("made", "g_ready", "l_ready", "s_ready", "gs_ready", "act_ready"))
    y_made, yg_dve, yg_act = (g.sem("moe_" + n) for n in ("y_made", "yg_dve", "yg_act"))
    w1, w2 = weight_slots(g)
    xg, yg = tiled(g, XG, JH, D), tiled(g, YG, JH, D)
    xt, act_t = tiled(g, XT, KT, JOB), tiled(g, ACT_T, FT, JOB)
    glu, sig, lin = at(g, EG, HALF), at(g, EG + HALF, HALF), at(g, EG + 2 * HALF, HALF)
    ent = g.arena[:, ENT:ENT + (JOBS + 2) * 2 * JH].rearrange("p (n h c) -> p n h c", h=JH, c=2)
    b1_t = tiled(g, B1_T, EXPERTS, 2 * FT)
    rows_in, rows_out = (at(g, ENT + (JOBS + 2) * 2 * JH + JH * s, JH).bitcast(I32) for s in range(2))
    weight = lambda n, h: g.arena[:, bass.ds(2 * JH * n + (ENT + 2 * h + 1), 1)]
    entries = io.lists.rearrange("(n h p) c -> p n h c", p=P, h=JH)

    with nc.Block() as block:

        @block.sync
        def _(sp):
            sp.wait_ge(g.acc_out, 16 * TT)
            for slot in (4, 5):
                load_weights(g, io, sp, 0, slot)
            total = sp.value_load(g.total[0:1, 0:1], min_val=EXPERTS, max_val=JOBS)
            with sp.Fori(1, JOBS) as n:
                with sp.If(total > n):
                    expert = sp.value_load(g.job_expert[0:1, bass.ds(n, 1)], min_val=0, max_val=EXPERTS - 1)
                    for c in range(6):
                        if c < 4:
                            sp.wait_ge(made, 8 * n + (2 * c - 6))
                        else:
                            sp.wait_ge(y_made, 4 * n + (2 * c - 10))
                        load_weights(g, io, sp, expert, c)
                with sp.Else():
                    sp.nop()

        @block.gpsimd
        def _(pool):
            def load_entries(n):
                place = pool.value_load(g.job_place[0:1, bass.ds(n, 1)], min_val=0, max_val=EXPERTS * LIST // JOB - 1)
                pool.dma_start(ent[:, bass.ds(n, 1)], entries[:, bass.ds(place, 1)]).then_inc(ent_in, 16)

            def gather(n, seen):
                nc.gpsimd.tensor_copy(rows_in, ent.bitcast(I32)[:, bass.ds(n, 1), :, 0]).then_inc(rows_known, 1)
                pool.wait_ge(rows_known, seen)
                pool.sem_inc(issued, 1)
                for h in range(JH):
                    pool.indirect_dma_start(out=xg[:, h, :], out_offset=None, in_=io.h2,
                                            in_offset=bass.IndirectOffsetOnAxis(ap=rows_in[:, h:h + 1], axis=0),
                                            bounds_check=ROWS - 1, oob_is_err=True).then_inc(gathered, 16)

            pool.sem_inc(yg_free, 1)
            load_entries(0)
            pool.wait_ge(ent_in, 16)
            gather(0, 1)
            load_entries(1)
            pool.wait_ge(g.acc_out, 16 * TT)
            total = pool.value_load(g.total[0:1, 0:1], min_val=EXPERTS, max_val=JOBS)
            with pool.Fori(0, JOBS) as n:
                with pool.If(total > n):
                    pool.wait_ge(ent_in, 16 * n + 32)
                    pool.wait_ge(x_turned, 4 * n + 4)
                    gather(n + 1, 2 * n + 2)
                    load_entries(n + 2)
                    pool.wait_ge(yg_dve, 2 * n + 4)
                    pool.wait_ge(yg_act, 2 * n + 4)
                    nc.gpsimd.tensor_copy(rows_out, ent.bitcast(I32)[:, bass.ds(n, 1), :, 0]).then_inc(rows_known, 1)
                    pool.wait_ge(rows_known, 2 * n + 3)
                    pool.sem_inc(issued, 1)
                    for h in range(JH):
                        pool.indirect_dma_start(out=io.acc, out_offset=bass.IndirectOffsetOnAxis(ap=rows_out[:, h:h + 1], axis=0),
                                                in_=yg[:, h, :], in_offset=None, compute_op=ALU.add,
                                                bounds_check=ROWS - 1, oob_is_err=True).then_inc(scattered, 16)
                    pool.wait_ge(scattered, 32 * n + 32)
                    pool.sem_inc(yg_free, 1)
                with pool.Else():
                    pool.nop()
            pool.wait_ge(ent_in, 16 * total + 32)

        @block.tensor
        def _(pe):
            def turn_x(halves):
                for k in range(KT):
                    for h in range(halves):
                        last = nc.tensor.transpose(bank(g, 4 + k // 2)[:, (k % 2) * JOB + h * P:(k % 2) * JOB + (h + 1) * P],
                                                   xg[:, h, k * P:(k + 1) * P], g.ident[:, :])
                    if k % 2 == 1:
                        last.then_inc(x_turned, 1)

            def job(n, width, next_count):
                pe.wait_ge(xt_dve, 2 * n + 2)
                pe.wait_ge(xt_act, 4 * n + 4)
                for c in range(4):
                    pe.wait_ge(g.w_in[c], 32 * n + 32)
                    if c >= 2:
                        pe.wait_ge(act_ready, 4 * n + (c - 1))
                    for s in range(2):
                        if c < 2:
                            pe.wait_ge((yg_dve, yg_act)[s], 2 * n + (c + 1))
                        for a in range(2):
                            for k in range(KT):
                                last = nc.tensor.matmul(bank(g, 2 * (c % 2) + s)[:, a * JOB:a * JOB + width], w1[c][:, s, k, a * P:(a + 1) * P],
                                                        xt[:, k, 0:width], start=(k == 0), stop=(k == KT - 1))
                        last.then_inc(made, 1)
                pe.wait_ge(gathered, 32 * n + 64)
                with pe.If(next_count > P):
                    turn_x(2)
                with pe.Else():
                    turn_x(1)

                halves = 1 if width <= P else 2

                def second(c, h, fs):
                    for f in fs:
                        last = nc.tensor.matmul(bank(g, 2 * h + c), act_t[:, f, h * P:(h + 1) * P], w2[c][:, f, :], start=(f == 0), stop=(f == FT - 1))
                    return last

                pe.wait_ge(act_ready, 4 * n + 3)
                pe.wait_ge(g.w_in[4], 16 * n + 16)
                second(0, 0, range(6))
                pe.wait_ge(act_ready, 4 * n + 4)
                second(0, 0, range(6, FT)).then_inc(y_made, 3 - halves)
                if halves == 2:
                    second(0, 1, range(FT)).then_inc(y_made, 1)
                pe.wait_ge(g.w_in[5], 16 * n + 16)
                second(1, 0, range(FT)).then_inc(y_made, 3 - halves)
                if halves == 2:
                    second(1, 1, range(FT)).then_inc(y_made, 1)

            def by_count(n, widths, count, next_count):
                if len(widths) == 1:
                    job(n, widths[0], next_count)
                    return
                with pe.If(count > widths[0]):
                    by_count(n, widths[1:], count, next_count)
                with pe.Else():
                    job(n, widths[0], next_count)

            pe.wait_ge(gathered, 32)
            turn_x(2)
            total = pe.value_load(g.total[0:1, 0:1], min_val=EXPERTS, max_val=JOBS)
            with pe.Fori(0, JOBS) as n:
                with pe.If(total > n):
                    count = pe.value_load(g.job_count[0:1, bass.ds(n, 1)], min_val=0, max_val=SEQ)
                    next_count = pe.value_load(g.job_count[0:1, bass.ds(n + 1, 1)], min_val=0, max_val=SEQ)
                    by_count(n, WIDTHS, count, next_count)
                with pe.Else():
                    pe.nop()

        @block.scalar
        def _(act):
            def take_x(n):
                for k in range(KT // 2, KT):
                    if k % 2 == 0:
                        act.wait_ge(x_turned, 4 * n + k // 2 + 1)
                    nc.scalar.activation(xt[:, k, :], bank(g, 4 + k // 2)[:, (k % 2) * JOB:(k % 2 + 1) * JOB], ACT.Copy,
                                         scale=g.gain_ffn[:, k:k + 1]).then_inc(xt_act, 1)

            act.sem_inc(yg_act, 2)
            take_x(0)
            total = act.value_load(g.total[0:1, 0:1], min_val=EXPERTS, max_val=JOBS)
            with act.Fori(0, JOBS) as n:
                with act.If(total > n):
                    for c in range(4):
                        act.wait_ge(g_ready, 8 * n + 2 * c + 2)
                        nc.scalar.activation(sig, glu, ACT.Sigmoid, scale=ALPHA).then_inc(s_ready, 1)
                    take_x(n + 1)
                    act.wait_ge(yg_free, n + 1)
                    for h in range(JH):
                        act.wait_ge(y_made, 4 * n + (3 + h))
                        nc.scalar.activation(yg[:, h, HALF:], bank(g, 2 * h + 1), ACT.Copy, scale=weight(n, h)).then_inc(yg_act, 1)
                with act.Else():
                    act.nop()

        @block.vector
        def _(dve):
            def take_x(n):
                for b in range(2):
                    dve.wait_ge(x_turned, 4 * n + b + 1)
                    nc.vector.tensor_tensor(xt[:, 2 * b:2 * b + 2, :], bank(g, 4 + b).rearrange("p (k t) -> p k t", k=2),
                                            g.gain_ffn[:, 2 * b:2 * b + 2].unsqueeze(2).broadcast_to([P, 2, JOB]), ALU.mult).then_inc(xt_dve, 1)

            dve.sem_inc(yg_dve, 2)
            take_x(0)
            total = dve.value_load(g.total[0:1, 0:1], min_val=EXPERTS, max_val=JOBS)
            with dve.Fori(0, JOBS) as n:
                with dve.If(total > n):
                    expert = dve.value_load(g.job_expert[0:1, bass.ds(n, 1)], min_val=0, max_val=EXPERTS - 1)
                    for c in range(4):
                        for s, (dst, ready, limit) in enumerate(((glu, g_ready, LIMIT), (lin, l_ready, LIMIT + 1.0))):
                            dve.wait_ge(made, 8 * n + 2 * c + s + 1)
                            for a in range(2):
                                nc.vector.tensor_scalar(dst[:, a * JOB:(a + 1) * JOB], bank(g, 2 * (c % 2) + s)[:, a * JOB:(a + 1) * JOB],
                                                        b1_t[:, bass.ds(expert, 1), s * FT + 2 * c + a], limit, ALU.add, ALU.min).then_inc(ready, 1)
                        dve.wait_ge(s_ready, 4 * n + c + 1)
                        dve.wait_ge(g_ready, 8 * n + 2 * c + 2)
                        nc.vector.tensor_tensor(sig, glu, sig, ALU.mult).then_inc(gs_ready, 1)
                        dve.wait_ge(gs_ready, 4 * n + c + 1)
                        dve.wait_ge(l_ready, 8 * n + 2 * c + 2)
                        nc.vector.scalar_tensor_tensor(out=at(g, ACT_T + 2 * c * JOB, 2 * JOB), in0=lin, scalar=1.0 - LIMIT, in1=sig,
                                                       op0=ALU.max, op1=ALU.mult).then_inc(act_ready, 1)
                        dve.wait_ge(act_ready, 4 * n + c + 1)
                    take_x(n + 1)
                    dve.wait_ge(yg_free, n + 1)
                    for h in range(JH):
                        dve.wait_ge(y_made, 4 * n + (1 + h))
                        nc.vector.tensor_scalar(yg[:, h, 0:HALF], bank(g, 2 * h), weight(n, h), None, ALU.mult).then_inc(yg_dve, 1)
                with dve.Else():
                    dve.nop()


def stage_final(g, io):
    nc = g.nc
    gain_in, rows_in = g.sem("final_gain_in"), [g.sem(f"final_in{s}") for s in range(2)]
    squared, rooted, inverted, normed, stored = (g.sem("final_" + n) for n in ("squared", "rooted", "inverted", "normed", "stored"))
    x, gain, y = tiled(g, 0, TT, D), at(g, TT * D, D), tiled(g, (TT + 1) * D, TT, D)
    total, root, inv = g.stat[:, 0:8], g.stat[:, 8:16], g.stat[:, 16:24]

    with nc.Block() as block:

        @block.sync
        def _(sp):
            sp.dma_start(gain, io.norm_final.partition_broadcast(P)).then_inc(gain_in, 16)
            for s, (a, b) in enumerate(((0, 2), (2, TT))):
                sp.dma_start(x[:, a:b, :], io.acc[a * P:b * P, :].rearrange("(t p) d -> p t d", p=P)).then_inc(rows_in[s], 16)

        @block.gpsimd
        def _(pool):
            for t in range(TT):
                pool.wait_ge(normed, t + 1)
                pool.dma_start(io.out[0, t * P:(t + 1) * P, :], y[:, t, :]).then_inc(stored, 16)
            pool.wait_ge(stored, 16 * TT)

        @block.scalar
        def _(act):
            for t in range(TT):
                act.wait_ge(rows_in[min(t // 2, 1)], 16)
                nc.scalar.activation(y[:, t, :], x[:, t, :], ACT.Square, accum_out=total[:, t:t + 1]).then_inc(squared, 1)
                act.wait_ge(squared, t + 1)
                nc.scalar.activation(root[:, t:t + 1], total[:, t:t + 1], ACT.Sqrt, scale=1.0 / D, bias=g.eps[:, 0:1]).then_inc(rooted, 1)

        @block.vector
        def _(dve):
            dve.wait_ge(gain_in, 16)
            for t in range(TT):
                dve.wait_ge(rooted, t + 1)
                nc.vector.reciprocal(inv[:, t:t + 1], root[:, t:t + 1]).then_inc(inverted, 1)
                dve.wait_ge(inverted, t + 1)
                nc.vector.scalar_tensor_tensor(out=y[:, t, :], in0=x[:, t, :], scalar=inv[:, t:t + 1], in1=gain,
                                               op0=ALU.mult, op1=ALU.mult).then_inc(normed, 1)


STAGES = [stage_norm, stage_latents, stage_mla, stage_diff, stage_merge, stage_out, stage_route, stage_experts, stage_final]


def program(nc, io):
    ctx = ExitStack()
    with ctx, nc.allow_non_contiguous_dma(reason="columns of gains and biases: a few KiB"):
        g = setup(nc, ctx)
        for stage in STAGES:
            stage(g, io)


_INS = ['x', 'positions', 'norm_mix', 'w_in', 'mla_q_norm', 'w_q_b', 'mla_kv_norm', 'w_kv_b', 'diff_lambda', 'diff_subln',
        'rel_bias', 'w_up_mla', 'w_up_diff', 'w_out', 'norm_ffn', 'w_router', 'b_router', 'w1', 'b1', 'w2', 'b2', 'norm_final']


def kernel(**inputs):
    import numpy as _np
    import concourse.bacc as _bacc
    from concourse import mybir as _mybir
    from concourse.bass_utils import run_bass_kernel_spmd as _run

    nc = _bacc.Bacc("TRN2", target_bir_lowering=False, num_devices=1)
    arrays, dram = {}, {}
    given = {name: inputs[name] for name in _INS} | {"rope_rows": rope_rows(), "bucket_rows": rel_buckets()}
    for name, a in given.items():
        a = _np.ascontiguousarray(a)
        if a.ndim > 1 and a.shape[0] == 1 and name not in ("x", "positions"):
            a = a.reshape(a.shape[1:])
        if a.ndim == 1:
            a = a.reshape(1, -1)
        arrays[f"in_{name}"] = a
        dram[name] = nc.dram_tensor(f"in_{name}", a.shape, _mybir.dt.from_np(a.dtype), kind="ExternalInput").ap()
    dram['out'] = nc.dram_tensor("out_0", (1, SEQ, D), _mybir.dt.float32, kind="ExternalOutput").ap()
    dram['acc'] = nc.dram_tensor("acc_rows", (ROWS, D), F32).ap()
    dram['h2'] = nc.dram_tensor("h2_rows", (ROWS, D), F32).ap()
    dram['lists'] = nc.dram_tensor("lists", (EXPERTS * LIST, 2), F32).ap()
    program(nc, Dram(dram))
    r = _run(nc, [arrays], core_ids=[0])
    return r.results[0]["out_0"]
```

```python
from contextlib import ExitStack

import numpy as np
import concourse.bass as bass
from concourse import mybir

F32 = mybir.dt.float32
I32 = mybir.dt.int32
U32 = mybir.dt.uint32
ALU = mybir.AluOpType
ACT = mybir.ActivationFunctionType
AX = mybir.AxisListType.X

P = 128
SEQ = 1024
D = 1024
KT = D // P
TT = SEQ // P
HALF = 512
EPS = 1e-5
NEG = -1e30

MLA_HEADS, NOPE, ROPE, MLA_V = 8, 64, 32, 64
Q_RANK, KV_RANK = 256, 128
HEAD_QK = NOPE + ROPE
DIFF_HEADS, DIFF_DIM, DIFF_V = 4, 64, 128
LAMBDA_INIT = 0.8 - 0.6
BUCKETS, MAX_DIST = 32, 128
MLA_SCALE = float(HEAD_QK) ** -0.5
DIFF_SCALE = float(DIFF_DIM) ** -0.5
OFF_KV = Q_RANK
OFF_KR = OFF_KV + KV_RANK
OFF_DQ = OFF_KR + ROPE
OFF_DK = OFF_DQ + DIFF_HEADS * 2 * DIFF_DIM
OFF_DV = OFF_DK + DIFF_HEADS * 2 * DIFF_DIM
OFF_GATE = OFF_DV + DIFF_HEADS * DIFF_V

EXPERTS, TOP_K, D_EXP = 32, 4, 1024
FT = D_EXP // P
LIMIT, ALPHA = 7.0, 1.702
JOB = 256
JH = JOB // P
LIST = SEQ
EXTRA_JOBS = SEQ * TOP_K // JOB
JOBS = EXPERTS + EXTRA_JOBS
TK = TT * TOP_K
WIDTHS = tuple(range(P, JOB + 1, 16))
DUMMY = SEQ
ROWS = SEQ + JOB

HT = 0
Y_MLA = 8192
Y_DIFF = 12288
R = 16384
RING_SLOT = 4096
RING_SLOTS = 6
X_IN, H_N, SQ, W_DV = R, R + 4096, R + 6144, R + 8192
BIAS_T = R + 9216
W_PAIR = R + 8192
V_MLA, V_DIFF = R + 12288, R + 16384
QK = R + 20480
PROB, PROB_T, ROT = R, R + 4096, R + 6144
QA, CKV, COS, SIN, KR, W_ST = 40960, 43008, 44032, 45056, 46080, 47104
ARENA = 51200
SEGMENTS = (0, 8192, R, R + 16384, 40960, 43008)
GENERAL, MASK_TILE = R, R + 10240
Y_T, MERGED, W_MERGE, GATE_T = R, 0, R + 8192, R + 14336
W_OUT, X_RES, H2, H2_T, X2 = R + 8192, 8192, 12288, 14336, R + 16384
W_ROUTER, B_ROUTER, LOGITS = 40960, 41216, 41248
CHOSEN, GATES, WEIGHTED = 41504, 42528, 42784
PICKED, MEMBER, EARLIER, PLACE, EXPERT_ROW, ENTRY, FILL, TRI, B_IN, ZERO = (
    43008, 44032, 44288, 44576, 44832, 45280, 45344, 45856, 46880, 49952)
XG, B1_T, ACT_T, XT, EG, YG = 0, 2048, 2560, 4608, 6656, 40960


def rel_buckets():
    n = np.maximum(255 - np.arange(383), 0)
    exact = BUCKETS // 2
    nf = np.maximum(n, 1).astype(np.float32)
    large = exact + (np.log(nf / np.float32(exact)) / np.float32(np.log(MAX_DIST / exact)) * (BUCKETS - exact)).astype(np.int32)
    b = np.where(n < exact, n, np.minimum(large, BUCKETS - 1))
    return (np.arange(BUCKETS)[:, None] == b[None, :]).astype(np.float32)


def rope_rows():
    half = np.arange(0, ROPE, 2, dtype=np.float32) / np.float32(ROPE)
    f = np.tile(np.power(np.float32(10000.0), -half), 2 * P // ROPE)
    sign = np.tile(np.repeat(np.float32([-1.0, 1.0]), ROPE // 2), P // ROPE)
    return np.stack([f, sign], axis=1).astype(np.float32)


class Core:

    def __init__(self, nc):
        self.nc = nc


class Dram:

    def __init__(self, a):
        self.x, self.positions, self.norm_mix, self.w_in = a["x"], a["positions"], a["norm_mix"], a["w_in"]
        self.mla_q_norm, self.w_q_b, self.mla_kv_norm, self.w_kv_b = a["mla_q_norm"], a["w_q_b"], a["mla_kv_norm"], a["w_kv_b"]
        self.diff_lambda, self.diff_subln, self.rel_bias = a["diff_lambda"], a["diff_subln"], a["rel_bias"]
        self.w_up_mla, self.w_up_diff, self.w_out = a["w_up_mla"], a["w_up_diff"], a["w_out"]
        self.norm_ffn, self.w_router, self.b_router = a["norm_ffn"], a["w_router"], a["b_router"]
        self.w1, self.b1, self.w2, self.b2, self.norm_final = a["w1"], a["b1"], a["w2"], a["b2"], a["norm_final"]
        self.rope_rows, self.bucket_rows = a["rope_rows"], a["bucket_rows"]
        self.out, self.acc, self.h2, self.lists = a["out"], a["acc"], a["h2"], a["lists"]
        self.pair_bias = a["pair_bias"]


class Chain:

    def __init__(self, eng, sem, base=0):
        self.eng, self.sem, self.n = eng, sem, base

    def step(self, ins):
        ins.then_inc(self.sem, 1)
        self.n += 1
        self.eng.wait_ge(self.sem, self.n)


def segments(g, scope, which):
    sizes = [b - a for a, b in zip(SEGMENTS, SEGMENTS[1:] + (ARENA,))]
    for n in which:
        g.arena[n] = scope.enter_context(g.nc.sbuf_tensor(f"arena{n}_{g.generation}", [P, sizes[n]], F32))
    g.generation += 1


def parts(g, scope, n):
    g.parts = [scope.enter_context(g.nc.sbuf_tensor(f"parts{s}_{g.generation}", [P, 8 * SEQ], mybir.dt.float32r)) for s in range(n)]
    g.generation += 1


def setup(nc, ctx):
    g = Core(nc)
    g.generation = 0
    g.sb = lambda name, shape, dt=F32: ctx.enter_context(nc.sbuf_tensor(name, shape, dt))
    g.sem = lambda name: ctx.enter_context(nc.semaphore(name))
    g.banks = ctx.enter_context(nc.psum_tensor("banks", [P, 8 * HALF], F32))
    g.ident = g.sb("ident", [P, P])
    g.ones = g.sb("ones", [P, P])
    g.flip = g.sb("flip", [P, P])
    g.before = g.sb("before", [P, P])
    g.causal = g.sb("causal", [P, P])
    g.gain_mix = g.sb("gain_mix", [P, KT])
    g.gain_q = g.sb("gain_q", [P, 2])
    g.gain_kv = g.sb("gain_kv", [P, 1])
    g.gain_sub = g.sb("gain_sub", [P, 2])
    g.gain_ffn = g.sb("gain_ffn", [P, KT])
    g.eps = g.sb("eps", [P, 1])
    g.stat = g.sb("stat", [P, 32])
    g.lam = g.sb("lam", [P, 8])
    g.den = g.sb("den", [P, 64])
    g.ssq = g.sb("ssq", [P, 32])
    g.best, g.best_at = g.sb("best", [P, 8 * TT]), g.sb("best_at", [P, 8 * TT], U32)
    g.total = g.sb("total", [P, 1], I32)
    g.job_expert, g.job_place, g.job_count = (g.sb(n, [P, JOBS + 2], I32) for n in ("job_expert", "job_place", "job_count"))
    g.entries, g.rows = g.sb("entries", [P, (JOBS + 2) * 2 * JH]), g.sb("rows", [P, 2 * JH], I32)
    g.w_in = [g.sem(f"w_in{s}") for s in range(RING_SLOTS)]
    g.scattered_positions = g.sb("scattered_positions", [P, 1], I32)
    g.rope, g.bias_far = g.sb("rope", [P, 2]), g.sb("bias_far", [P, DIFF_HEADS])
    g.arena = [None] * len(SEGMENTS)
    segments(g, ctx, (0, 2, 4))
    g.squared, g.rooted, g.inverted, g.normed = (g.sem(n) for n in ("squared", "rooted", "inverted", "normed"))
    g.general_dma, g.general_steps = g.sem("general_dma"), g.sem("general_steps")
    g.w_pair, g.w_out_in = g.sem("w_pair"), [g.sem(f"w_out_in{c}") for c in range(2)]
    g.ent_in, g.gathered, g.rows_known = g.sem("entries_in"), g.sem("gathered"), g.sem("rows_known")
    g.carried = g.sem("carried")
    g.listed, g.zeros, g.acc_out = g.sem("listed"), g.sem("zeros"), g.sem("acc_out")
    return g


def at(g, off, n):
    for tensor, start in zip(g.arena, SEGMENTS):
        if start <= off and off + n <= start + tensor.shape[1]:
            return tensor[:, off - start:off - start + n]
    raise ValueError("a region lies across segments of the arena")


def tiled(g, off, a, n):
    return at(g, off, a * n).rearrange("p (a n) -> p a n", a=a)


def bank(g, b, n=1):
    return g.banks[:, b * HALF:(b + n) * HALF]


def stage_norm(g, io):
    nc = g.nc
    x_in = [g.sem(f"x_in{s}") for s in range(4)]
    gains_in, turned, ht_ready = (g.sem(n) for n in ("gains_in", "turned", "ht_ready"))
    squared, norm_known, inverted, h_ready = g.squared, g.rooted, g.inverted, g.normed
    filled, shaped = g.sem("filled"), g.sem("shaped")
    ht = tiled(g, HT, KT, SEQ)
    xs, hs = tiled(g, X_IN, 4, D), tiled(g, H_N, 2, D)
    total, root, inv = g.stat[:, 0:8], g.stat[:, 8:16], g.stat[:, 16:24]

    with nc.Block() as block:

        @block.sync
        def _(sp):
            for t in range(TT):
                if t >= 4:
                    sp.wait_ge(h_ready, t - 3)
                sp.dma_start(xs[:, t % 4, :], io.x[0, t * P:(t + 1) * P, :]).then_inc(x_in[t % 4], 16)

        @block.gpsimd
        def _(pool):
            for m, v in ((g.ident, 0.0), (g.ones, 1.0), (g.flip, 0.0), (g.before, 1.0), (g.causal, 0.0), (g.eps, EPS)):
                pool.memset(m[:, :], v).then_inc(filled, 1)
            pool.wait_ge(filled, 6)
            for m, op, fill, base, step, mult in (
                    (g.ident, ALU.not_equal, 1.0, 0, -1, 1),
                    (g.flip, ALU.not_equal, 1.0, -(P - 1), 1, 1),
                    (g.before, ALU.is_gt, 0.0, 0, 1, -1),
                    (g.causal, ALU.is_ge, NEG, 0, -1, 1)):
                pool.affine_select(out=m[:, :], in_=m[:, :], compare_op=op, fill=fill, base=base,
                                   pattern=[[step, P]], channel_multiplier=mult).then_inc(shaped, 1)
            pool.wait_ge(shaped, 4)

        @block.scalar
        def _(act):
            for gain, src in ((g.gain_mix, io.norm_mix), (g.gain_q, io.mla_q_norm), (g.gain_kv, io.mla_kv_norm),
                              (g.gain_sub, io.diff_subln), (g.gain_ffn, io.norm_ffn)):
                act.dma_start(gain[:, 0:src.shape[1] // P], src.rearrange("a (k p) -> (a p) k", p=P)).then_inc(gains_in, 16)
            act.wait_ge(filled, 6)
            with act.Fori(0, 2) as i:
                for s in range(4):
                    act.wait_ge(x_in[s], 16 * i + 16)
                    nc.scalar.activation(bank(g, 4 + 2 * (s % 2), 2), xs[:, s, :], ACT.Square,
                                         accum_out=total[:, bass.ds(4 * i + s, 1)]).then_inc(squared, 1)
                    act.wait_ge(squared, 4 * i + s + 1)
                    nc.scalar.activation(root[:, bass.ds(4 * i + s, 1)], total[:, bass.ds(4 * i + s, 1)], ACT.Sqrt,
                                         scale=1.0 / D, bias=g.eps[:, 0:1]).then_inc(norm_known, 1)
            act.wait_ge(gains_in, 5 * 16)

        @block.tensor
        def _(pe):
            pe.wait_ge(shaped, 4)
            for t in range(TT):
                pe.wait_ge(h_ready, t + 1)
                if t >= 2:
                    pe.wait_ge(ht_ready, t - 1)
                for k in range(KT):
                    last = nc.tensor.transpose(bank(g, 2 * (t % 2), 2)[:, k * P:(k + 1) * P],
                                               hs[:, t % 2, k * P:(k + 1) * P], g.ident[:, :])
                last.then_inc(turned, 1)

        @block.vector
        def _(dve):
            def normalise(t):
                dve.wait_ge(norm_known, t + 1)
                nc.vector.reciprocal(inv[:, t:t + 1], root[:, t:t + 1]).then_inc(inverted, 1)
                dve.wait_ge(inverted, t + 1)
                nc.vector.tensor_scalar(hs[:, t % 2, :], xs[:, t % 4, :], inv[:, t:t + 1], None, ALU.mult).then_inc(h_ready, 1)

            dve.wait_ge(gains_in, 5 * 16)
            normalise(0)
            for t in range(TT):
                if t + 1 < TT:
                    normalise(t + 1)
                dve.wait_ge(turned, t + 1)
                nc.vector.tensor_tensor(ht[:, :, t * P:(t + 1) * P], bank(g, 2 * (t % 2), 2).rearrange("p (k t) -> p k t", k=KT),
                                        g.gain_mix[:, :].unsqueeze(2).broadcast_to([P, KT, P]), ALU.mult).then_inc(ht_ready, 1)
            dve.wait_ge(ht_ready, TT)


def stage_latents(g, io):
    nc = g.nc
    w_ready = [g.sem(f"w_latent{m}") for m in range(4)]
    rows_in, values_in = g.sem("rows_in"), g.sem("values_in")
    projected, lat_out, lat_sq, lat_sum, lat_root, lat_done = (
        g.sem(n) for n in ("projected", "lat_out", "lat_sq", "lat_sum", "lat_root", "lat_done"))
    row_made, row_out, row_moved, row_flipped, bias_made, bias_masked = (
        g.sem(n) for n in ("row_made", "row_out", "row_moved", "row_flipped", "bias_made", "bias_masked"))
    value_made, value_out, angles, trig, steps = (
        g.sem(n) for n in ("value_made", "value_out", "angles", "trig", "latent_steps"))
    w_v = io.w_in.rearrange("(k p) n -> p k n", p=P)
    ht = tiled(g, HT, KT, SEQ)
    wst = at(g, W_ST, 4 * SEQ).rearrange("p (s k c) -> p s k c", s=4, k=KT)
    wdv = tiled(g, W_DV, KT, HALF)
    sq = tiled(g, SQ, 2, HALF)
    root = at(g, X_IN, 2 * SEQ)
    arg_sin, arg_cos = at(g, X_IN + 2048, SEQ), at(g, X_IN + 3072, SEQ)
    pos_i, posf, angle = at(g, KR, SEQ).bitcast(I32), at(g, COS, SEQ), at(g, SIN, SEQ)
    rows = g.rope
    bias_far = g.bias_far
    rel = at(g, QK + 3072, DIFF_HEADS)[0:BUCKETS]
    onehot = at(g, QK, 383)[0:BUCKETS]
    by_distance = at(g, QK + 512, 383)[0:DIFF_HEADS]
    shifted = tiled(g, QK + 1024, DIFF_HEADS, 256)
    lamv, lamp = at(g, QK + 2048, 256), at(g, QK + 2304, 128)
    wv = at(g, QK + 2560, HALF)
    bias_t = tiled(g, BIAS_T, DIFF_HEADS, 256)
    kr, rot = at(g, KR, SEQ)[NOPE:HEAD_QK], at(g, SQ, SEQ)[NOPE:HEAD_QK]
    toeplitz = nc.dram_tensor("bias_by_distance", (DIFF_HEADS, 384), F32).ap()

    with nc.Block() as block:

        @block.sync
        def _(sp):
            for m, col in enumerate((0, P, OFF_KV)):
                sp.dma_start(wst[:, m], w_v[:, :, col:col + P]).then_inc(w_ready[m], 16)
            half = ROPE // 2
            for to, col, n in ((0, OFF_KR, ROPE), (ROPE, OFF_KR + half, half), (ROPE + half, OFF_KR, half)):
                sp.dma_start(wst[:, 3, :, to:to + n], w_v[:, :, col:col + n]).then_inc(w_ready[3], 16)
            sp.dma_start(wdv, w_v[:, :, OFF_DV:OFF_DV + HALF]).then_inc(values_in, 16)
            sp.wait_ge(row_out, 1)
            sp.dma_start(toeplitz[:, 0:383], by_distance).then_inc(row_moved, 16)
            sp.wait_ge(row_moved, 16)
            for h in range(DIFF_HEADS):
                src = bass.AP(tensor=toeplitz.tensor, offset=h * 384, ap=[[1, P], [1, 256]])
                sp.dma_start(shifted[:, h, :], src).then_inc(row_moved, 16)
            sp.wait_ge(row_moved, 16 + 16 * DIFF_HEADS)
            sp.wait_ge(value_made, TT)
            load_pair(g, io, sp, 0)

        @block.gpsimd
        def _(pool):
            pool.wait_ge(bias_made, DIFF_HEADS)
            for h in range(DIFF_HEADS):
                pool.affine_select(out=bias_t[:, h, P:], in_=bias_t[:, h, P:], compare_op=ALU.is_ge, fill=NEG,
                                   base=0, pattern=[[-1, P]], channel_multiplier=1).then_inc(bias_masked, 1)
            pool.wait_ge(bias_masked, DIFF_HEADS)

        @block.scalar
        def _(act):
            for out, src in ((rel, io.rel_bias), (onehot, io.bucket_rows), (pos_i, io.positions.partition_broadcast(P)),
                             (rows[:, :], io.rope_rows), (bias_far[:, :], io.rel_bias[BUCKETS - 1:BUCKETS, :].partition_broadcast(P)),
                             (lamv, io.diff_lambda.rearrange("(o a) b -> o (a b)", o=1).partition_broadcast(P))):
                act.dma_start(out, src).then_inc(rows_in, 16)
            act.dma_start(wv.rearrange("p (h c) -> p h c", c=MLA_V),
                          io.w_kv_b.rearrange("p (h c) -> p h c", c=NOPE + MLA_V)[:, :, NOPE:]).then_inc(values_in, 16)
            for m in range(3):
                act.wait_ge(lat_out, m + 1)
                for h in range(2):
                    if m >= 1:
                        act.wait_ge(lat_sum, 2 * m + h - 1)
                    nc.scalar.activation(sq[:, h, :], bank(g, 4 + 2 * (m % 2) + h), ACT.Square).then_inc(lat_sq, 1)
            act.wait_ge(lat_sum, 6)
            nc.scalar.activation(root[:, 0:SEQ], bank(g, 0, 2), ACT.Sqrt, scale=1.0 / Q_RANK, bias=g.eps[:, 0:1]).then_inc(lat_root, 1)
            nc.scalar.activation(root[:, SEQ:], bank(g, 2, 2), ACT.Sqrt, scale=1.0 / KV_RANK, bias=g.eps[:, 0:1]).then_inc(lat_root, 1)
            act.wait_ge(angles, 1)
            nc.scalar.activation(at(g, SIN, SEQ), arg_sin, ACT.Sin, scale=rows[:, 1:2]).then_inc(trig, 1)
            nc.scalar.activation(at(g, COS, SEQ), arg_cos, ACT.Sin).then_inc(trig, 1)

        @block.tensor
        def _(pe):
            for m in range(3):
                pe.wait_ge(w_ready[m], 16)
                if m == 2:
                    pe.wait_ge(lat_sq, 2)
                for h in range(2):
                    for k in range(KT):
                        last = nc.tensor.matmul(bank(g, 4 + 2 * (m % 2) + h), wst[:, m, k, :], ht[:, k, h * HALF:(h + 1) * HALF],
                                                start=(k == 0), stop=(k == KT - 1))
                last.then_inc(projected, 1)
                if m == 0:
                    pe.wait_ge(rows_in, 6 * 16)
                    nc.tensor.matmul(bank(g, 2)[0:DIFF_HEADS, 0:383], rel, onehot, start=True, stop=True).then_inc(row_made, 1)
                if m == 2:
                    pe.wait_ge(row_out, 1)
                for h in range(2):
                    pe.wait_ge(lat_sq, 2 * m + h + 1)
                    nc.tensor.matmul(bank(g, (0 if m < 2 else 2) + h), g.ones[:, :], sq[:, h, :],
                                     start=(m != 1), stop=(m != 0)).then_inc(lat_sum, 1)
            pe.wait_ge(w_ready[3], 48)
            for swapped, b in ((0, 6), (1, 4)):
                for h in range(2):
                    for k in range(KT):
                        last = nc.tensor.matmul(bank(g, b + h)[NOPE:HEAD_QK, :], wst[:, 3, k, swapped * ROPE:(swapped + 1) * ROPE],
                                                ht[:, k, h * HALF:(h + 1) * HALF], start=(k == 0), stop=(k == KT - 1))
            last.then_inc(projected, 1)
            pe.wait_ge(values_in, 32)
            pe.wait_ge(lat_root, 2)
            for t in range(TT):
                if t >= 4:
                    pe.wait_ge(value_out, t - 3)
                for k in range(KT):
                    last = nc.tensor.matmul(bank(g, t % 4), ht[:, k, t * P:(t + 1) * P], wdv[:, k, :],
                                            start=(k == 0), stop=(k == KT - 1))
                last.then_inc(value_made, 1)
            pe.wait_ge(lat_done, 3)
            for t in range(TT):
                pe.wait_ge(value_out, t + 5)
                nc.tensor.matmul(bank(g, t % 4), at(g, CKV, SEQ)[:, t * P:(t + 1) * P], wv,
                                 start=True, stop=True).then_inc(value_made, 1)
            pe.wait_ge(row_moved, 16 + 16 * DIFF_HEADS)
            for h in range(DIFF_HEADS):
                nc.tensor.matmul(bank(g, 4 + h % 2)[:, (h // 2) * 256:(h // 2) * 256 + 256], g.flip[:, :], shifted[:, h, :],
                                 start=True, stop=True).then_inc(row_flipped, 1)

        @block.vector
        def _(dve):
            chain = Chain(dve, steps)
            dve.wait_ge(rows_in, 6 * 16)
            turn = 2 * np.pi
            part1 = 6.28125
            part2 = round((turn - part1) * 2 ** 21) / 2 ** 21
            part3 = turn - part1 - part2
            limit = 3.1415925
            chain.step(nc.vector.tensor_copy(posf, pos_i))
            steps_up, is_one = at(g, H_N, SEQ), at(g, H_N + SEQ, SEQ)
            chain.step(nc.vector.tensor_tensor(steps_up[:, 1:], posf[:, 1:], posf[:, 0:SEQ - 1], ALU.subtract))
            chain.step(nc.vector.tensor_scalar(is_one[:, 1:], steps_up[:, 1:], 1.0, None, ALU.is_equal))
            chain.step(nc.vector.reduce_sum(steps_up[:, 0:1], is_one[:, 1:], AX))
            chain.step(nc.vector.tensor_scalar(g.scattered_positions[:, :], steps_up[:, 0:1], SEQ - 1.5, None, ALU.is_lt))
            chain.step(nc.vector.tensor_scalar(angle, posf, rows[:, 0:1], None, ALU.mult))
            turns_i, turns = at(g, H_N, SEQ).bitcast(I32), at(g, H_N + 1024, SEQ)

            def argument(quarter, out):
                chain.step(nc.vector.tensor_scalar(turns_i, angle, 1.0 / turn, quarter, ALU.mult, ALU.add))
                chain.step(nc.vector.tensor_copy(turns, turns_i))
                src = angle
                for part in (part1, part2, part3):
                    chain.step(nc.vector.scalar_tensor_tensor(out=out, in0=turns, scalar=-float(part), in1=src, op0=ALU.mult, op1=ALU.add))
                    src = out
                chain.step(nc.vector.tensor_scalar(out, out, quarter * turn, limit, ALU.add, ALU.min))
                chain.step(nc.vector.tensor_scalar(out, out, -limit, None, ALU.max))

            dve.wait_ge(row_made, 1)
            nc.vector.tensor_copy(by_distance, bank(g, 2)[0:DIFF_HEADS, 0:383]).then_inc(row_out, 1)
            for m in range(3):
                dve.wait_ge(projected, m + 1)
                gain = g.gain_q[:, m:m + 1] if m < 2 else g.gain_kv[:, 0:1]
                nc.vector.tensor_scalar(at(g, QA + m * SEQ, SEQ), bank(g, 4 + 2 * (m % 2), 2), gain, None, ALU.mult).then_inc(lat_out, 1)
                if m == 0:
                    argument(0.0, arg_sin)
                if m == 1:
                    argument(0.25, arg_cos)
                    dve.sem_inc(angles, 1)
            for j in range(2):
                chain.step(nc.vector.tensor_tensor(lamp[:, j * 64:(j + 1) * 64], lamv[:, 128 * j:128 * j + 64],
                                                   lamv[:, 128 * j + 64:128 * j + 128], ALU.mult))
                chain.step(nc.vector.reduce_sum(g.lam[:, j:j + 1], lamp[:, j * 64:(j + 1) * 64], AX))
            dve.wait_ge(lat_root, 2)
            chain.step(nc.vector.reciprocal(root, root))
            dve.wait_ge(lat_out, 3)
            for m in range(3):
                r = root[:, 0:SEQ] if m < 2 else root[:, SEQ:]
                nc.vector.tensor_tensor(at(g, QA + m * SEQ, SEQ), at(g, QA + m * SEQ, SEQ), r, ALU.mult).then_inc(lat_done, 1)
            dve.wait_ge(trig, 2)
            dve.wait_ge(projected, 4)
            chain.step(nc.vector.tensor_tensor(kr, bank(g, 6, 2)[NOPE:HEAD_QK], at(g, COS, SEQ)[NOPE:HEAD_QK], ALU.mult))
            chain.step(nc.vector.tensor_tensor(rot, bank(g, 4, 2)[NOPE:HEAD_QK], at(g, SIN, SEQ)[NOPE:HEAD_QK], ALU.mult))
            chain.step(nc.vector.tensor_tensor(kr, kr, rot, ALU.add))
            chain.step(nc.vector.tensor_scalar(kr, kr, MLA_SCALE, None, ALU.mult))
            for t in range(2 * TT):
                dve.wait_ge(value_made, t + 1)
                out = at(g, (V_DIFF if t < TT else V_MLA) + (t % TT) * HALF, HALF)
                nc.vector.tensor_copy(out, bank(g, t % 4)).then_inc(value_out, 1)
            dve.wait_ge(row_flipped, DIFF_HEADS)
            for h in range(DIFF_HEADS):
                nc.vector.tensor_scalar(bias_t[:, h, :], bank(g, 4 + h % 2)[:, (h // 2) * 256:(h // 2) * 256 + 256],
                                        bias_far[:, h:h + 1], None, ALU.subtract).then_inc(bias_made, 1)


def key_range(general):
    def end(i):
        return TT - 1 if general else i

    def late_before(u):
        return sum(end(w % TT) >= 4 for w in range(u))

    return end, late_before


def either(g, eng, work):
    flag = eng.value_load(g.scattered_positions[0:1, 0:1], min_val=0, max_val=1)
    with eng.If(flag > 0):
        work(True)
    with eng.Else():
        work(False)


def thresholds():
    bucket = rel_buckets().argmax(0)[::-1]
    return [int(np.argmax(bucket >= b)) - 127 for b in range(1, BUCKETS)]


GENERAL_IN = 3 * 16
GENERAL_OUT = 16 * (1 + DIFF_HEADS)
MLA_MASKS_IN = GENERAL_IN + TT * GENERAL_OUT
DIFF_BIASES_IN = MLA_MASKS_IN + 16 * TT * MLA_HEADS
GENERAL_STEPS = 2 + DIFF_HEADS * (1 + 2 * (BUCKETS - 1))


def general_views(g):
    v = Core(g.nc)
    v.kpos, v.dist, v.acc, v.tmp = (at(g, GENERAL + n * SEQ, SEQ) for n in range(4))
    v.mask = at(g, GENERAL + 4 * SEQ, SEQ)
    small = GENERAL + 5 * SEQ
    v.qpos_i, v.qpos, v.rel, v.delta = at(g, small, TT).bitcast(I32), at(g, small + TT, TT), at(g, small + 128, 128), at(g, small + 256, 128)
    return v


def move_pair_biases(g, io, pool):
    v = general_views(g)
    pool.dma_start(v.tmp.bitcast(I32), io.positions.partition_broadcast(P)).then_inc(g.general_dma, 16)
    pool.dma_start(v.qpos_i, io.positions.rearrange("o (t p) -> p (o t)", p=P)).then_inc(g.general_dma, 16)
    pool.dma_start(v.rel, io.rel_bias.rearrange("(o b) h -> o (b h)", o=1).partition_broadcast(P)).then_inc(g.general_dma, 16)
    pool.wait_ge(g.general_dma, GENERAL_IN)
    with pool.Fori(0, TT) as i:
        for n in range(1 + DIFF_HEADS):
            pool.wait_ge(g.general_steps, GENERAL_STEPS * i + (3 + 2 + n * (1 + 2 * (BUCKETS - 1))))
            pool.sem_inc(g.carried, 1)
            pool.dma_start(io.pair_bias[n, bass.ds(i * P, P), :], v.acc if n else v.mask).then_inc(g.general_dma, 16)
            pool.wait_ge(g.general_dma, GENERAL_OUT * i + (GENERAL_IN + 16 * (n + 1)))
            pool.sem_inc(g.carried, 1)


def make_pair_biases(g, dve):
    nc, v = g.nc, general_views(g)
    dve.wait_ge(g.general_dma, GENERAL_IN)
    first = Chain(dve, g.general_steps)
    first.step(nc.vector.tensor_copy(v.kpos, v.tmp.bitcast(I32)))
    first.step(nc.vector.tensor_copy(v.qpos, v.qpos_i))
    n = (BUCKETS - 1) * DIFF_HEADS
    first.step(nc.vector.tensor_tensor(v.delta[:, 0:n], v.rel[:, DIFF_HEADS:], v.rel[:, 0:n], ALU.subtract))
    with dve.Fori(0, TT) as i:
        chain = Chain(dve, g.general_steps, GENERAL_STEPS * i + first.n)
        chain.step(nc.vector.tensor_scalar(v.dist, v.kpos, v.qpos[:, bass.ds(i, 1)], -1.0, ALU.subtract, ALU.mult))
        chain.step(nc.vector.tensor_scalar(v.mask, v.dist, 0.0, NEG, ALU.is_lt, ALU.mult))
        dve.wait_ge(g.general_dma, GENERAL_OUT * i + (GENERAL_IN + 16))
        for h in range(DIFF_HEADS):
            chain.step(nc.vector.tensor_scalar(v.acc, v.mask, v.rel[:, h:h + 1], None, ALU.add))
            for b, least in enumerate(thresholds()):
                col = b * DIFF_HEADS + h
                chain.step(nc.vector.tensor_scalar(v.tmp, v.dist, float(least), v.delta[:, col:col + 1], ALU.is_ge, ALU.mult))
                chain.step(nc.vector.tensor_tensor(v.acc, v.acc, v.tmp, ALU.add))
            dve.wait_ge(g.general_dma, GENERAL_OUT * i + (GENERAL_IN + 16 * (h + 2)))


PAIR_DMAS = 9


def load_pair(g, io, sp, hp):
    wq, wk = tiled(g, W_PAIR, 2, 256), at(g, W_PAIR + 512, P)
    wq_v = io.w_q_b.rearrange("(k p) (h c) -> p k h c", p=P, c=HEAD_QK)
    wk_v = io.w_kv_b.rearrange("p (h c) -> p h c", c=NOPE + MLA_V)
    half = ROPE // 2
    for k in range(2):
        for to, step, col, n in ((0, NOPE, 0, NOPE), (2 * NOPE, ROPE, NOPE, ROPE),
                                 (2 * NOPE + 2 * ROPE, ROPE, NOPE + half, half),
                                 (2 * NOPE + 2 * ROPE + half, ROPE, NOPE, half)):
            dst = wq[:, k, (to // step) * step:(to // step + 2) * step].rearrange("p (j c) -> p j c", j=2)
            sp.dma_start(dst[:, :, to % step:to % step + n],
                         wq_v[:, k, bass.ds(2 * hp, 2), col:col + n]).then_inc(g.w_pair, 16)
    sp.dma_start(wk.rearrange("p (j c) -> p j c", j=2),
                 wk_v[:, bass.ds(2 * hp, 2), 0:NOPE]).then_inc(g.w_pair, 16)


def stage_mla(g, io):
    nc = g.nc
    w_pair = g.w_pair
    projected, qk_copied, q_rotated, rot_steps = (
        g.sem(n) for n in ("pair_projected", "qk_copied", "q_rotated", "rot_steps"))
    scored, masked, max_known, exped, turned0, turned1, pt_act, pt_dve, applied, inverted, y_out = (
        g.sem("mla_" + n) for n in ("scored", "masked", "max_known", "exped", "turned0", "turned1", "pt_act", "pt_dve",
                                    "applied", "inverted", "y_out"))
    UNITS = 2 * TT
    mask = tiled(g, MASK_TILE, 2, SEQ)
    qa, ckv = tiled(g, QA, 2, SEQ), at(g, CKV, SEQ)
    wq = tiled(g, W_PAIR, 2, 256)
    wk = at(g, W_PAIR + 512, P)
    q_t = [at(g, QK + (2 * j) * SEQ, SEQ) for j in range(2)]
    k_t = [at(g, QK + (2 * j + 1) * SEQ, SEQ) for j in range(2)]
    prob, prob_t, rot = tiled(g, PROB, 2, SEQ), tiled(g, PROB_T, 2, SEQ), tiled(g, ROT, 2, SEQ)
    v, y = tiled(g, V_MLA, TT, HALF), tiled(g, Y_MLA, TT, HALF)
    neg_max, total, inv = g.den[:, 0:16], g.den[:, 16:32], g.den[:, 32:48]

    with nc.Block() as block:

        @block.sync
        def _(sp):
            with sp.Fori(1, MLA_HEADS // 2) as hp:
                sp.wait_ge(projected, 3 * hp)
                load_pair(g, io, sp, hp)

        @block.gpsimd
        def _(pool):
            def bring_masks(general):
                if not general:
                    pool.nop()
                    return
                move_pair_biases(g, io, pool)
                with pool.Fori(0, MLA_HEADS // 2) as hp:
                    for u in range(UNITS):
                        pool.wait_ge(scored, UNITS * hp + (u + 1))
                        pool.sem_inc(g.carried, 1)
                        pool.dma_start(mask[:, u % 2, :], io.pair_bias[0, (u % TT) * P:(u % TT + 1) * P, :]).then_inc(g.general_dma, 16)
                        pool.wait_ge(g.general_dma, MLA_MASKS_IN + 16 * (UNITS * hp + (u + 1)))
                        pool.sem_inc(g.carried, 1)

            either(g, pool, bring_masks)

        @block.tensor
        def _(pe):
            def attend(general):
                end, late_before = key_range(general)
                with pe.Fori(0, MLA_HEADS // 2) as hp:
                    base = UNITS * hp
                    pe.wait_ge(w_pair, 16 * PAIR_DMAS * hp + 16 * PAIR_DMAS)
                    for b, lhs in ((2, lambda k: wq[:, k, P:2 * P]), (0, lambda k: wq[:, k, 0:P])):
                        for h in range(2):
                            for k in range(2):
                                last = nc.tensor.matmul(bank(g, b + h), lhs(k), qa[:, k, h * HALF:(h + 1) * HALF],
                                                        start=(k == 0), stop=(k == 1))
                        last.then_inc(projected, 1)
                    for h in range(2):
                        last = nc.tensor.matmul(bank(g, 4 + h), wk, ckv[:, h * HALF:(h + 1) * HALF], start=True, stop=True)
                    last.then_inc(projected, 1)
                    pe.wait_ge(qk_copied, 4 * hp + 4)
                    pe.wait_ge(q_rotated, 2 * hp + 3)

                    def score(u):
                        j, i = divmod(u, TT)
                        if u >= 2:
                            pe.wait_ge(exped, base + u - 1)
                        keys = (end(i) + 1) * P
                        for c in range(0, keys, HALF):
                            n = min(HALF, keys - c)
                            last = nc.tensor.matmul(bank(g, 2 * (u % 2) + c // HALF)[:, 0:n], q_t[j][0:HEAD_QK, i * P:(i + 1) * P],
                                                    k_t[j][0:HEAD_QK, c:c + n], start=True, stop=True)
                        last.then_inc(scored, 1)

                    def turn(u):
                        j, i = divmod(u, TT)
                        pe.wait_ge(exped, base + u + 1)
                        for grp in range(1 + end(i) // 4):
                            if grp == 0 and u >= 1:
                                pe.wait_ge(pt_act, base + u)
                            if grp == 1 and late_before(u):
                                pe.wait_ge(pt_dve, late_before(UNITS) * hp + late_before(u))
                            for kt in range(4 * grp, min(4 * grp + 4, end(i) + 1)):
                                last = nc.tensor.transpose(bank(g, 4 + grp)[:, (kt % 4) * P:(kt % 4 + 1) * P],
                                                           prob[:, u % 2, kt * P:(kt + 1) * P], g.ident[:, :])
                            last.then_inc((turned0, turned1)[grp], 1)

                    def apply(u):
                        j, i = divmod(u, TT)
                        pe.wait_ge(pt_act, base + u + 1)
                        if end(i) >= 4:
                            pe.wait_ge(pt_dve, late_before(UNITS) * hp + (late_before(u) + 1))
                        pe.wait_ge(y_out, base + u + 1)
                        for kt in range(end(i) + 1):
                            last = nc.tensor.matmul(bank(g, 6 + u % 2)[:, 0:MLA_V], prob_t[:, u % 2, kt * P:(kt + 1) * P],
                                                    v[:, kt, bass.ds((2 * hp + j) * MLA_V, MLA_V)], start=(kt == 0), stop=(kt == end(i)))
                        last.then_inc(applied, 1)

                    score(0)
                    for u in range(UNITS):
                        if u + 1 < UNITS:
                            score(u + 1)
                        if u == UNITS - 1:
                            apply(u - 1)
                        turn(u)
                        if 1 <= u < UNITS - 1:
                            apply(u - 1)
                    apply(UNITS - 1)

            either(g, pe, attend)

        @block.vector
        def _(dve):
            nc.vector.tensor_copy(k_t[0][NOPE:HEAD_QK, :], at(g, KR, SEQ)[NOPE:HEAD_QK]).then_inc(q_rotated, 1)
            nc.vector.tensor_copy(k_t[1][NOPE:HEAD_QK, :], at(g, KR, SEQ)[NOPE:HEAD_QK]).then_inc(y_out, 2)
            def attend(general):
                end, late_before = key_range(general)
                if general:
                    make_pair_biases(g, dve)
                with dve.Fori(0, MLA_HEADS // 2) as hp:
                    base = UNITS * hp
                    dve.wait_ge(projected, 3 * hp + 1)
                    nc.vector.tensor_tensor(rot[0:NOPE, 0, :], bank(g, 2, 2)[0:NOPE], at(g, COS, SEQ)[0:NOPE], ALU.mult).then_inc(rot_steps, 1)
                    nc.vector.tensor_tensor(rot[0:NOPE, 1, :], bank(g, 2, 2)[NOPE:P], at(g, SIN, SEQ)[NOPE:P], ALU.mult).then_inc(rot_steps, 1)
                    dve.wait_ge(rot_steps, 2 * hp + 2)
                    for j in range(2):
                        nc.vector.tensor_tensor(q_t[j][NOPE:HEAD_QK, :], rot[j * ROPE:(j + 1) * ROPE, 0, :],
                                                rot[j * ROPE:(j + 1) * ROPE, 1, :], ALU.add).then_inc(q_rotated, 1)

                    def row_max(u):
                        i = u % TT
                        dve.wait_ge(scored, base + u + 1)
                        s = bank(g, 2 * (u % 2), 2)
                        if general:
                            dve.wait_ge(g.general_dma, MLA_MASKS_IN + 16 * (base + u + 1))
                            nc.vector.tensor_tensor(s, s, mask[:, u % 2, :], ALU.add).then_inc(masked, 1)
                        else:
                            nc.vector.tensor_tensor(s[:, i * P:(i + 1) * P], s[:, i * P:(i + 1) * P], g.causal[:, :], ALU.add).then_inc(masked, 1)
                        dve.wait_ge(masked, base + u + 1)
                        nc.vector.reduce_max(neg_max[:, u:u + 1], s[:, 0:(end(i) + 1) * P], AX, negate=True).then_inc(max_known, 1)

                    def copy_late(u):
                        j, i = divmod(u, TT)
                        if end(i) < 4:
                            return
                        dve.wait_ge(turned1, late_before(UNITS) * hp + (late_before(u) + 1))
                        nc.vector.tensor_copy(prob_t[:, u % 2, HALF:(end(i) + 1) * P], bank(g, 5)[:, 0:(end(i) - 3) * P]).then_inc(pt_dve, 1)

                    def store_y(u):
                        j, i = divmod(u, TT)
                        dve.wait_ge(applied, base + u + 1)
                        nc.vector.reciprocal(inv[:, u:u + 1], total[:, u:u + 1]).then_inc(inverted, 1)
                        dve.wait_ge(inverted, base + u + 1)
                        nc.vector.tensor_scalar(y[:, i, bass.ds((2 * hp + j) * MLA_V, MLA_V)], bank(g, 6 + u % 2)[:, 0:MLA_V],
                                                inv[:, u:u + 1], None, ALU.mult).then_inc(y_out, 1)

                    row_max(0)
                    for u in range(UNITS):
                        if u + 1 < UNITS:
                            row_max(u + 1)
                        copy_late(u)
                        if u >= 1:
                            store_y(u - 1)
                    store_y(UNITS - 1)

            either(g, dve, attend)
            dve.wait_ge(y_out, UNITS * MLA_HEADS // 2 + 2)

        @block.scalar
        def _(act):
            def attend(general):
                end, late_before = key_range(general)
                with act.Fori(0, MLA_HEADS // 2) as hp:
                    base = UNITS * hp
                    act.wait_ge(projected, 3 * hp + 2)
                    for j in range(2):
                        nc.scalar.activation(q_t[j][0:NOPE, :], bank(g, 0, 2)[j * NOPE:(j + 1) * NOPE], ACT.Copy).then_inc(qk_copied, 1)
                    act.wait_ge(projected, 3 * hp + 3)
                    for j in range(2):
                        nc.scalar.activation(k_t[j][0:NOPE, :], bank(g, 4, 2)[j * NOPE:(j + 1) * NOPE], ACT.Copy,
                                             scale=MLA_SCALE).then_inc(qk_copied, 1)

                    def exp(u):
                        keys = (end(u % TT) + 1) * P
                        act.wait_ge(max_known, base + u + 1)
                        nc.scalar.activation(prob[:, u % 2, 0:keys], bank(g, 2 * (u % 2), 2)[:, 0:keys], ACT.Exp,
                                             bias=neg_max[:, u:u + 1], accum_out=total[:, u:u + 1]).then_inc(exped, 1)

                    def copy_early(u):
                        keys = min(HALF, (end(u % TT) + 1) * P)
                        act.wait_ge(turned0, base + u + 1)
                        nc.scalar.activation(prob_t[:, u % 2, 0:keys], bank(g, 4)[:, 0:keys], ACT.Copy).then_inc(pt_act, 1)

                    exp(0)
                    for u in range(UNITS):
                        if u + 1 < UNITS:
                            exp(u + 1)
                        copy_early(u)

            either(g, act, attend)


def stage_diff(g, io):
    nc = g.nc
    w_q, w_k, projected, q_copied, k_copied, lam_steps = (
        g.sem("diff_" + n) for n in ("w_q", "w_k", "projected", "q_copied", "k_copied", "lam_steps"))
    scored, biased, max_known, exped, weighed, combined, turned0, turned1, pt_act, pt_dve, applied, y_out = (
        g.sem("diff_" + n) for n in ("scored", "biased", "max_known", "exped", "weighed", "combined", "turned0", "turned1",
                                     "pt_act", "pt_dve", "applied", "y_out"))
    summed = g.sem("diff_summed")
    HALVES = 2 * TT
    pair_bias = tiled(g, MASK_TILE, 2, SEQ)
    ht = tiled(g, HT, KT, SEQ)
    wst = at(g, W_ST, 2 * SEQ).rearrange("p (s k c) -> p s k c", s=2, k=KT)
    q_t, k_t = at(g, QK, SEQ), at(g, QK + SEQ, SEQ)
    prob, prob_t = tiled(g, PROB, 4, SEQ), tiled(g, PROB_T, 2, SEQ)
    v, y = tiled(g, V_DIFF, TT, HALF), tiled(g, Y_DIFF, TT, HALF)
    bias_t = tiled(g, BIAS_T, DIFF_HEADS, 256)
    neg_max, total, inv, share = g.den[:, 0:16], g.den[:, 16:32], g.den[:, 32:48], g.den[:, 48:56]
    w_v = io.w_in.rearrange("(k p) n -> p k n", p=P)

    with nc.Block() as block:

        @block.sync
        def _(sp):
            def load_head(h):
                sp.dma_start(wst[:, 0], w_v[:, :, bass.ds(OFF_DQ + P * h, P)]).then_inc(w_q, 16)
                sp.dma_start(wst[:, 1], w_v[:, :, bass.ds(OFF_DK + P * h, P)]).then_inc(w_k, 16)
            load_head(0)
            with sp.Fori(1, DIFF_HEADS) as h:
                sp.wait_ge(projected, 2 * h)
                load_head(h)

        @block.gpsimd
        def _(pool):
            def bring_biases(general):
                if not general:
                    pool.nop()
                    return
                with pool.Fori(0, DIFF_HEADS) as h:
                    for i in range(TT):
                        pool.wait_ge(scored, HALVES * h + (2 * i + 1))
                        pool.sem_inc(g.carried, 1)
                        pool.dma_start(pair_bias[:, i % 2, :].unsqueeze(1), io.pair_bias.rearrange("h (i p) k -> p h i k", p=P)[:, bass.ds(h + 1, 1), i, :]).then_inc(g.general_dma, 16)
                        pool.wait_ge(g.general_dma, DIFF_BIASES_IN + 16 * (TT * h + (i + 1)))
                        pool.sem_inc(g.carried, 1)

            either(g, pool, bring_biases)

        @block.tensor
        def _(pe):
            def attend(general):
                end, late_before = key_range(general)
                with pe.Fori(0, DIFF_HEADS) as h:
                    base, ub = HALVES * h, TT * h
                    for s, w in ((0, w_q), (1, w_k)):
                        pe.wait_ge(w, 16 * h + 16)
                        for c in range(2):
                            for k in range(KT):
                                last = nc.tensor.matmul(bank(g, 2 * s + c), wst[:, s, k, :], ht[:, k, c * HALF:(c + 1) * HALF],
                                                        start=(k == 0), stop=(k == KT - 1))
                        last.then_inc(projected, 1)
                    pe.wait_ge(q_copied, h + 1)
                    pe.wait_ge(k_copied, h + 1)

                    def score(i):
                        keys = (end(i) + 1) * P
                        for c in range(2):
                            s = 2 * i + c
                            if s >= 2:
                                pe.wait_ge(exped, base + s - 1)
                            rows = slice(c * DIFF_DIM, (c + 1) * DIFF_DIM)
                            for a in range(0, keys, HALF):
                                n = min(HALF, keys - a)
                                last = nc.tensor.matmul(bank(g, 2 * c + a // HALF)[:, 0:n], q_t[rows, i * P:(i + 1) * P],
                                                        k_t[rows, a:a + n], start=True, stop=True)
                            last.then_inc(scored, 1)

                    def turn(i):
                        pe.wait_ge(combined, ub + i + 1)
                        for grp in range(1 + end(i) // 4):
                            if grp == 0 and i >= 1:
                                pe.wait_ge(pt_act, ub + i)
                            if grp == 1 and late_before(i):
                                pe.wait_ge(pt_dve, late_before(TT) * h + late_before(i))
                            for kt in range(4 * grp, min(4 * grp + 4, end(i) + 1)):
                                last = nc.tensor.transpose(bank(g, 4 + grp)[:, (kt % 4) * P:(kt % 4 + 1) * P],
                                                           prob[:, 2 * (i % 2), kt * P:(kt + 1) * P], g.ident[:, :])
                            last.then_inc((turned0, turned1)[grp], 1)

                    def apply(i):
                        pe.wait_ge(pt_act, ub + i + 1)
                        if end(i) >= 4:
                            pe.wait_ge(pt_dve, late_before(TT) * h + (late_before(i) + 1))
                        pe.wait_ge(y_out, ub + i + 1)
                        for kt in range(end(i) + 1):
                            last = nc.tensor.matmul(bank(g, 6 + i % 2)[:, 0:DIFF_V], prob_t[:, i % 2, kt * P:(kt + 1) * P],
                                                    v[:, kt, bass.ds(h * DIFF_V, DIFF_V)], start=(kt == 0), stop=(kt == end(i)))
                        last.then_inc(applied, 1)

                    score(0)
                    for i in range(TT):
                        if i + 1 < TT:
                            score(i + 1)
                        if i == TT - 1:
                            apply(i - 1)
                        turn(i)
                        if 1 <= i < TT - 1:
                            apply(i - 1)
                    apply(TT - 1)

            either(g, pe, attend)

        @block.vector
        def _(dve):
            dve.wait_ge(lam_steps, 1)
            nc.vector.tensor_tensor(g.lam[:, 4:5], g.lam[:, 3:4], g.lam[:, 2:3], ALU.subtract).then_inc(lam_steps, 1)
            dve.wait_ge(lam_steps, 2)
            nc.vector.tensor_scalar(g.lam[:, 5:6], g.lam[:, 4:5], -LAMBDA_INIT, None, ALU.add).then_inc(lam_steps, 1)
            dve.wait_ge(lam_steps, 3)
            nc.vector.tensor_copy(g.lam[:, 6:7], g.lam[:, 5:6]).then_inc(y_out, 2)
            def attend(general):
                end, late_before = key_range(general)
                with dve.Fori(0, DIFF_HEADS) as h:
                    base, ub = HALVES * h, TT * h
                    dve.wait_ge(projected, 2 * h + 2)
                    nc.vector.tensor_copy(k_t, bank(g, 2, 2)).then_inc(k_copied, 1)

                    def row_max(i):
                        keys, near = (end(i) + 1) * P, 0 if general else max(0, i - 1) * P
                        for c in range(2):
                            s = 2 * i + c
                            dve.wait_ge(scored, base + s + 1)
                            sc = bank(g, 2 * c, 2)
                            if general:
                                dve.wait_ge(g.general_dma, DIFF_BIASES_IN + 16 * (ub + i + 1))
                                nc.vector.tensor_tensor(sc, sc, pair_bias[:, i % 2, :], ALU.add).then_inc(biased, 1)
                            else:
                                nc.vector.tensor_tensor(sc[:, near:keys], sc[:, near:keys],
                                                        bias_t[:, bass.ds(h, 1), 2 * P - (keys - near):2 * P], ALU.add).then_inc(biased, 1)
                            dve.wait_ge(biased, base + s + 1)
                            nc.vector.reduce_max(neg_max[:, s:s + 1], sc[:, 0:keys], AX, negate=True).then_inc(max_known, 1)

                    def combine(i):
                        dve.wait_ge(exped, base + 2 * i + 2)
                        nc.vector.reciprocal(inv[:, 2 * i:2 * i + 2], total[:, 2 * i:2 * i + 2]).then_inc(weighed, 1)
                        dve.wait_ge(weighed, 2 * (ub + i) + 1)
                        nc.vector.scalar_tensor_tensor(out=share[:, i:i + 1], in0=total[:, 2 * i:2 * i + 1], scalar=g.lam[:, 5:6],
                                                       in1=inv[:, 2 * i + 1:2 * i + 2], op0=ALU.mult, op1=ALU.mult).then_inc(weighed, 1)
                        dve.wait_ge(weighed, 2 * (ub + i) + 2)
                        keys, s = (end(i) + 1) * P, 2 * (i % 2)
                        nc.vector.scalar_tensor_tensor(out=prob[:, s, 0:keys], in0=prob[:, s + 1, 0:keys], scalar=share[:, i:i + 1],
                                                       in1=prob[:, s, 0:keys], op0=ALU.mult, op1=ALU.add).then_inc(combined, 1)

                    def copy_late(i):
                        if end(i) < 4:
                            return
                        dve.wait_ge(turned1, late_before(TT) * h + (late_before(i) + 1))
                        nc.vector.tensor_copy(prob_t[:, i % 2, HALF:(end(i) + 1) * P], bank(g, 5)[:, 0:(end(i) - 3) * P]).then_inc(pt_dve, 1)

                    def store_y(i):
                        dve.wait_ge(applied, ub + i + 1)
                        nc.vector.tensor_scalar(y[:, i, bass.ds(h * DIFF_V, DIFF_V)], bank(g, 6 + i % 2)[:, 0:DIFF_V],
                                                inv[:, 2 * i:2 * i + 1], None, ALU.mult).then_inc(y_out, 1)

                    row_max(0)
                    combine(0)
                    for i in range(TT):
                        if i + 1 < TT:
                            row_max(i + 1)
                        copy_late(i)
                        if i + 1 < TT:
                            combine(i + 1)
                        if i >= 1:
                            store_y(i - 1)
                    store_y(TT - 1)

            either(g, dve, attend)
            dve.wait_ge(y_out, TT * DIFF_HEADS + 2)

        @block.scalar
        def _(act):
            nc.scalar.activation(g.lam[:, 2:4], g.lam[:, 0:2], ACT.Exp).then_inc(lam_steps, 1)
            def attend(general):
                end, late_before = key_range(general)
                with act.Fori(0, DIFF_HEADS) as h:
                    base, ub = HALVES * h, TT * h
                    act.wait_ge(projected, 2 * h + 1)
                    nc.scalar.activation(q_t, bank(g, 0, 2), ACT.Copy, scale=DIFF_SCALE).then_inc(q_copied, 1)

                    def exp(i):
                        keys = (end(i) + 1) * P
                        for c in range(2):
                            s = 2 * i + c
                            act.wait_ge(max_known, base + s + 1)
                            nc.scalar.activation(prob[:, s % 4, 0:keys], bank(g, 2 * c, 2)[:, 0:keys], ACT.Exp,
                                                 bias=neg_max[:, s:s + 1], accum_out=total[:, s:s + 1]).then_inc(exped, 1)

                    def square(i):
                        act.wait_ge(y_out, ub + i + 3)
                        nc.scalar.activation(at(g, QA, P), y[:, i, bass.ds(h * DIFF_V, DIFF_V)], ACT.Square,
                                             accum_out=g.ssq[:, bass.ds(h + 4 * i, 1)]).then_inc(summed, 1)
                        act.wait_ge(summed, ub + i + 1)

                    def copy_early(i):
                        keys = min(HALF, (end(i) + 1) * P)
                        act.wait_ge(turned0, ub + i + 1)
                        nc.scalar.activation(prob_t[:, i % 2, 0:keys], bank(g, 4)[:, 0:keys], ACT.Copy).then_inc(pt_act, 1)

                    exp(0)
                    for i in range(TT):
                        if i + 1 < TT:
                            exp(i + 1)
                        copy_early(i)
                        if i >= 2:
                            square(i - 2)
                    square(TT - 2)
                    square(TT - 1)

            either(g, act, attend)


OUT_FIRST = 3


def out_weights(io):
    return io.w_out.rearrange("(k p) n -> p k n", p=P)


def stage_merge(g, io):
    nc = g.nc
    sub_steps = g.sem("sub_steps")
    GAIN, ROOTED, INVERTED, NORMED, ALL_NORMED = 1, 2, 3, 4, 5
    turned, copied_a, copied_d = g.sem("y_turned"), g.sem("y_copied_act"), g.sem("y_copied_dve")
    w_tile = [g.sem(f"w_merge{s}") for s in range(2)]
    h_hi_ready, h_lo_ready, w_hi_ready, w_lo_ready = (g.sem("merge_" + n) for n in ("h_hi", "h_lo", "w_hi", "w_lo"))
    made, gated, scaled, merged = (g.sem("merge_" + n) for n in ("made", "gated", "scaled", "merged"))
    ht, yt = tiled(g, HT, KT, SEQ), tiled(g, Y_T, KT, SEQ)
    y_m, y_d = tiled(g, Y_MLA, TT, HALF), tiled(g, Y_DIFF, TT, HALF)
    h_hi, h_lo = (part[:, :].rearrange("p (k t) -> p k t", k=KT) for part in g.parts[0:2])
    w_parts = g.parts[2][:, :].rearrange("p (s c b k n) -> p s c b k n", s=2, c=2, b=2, k=KT)
    out = tiled(g, MERGED, KT, SEQ)
    gate = tiled(g, GATE_T, 4, HALF)
    w = [[tiled(g, W_MERGE + 3072 * s + o, n, P) for o, n in ((0, KT), (1024, KT), (2048, 4), (2560, 4))] for s in range(2)]
    w_in = io.w_in.rearrange("(k p) n -> p k n", p=P)
    w_um, w_ud = (a.rearrange("(k p) n -> p k n", p=P) for a in (io.w_up_mla, io.w_up_diff))

    with nc.Block() as block:

        @block.sync
        def _(sp):
            def load(f, s):
                for dst, src, col in zip(w[s], (w_in, w_in, w_um, w_ud), (OFF_GATE, OFF_GATE + D, 0, 0)):
                    sp.dma_start(dst, src[:, :, bass.ds(f * P + col, P)]).then_inc(w_tile[s], 16)
            load(0, 0)
            load(1, 1)
            with sp.Fori(1, KT // 2) as i:
                for s in range(2):
                    sp.wait_ge(made, 4 * i + 2 * s)
                    load(2 * i + s, s)
            sp.wait_ge(made, 2 * KT)
            sp.dma_start(at(g, W_OUT, OUT_FIRST * D).rearrange("p (k n) -> p k n", n=D), out_weights(io)[:, 0:OUT_FIRST, :]).then_inc(g.w_out_in[0], 16)

        @block.tensor
        def _(pe):
            for n in range(16):
                a, h = divmod(n, 2)
                src = y_m if a < 4 else y_d
                if n in (8, 9):
                    pe.wait_ge(sub_steps, (NORMED, ALL_NORMED)[h])
                if n >= 8:
                    pe.wait_ge(copied_a if n % 2 == 0 else copied_d, (n - 8) // 2 + 1)
                for t in range(4):
                    last = nc.tensor.transpose(bank(g, n % 8)[:, t * P:(t + 1) * P], src[:, 4 * h + t, (a % 4) * P:(a % 4 + 1) * P], g.ident[:, :])
                last.then_inc(turned, 1)
            pe.wait_ge(copied_a, 8)
            pe.wait_ge(copied_d, 8)
            pe.sem_inc(made, 2)
            with pe.Fori(0, KT // 2) as i:
                for s in range(2):
                    pe.wait_ge(w_tile[s], 64 * i + 64)
                    for h in range(2):
                        n = 4 * i + 2 * s + h
                        pe.wait_ge(merged, n + 1)
                        cols = slice(h * HALF, (h + 1) * HALF)
                        for b, k0 in ((2, 0), (3, 4)):
                            for k in range(4):
                                nc.tensor.matmul(bank(g, 4 * h + b), w[s][b][:, k, :], yt[:, k0 + k, cols], start=(k == 0), stop=(k == 3))
                        if h == 0:
                            pe.wait_ge(h_lo_ready, KT)
                            pe.wait_ge(w_hi_ready, 2 * i + s + 1)
                            pe.wait_ge(w_lo_ready, 2 * i + s + 1)
                        for b in range(2):
                            for k in range(KT):
                                for c, part in ((0, h_hi), (0, h_lo), (1, h_hi)):
                                    last = nc.tensor.matmul(bank(g, 4 * h + b), w_parts[:, s, c, b, k, :], part[:, k, cols],
                                                            start=(k == 0 and c == 0 and part is h_hi), stop=(k == KT - 1 and c == 1))
                        last.then_inc(made, 1)

        @block.scalar
        def _(act):
            act.wait_ge(sub_steps, GAIN)
            nc.scalar.activation(g.ssq[:, :], g.ssq[:, :], ACT.Sqrt, scale=1.0 / DIFF_V, bias=g.eps[:, 0:1]).then_inc(sub_steps, 1)
            for n in range(0, 16, 2):
                act.wait_ge(turned, n + 1)
                if n < 8:
                    last = nc.scalar.activation(yt[:, n // 2, 0:HALF], bank(g, n % 8), ACT.Copy)
                else:
                    last = nc.scalar.activation(yt[:, n // 2, 0:HALF], bank(g, n % 8), ACT.Copy, scale=g.gain_sub[:, 1:2])
                last.then_inc(copied_a, 1)
            for k in range(KT):
                nc.scalar.activation(h_hi[:, k, :], ht[:, k, :], ACT.Copy).then_inc(h_hi_ready, 1)

            def high(s, rounds):
                act.wait_ge(w_tile[s], 64 * rounds + 64)
                nc.scalar.activation(w_parts[:, s, 0], at(g, W_MERGE + 3072 * s, 2 * SEQ).rearrange("p (b k n) -> p b k n", b=2, k=KT),
                                     ACT.Copy).then_inc(w_hi_ready, 1)

            def gates(i, last):
                for s in range(2):
                    if not (last and s == 1):
                        act.wait_ge(made, 4 * i + 2 * s + 2)
                        high(1 - s, i + s)
                    for u in (2 * s, 2 * s + 1):
                        act.wait_ge(made, 4 * i + u + 3)
                        for b in range(2):
                            nc.scalar.activation(gate[:, 2 * (u % 2) + b, :], bank(g, 4 * (u % 2) + b), ACT.Sigmoid).then_inc(gated, 1)

            high(0, 0)
            with act.Fori(0, KT // 2 - 1) as i:
                gates(i, False)
            gates(KT // 2 - 1, True)

        @block.vector
        def _(dve):
            dve.sem_inc(merged, 2)
            nc.vector.tensor_scalar(g.gain_sub[:, 1:2], g.gain_sub[:, 0:1], 1.0 - LAMBDA_INIT, None, ALU.mult).then_inc(sub_steps, 1)
            dve.wait_ge(sub_steps, ROOTED)
            nc.vector.reciprocal(g.ssq[:, :], g.ssq[:, :]).then_inc(sub_steps, 1)
            dve.wait_ge(sub_steps, INVERTED)
            yv = at(g, Y_DIFF, TT * HALF).rearrange("p (a n) -> p a n", n=DIFF_V)
            for rows in (slice(0, 16), slice(16, 32)):
                nc.vector.tensor_tensor(yv[:, rows], yv[:, rows], g.ssq[:, rows].unsqueeze(2).broadcast_to([P, 16, DIFF_V]),
                                        ALU.mult).then_inc(sub_steps, 1)
            for n in range(1, 16, 2):
                dve.wait_ge(turned, n + 1)
                if n < 8:
                    last = nc.vector.tensor_copy(yt[:, n // 2, HALF:], bank(g, n % 8))
                else:
                    last = nc.vector.tensor_scalar(yt[:, n // 2, HALF:], bank(g, n % 8), g.gain_sub[:, 1:2], None, ALU.mult)
                last.then_inc(copied_d, 1)
            dve.wait_ge(turned, 16)
            for k in range(KT):
                dve.wait_ge(h_hi_ready, k + 1)
                nc.vector.tensor_tensor(h_lo[:, k, :], ht[:, k, :], h_hi[:, k, :], ALU.subtract).then_inc(h_lo_ready, 1)

            def low(f, s):
                dve.wait_ge(w_hi_ready, f + 1)
                nc.vector.tensor_tensor(w_parts[:, s, 1], at(g, W_MERGE + 3072 * s, 2 * SEQ).rearrange("p (b k n) -> p b k n", b=2, k=KT),
                                        w_parts[:, s, 0], ALU.subtract).then_inc(w_lo_ready, 1)

            def merge(i, last):
                for s in range(2):
                    if not (last and s == 1):
                        low(2 * i + s + 1, 1 - s)
                    for h in range(2):
                        n = 4 * i + 2 * s + h
                        for b in range(2):
                            dve.wait_ge(gated, 2 * n + b + 1)
                            nc.vector.tensor_tensor(gate[:, 2 * h + b, :], bank(g, 4 * h + 2 + b), gate[:, 2 * h + b, :], ALU.mult).then_inc(scaled, 1)
                        dve.wait_ge(scaled, 2 * n + 2)
                        nc.vector.tensor_tensor(out[:, bass.ds(2 * i + s, 1), h * HALF:(h + 1) * HALF], gate[:, 2 * h, :],
                                                gate[:, 2 * h + 1, :], ALU.add).then_inc(merged, 1)

            low(0, 0)
            with dve.Fori(0, KT // 2 - 1) as i:
                merge(i, False)
            merge(KT // 2 - 1, True)
            dve.wait_ge(merged, 2 * KT + 2)


def routing_views(g):
    v = Core(g.nc)
    v.chosen = tiled(g, CHOSEN, TK, EXPERTS)
    v.earlier = tiled(g, EARLIER, TT + 1, EXPERTS)
    v.gates = tiled(g, GATES, TT, EXPERTS)
    v.expert_row = at(g, EXPERT_ROW, EXPERTS)
    v.tri = tiled(g, TRI, EXPERTS, EXPERTS)
    v.job_no = at(g, EXPERT_ROW + 352, EXTRA_JOBS).bitcast(I32)
    v.x2 = tiled(g, X2, TT, D)
    return v


def to_lists(g, io, pool, t):
    dest_i, entry = at(g, EXPERT_ROW + 192, TK).bitcast(I32), at(g, ENTRY, 2 * TK)
    for n in range(t * TOP_K, (t + 1) * TOP_K):
        pool.indirect_dma_start(out=io.lists, out_offset=bass.IndirectOffsetOnAxis(ap=dest_i[:, n:n + 1], axis=0),
                                in_=entry[:, 2 * n:2 * n + 2], in_offset=None,
                                bounds_check=EXPERTS * LIST - 1, oob_is_err=True).then_inc(g.listed, 16)


def stage_out(g, io):
    nc = g.nc
    w_out_in, x_in = g.w_out_in, [g.sem(f"x_res{s}") for s in range(2)]
    router_in = g.sem("router_in")
    h2_out = [g.sem(f"h2_out{s}") for s in range(2)]
    ids, fill_out, shifted, exps, ranked, placed, data_ready, chain_s = (
        g.sem("route_" + n) for n in ("ids", "fill_out", "shifted", "exps", "ranked", "placed", "data_ready", "chain"))
    made, added, squared, rooted, normed, turned, h2t_ready, scored, biased, chosen = (
        g.sem("out_" + n) for n in ("made", "added", "squared", "rooted", "normed", "turned", "h2t_ready", "scored", "biased", "chosen"))
    w_out, merged = tiled(g, W_OUT, KT, D), tiled(g, MERGED, KT, SEQ)
    x, h2 = tiled(g, X_RES, 2, D), tiled(g, H2, 2, D)
    h2t = at(g, H2_T, 2 * D).rearrange("p (s k t) -> p s k t", s=2, k=KT)
    w_r = tiled(g, W_ROUTER, KT, EXPERTS)
    b_r = at(g, B_ROUTER, EXPERTS)
    logits = tiled(g, LOGITS, TT, EXPERTS)
    v = routing_views(g)
    x2, chosen_by, earlier = v.x2, v.chosen, v.earlier
    picked, weighted = tiled(g, PICKED, TK, EXPERTS), tiled(g, WEIGHTED, TOP_K, EXPERTS)
    member, place = tiled(g, MEMBER, TT, EXPERTS), tiled(g, PLACE, TT, EXPERTS)
    expert_i, start_row = at(g, EXPERT_ROW + 32, EXPERTS).bitcast(I32), at(g, EXPERT_ROW + 64, EXPERTS)
    best_f, dest, wts = at(g, EXPERT_ROW + 96, TK), at(g, EXPERT_ROW + 128, TK), at(g, EXPERT_ROW + 160, TK)
    dest_i, sums = at(g, EXPERT_ROW + 192, TK).bitcast(I32), at(g, EXPERT_ROW + 224, TT)
    entry, fill, zero = at(g, ENTRY, 2 * TK), at(g, FILL, 512), at(g, ZERO, D)
    total, root, inv = g.stat[:, 0:8], g.stat[:, 8:16], g.stat[:, 16:24]

    with nc.Block() as block:

        @block.sync
        def _(sp):
            def load_x(t):
                if t >= 2:
                    sp.wait_ge(added, t - 1)
                sp.dma_start(x[:, t % 2, :], io.x[0, t * P:(t + 1) * P, :]).then_inc(x_in[t % 2], 16)

            sp.dma_start(w_out[:, OUT_FIRST:, :], out_weights(io)[:, OUT_FIRST:, :]).then_inc(w_out_in[1], 16)
            load_x(0)
            sp.dma_start(w_r, io.w_router.rearrange("(k p) n -> p k n", p=P)).then_inc(router_in, 16)
            sp.dma_start(b_r, io.b_router.partition_broadcast(P)).then_inc(router_in, 16)
            load_x(1)
            for t in range(2, TT):
                load_x(t)
                if t in (2, 3):
                    load_weights(g, io, sp, 0, t - 2)

        @block.gpsimd
        def _(pool):
            pool.iota(expert_i, pattern=[[1, EXPERTS]], base=0, channel_multiplier=0).then_inc(ids, 1)
            pool.iota(entry.bitcast(I32).rearrange("p (n c) -> p n c", c=2)[:, :, 0:1].rearrange("p (t k) c -> p t (k c)", t=TT),
                      pattern=[[P, TT], [0, TOP_K]], base=0, channel_multiplier=1).then_inc(ids, 1)
            pool.memset(fill, 0.0).then_inc(ids, 1)
            pool.memset(v.tri, 1.0).then_inc(ids, 1)
            pool.memset(zero, 0.0).then_inc(ids, 1)
            pool.iota(v.job_no, pattern=[[1, EXTRA_JOBS]], base=0, channel_multiplier=0).then_inc(ids, 1)
            pool.wait_ge(ids, 6)
            pool.iota(fill.bitcast(I32).rearrange("p (n c) -> p n c", c=2)[:, :, 0], pattern=[[1, 256]],
                      base=DUMMY, channel_multiplier=0).then_inc(ids, 1)
            pool.affine_select(out=v.tri, in_=v.tri, compare_op=ALU.is_ge, fill=0.0, base=0,
                               pattern=[[1, EXPERTS], [-1, EXPERTS]], channel_multiplier=0).then_inc(ids, 1)
            pool.wait_ge(ids, 8)
            pool.dma_start(io.lists.rearrange("(p n) c -> p (n c)", p=P), fill).then_inc(fill_out, 16)
            for r in range(DUMMY, ROWS, P):
                pool.dma_start(io.h2[r:r + P, :], zero).then_inc(g.zeros, 16)
                pool.dma_start(io.acc[r:r + P, :], zero).then_inc(g.zeros, 16)
            pool.wait_ge(fill_out, 16)

            for t in range(TT):
                pool.wait_ge(normed, t + 1)
                pool.dma_start(io.h2[t * P:(t + 1) * P, :], h2[:, t % 2, :]).then_inc(h2_out[t % 2], 16)
                if t >= 2:
                    pool.wait_ge(data_ready, t - 1)
                    to_lists(g, io, pool, t - 2)
            for s in range(2):
                pool.wait_ge(h2_out[s], 16 * TT // 2)

        @block.tensor
        def _(pe):

            def project(t):
                if t >= 2:
                    pe.wait_ge(added, t - 1)
                for c, ks, h in ((0, range(OUT_FIRST), 0), (0, range(OUT_FIRST), 1), (1, range(OUT_FIRST, KT), 0), (1, range(OUT_FIRST, KT), 1)):
                    if t == 0 and h == 0:
                        pe.wait_ge(w_out_in[c], 16)
                    for k in ks:
                        last = nc.tensor.matmul(bank(g, 2 * (t % 2) + h), merged[:, k, t * P:(t + 1) * P], w_out[:, k, h * HALF:(h + 1) * HALF],
                                                start=(k == 0), stop=(k == KT - 1))
                last.then_inc(made, 1)

            def turn(t):
                pe.wait_ge(normed, t + 1)
                if t >= 1:
                    pe.wait_ge(h2t_ready, t)
                for k in range(KT):
                    last = nc.tensor.transpose(bank(g, 4, 2)[:, k * P:(k + 1) * P], h2[:, t % 2, k * P:(k + 1) * P], g.ident[:, :])
                last.then_inc(turned, 1)

            def route(t):
                pe.wait_ge(h2t_ready, t + 1)
                if t == 0:
                    pe.wait_ge(router_in, 32)
                if t >= 1:
                    pe.wait_ge(biased, t)
                for k in range(KT):
                    last = nc.tensor.matmul(bank(g, 6)[:, 0:EXPERTS], h2t[:, t % 2, k, :], w_r[:, k, :], start=(k == 0), stop=(k == KT - 1))
                last.then_inc(scored, 1)

            def rank(t):
                pe.wait_ge(ranked, t + 1)
                if t >= 1:
                    pe.wait_ge(data_ready, t)
                cols = bank(g, 7)[:, t * EXPERTS:(t + 1) * EXPERTS]
                nc.tensor.matmul(cols, g.before[:, :], member[:, t, :], start=True, stop=False)
                nc.tensor.matmul(cols, g.ones[:, :], earlier[:, t, :], start=False, stop=True).then_inc(placed, 1)

            project(0)
            for t in range(TT):
                if t + 1 < TT:
                    project(t + 1)
                turn(t)
                if t >= 1:
                    route(t - 1)
                if t >= 2:
                    rank(t - 2)
            route(TT - 1)
            rank(TT - 2)
            rank(TT - 1)

        @block.scalar
        def _(act):
            def exp(t):
                act.wait_ge(shifted, t + 1)
                tile = wts[:, t * TOP_K:(t + 1) * TOP_K]
                nc.scalar.activation(tile, tile, ACT.Exp).then_inc(exps, 1)

            for t in range(TT):
                act.wait_ge(added, t + 1)
                nc.scalar.activation(h2[:, t % 2, :], x2[:, t, :], ACT.Square, accum_out=total[:, t:t + 1]).then_inc(squared, 1)
                act.wait_ge(squared, t + 1)
                nc.scalar.activation(root[:, t:t + 1], total[:, t:t + 1], ACT.Sqrt, scale=1.0 / D, bias=g.eps[:, 0:1]).then_inc(rooted, 1)
                if t >= 2:
                    exp(t - 2)
            exp(TT - 2)
            exp(TT - 1)

        @block.vector
        def _(dve):
            chain = g.chain = Chain(dve, chain_s)

            def add(t):
                s = t % 2
                if t >= 2:
                    dve.wait_ge(h2_out[s], 16 * (t // 2))
                    dve.wait_ge(turned, t - 1)
                dve.wait_ge(made, t + 1)
                dve.wait_ge(x_in[s], 16 * (t // 2) + 16)
                nc.vector.tensor_tensor(x2[:, t, :], bank(g, 2 * s, 2), x[:, s, :], ALU.add).then_inc(added, 1)

            def norm(t):
                dve.wait_ge(rooted, t + 1)
                chain.step(nc.vector.reciprocal(inv[:, t:t + 1], root[:, t:t + 1]))
                nc.vector.tensor_scalar(h2[:, t % 2, :], x2[:, t, :], inv[:, t:t + 1], None, ALU.mult).then_inc(normed, 1)

            def copy(t):
                dve.wait_ge(turned, t + 1)
                nc.vector.tensor_tensor(h2t[:, t % 2], bank(g, 4, 2).rearrange("p (k t) -> p k t", k=KT),
                                        g.gain_ffn[:, :].unsqueeze(2).broadcast_to([P, KT, P]), ALU.mult).then_inc(h2t_ready, 1)

            def choose(t):
                dve.wait_ge(scored, t + 1)
                nc.vector.tensor_tensor(logits[:, t, :], bank(g, 6)[:, 0:EXPERTS], b_r, ALU.add).then_inc(biased, 1)
                dve.wait_ge(biased, t + 1)
                chain.step(nc.vector.max(g.best[:, 8 * t:8 * t + 8], logits[:, t, :]))
                nc.vector.max_index(g.best_at[:, 8 * t:8 * t + 8], g.best[:, 8 * t:8 * t + 8], logits[:, t, :]).then_inc(chosen, 1)

            best_at = g.best_at[:, :].rearrange("p (t k) -> p t k", t=TT)
            best_v = g.best[:, :].rearrange("p (t k) -> p t k", t=TT)

            def member_of(t):
                ranks = slice(t * TOP_K, (t + 1) * TOP_K)
                dve.wait_ge(chosen, t + 1)
                nc.vector.tensor_tensor(wts[:, ranks], best_v[:, t, 0:TOP_K], best_v[:, t, 0:1].broadcast_to([P, TOP_K]),
                                        ALU.subtract).then_inc(shifted, 1)
                chain.step(nc.vector.tensor_copy(best_f[:, ranks], best_at[:, t, 0:TOP_K]))
                chain.step(nc.vector.tensor_tensor(chosen_by[:, ranks, :], v.expert_row.unsqueeze(1).broadcast_to([P, TOP_K, EXPERTS]),
                                                   best_f[:, ranks].unsqueeze(2).broadcast_to([P, TOP_K, EXPERTS]), ALU.is_equal))
                chain.step(nc.vector.reduce_sum(member[:, t, :], chosen_by[:, ranks, :].rearrange("p k e -> p e k"), AX))
                nc.vector.tensor_tensor(earlier[:, t + 1, :], earlier[:, t, :], member[:, t, :], ALU.add).then_inc(ranked, 1)
                dve.wait_ge(ranked, t + 1)

            def place_of(t):
                ranks = slice(t * TOP_K, (t + 1) * TOP_K)
                dve.wait_ge(exps, t + 1)
                chain.step(nc.vector.reduce_sum(sums[:, t:t + 1], wts[:, ranks], AX))
                chain.step(nc.vector.reciprocal(sums[:, t:t + 1], sums[:, t:t + 1]))
                chain.step(nc.vector.tensor_scalar(wts[:, ranks], wts[:, ranks], sums[:, t:t + 1], None, ALU.mult))
                chain.step(nc.vector.tensor_copy(entry.rearrange("p (n c) -> p n c", c=2)[:, ranks, 1], wts[:, ranks]))
                chain.step(nc.vector.tensor_tensor(weighted, chosen_by[:, ranks, :], wts[:, ranks].unsqueeze(2).broadcast_to([P, TOP_K, EXPERTS]), ALU.mult))
                chain.step(nc.vector.reduce_sum(v.gates[:, t, :], weighted.rearrange("p k e -> p e k"), AX))
                dve.wait_ge(placed, t + 1)
                chain.step(nc.vector.tensor_tensor(place[:, t, :], bank(g, 7)[:, t * EXPERTS:(t + 1) * EXPERTS], start_row, ALU.add))
                chain.step(nc.vector.tensor_tensor(picked[:, ranks, :], chosen_by[:, ranks, :], place[:, t:t + 1, :].broadcast_to([P, TOP_K, EXPERTS]), ALU.mult))
                chain.step(nc.vector.reduce_sum(dest[:, ranks], picked[:, ranks, :], AX))
                nc.vector.tensor_copy(dest_i[:, ranks], dest[:, ranks]).then_inc(data_ready, 1)

            dve.wait_ge(ids, 8)
            chain.step(nc.vector.tensor_copy(v.expert_row, expert_i))
            chain.step(nc.vector.tensor_scalar(start_row, v.expert_row, float(LIST), None, ALU.mult))
            chain.step(nc.vector.memset(earlier[:, 0, :], 0.0))
            dve.wait_ge(router_in, 32)
            add(0)
            for t in range(TT):
                norm(t)
                if t + 1 < TT:
                    add(t + 1)
                copy(t)
                if t >= 1:
                    choose(t - 1)
                    member_of(t - 1)
                if t >= 2:
                    place_of(t - 2)
            choose(TT - 1)
            member_of(TT - 1)
            place_of(TT - 2)
            place_of(TT - 1)
            dve.wait_ge(data_ready, TT)


def stage_route(g, io):
    nc = g.nc
    counted, gates_turned, gates_out, bias_made, based = (
        g.sem("table_" + n) for n in ("counted", "gates_turned", "gates_out", "bias_made", "based"))
    bias_in, bias_turned = g.sem("table_bias_in"), g.sem("table_bias_turned")
    v = routing_views(g)
    cnt, more, upto = (at(g, EXPERT_ROW + 256 + 32 * n, EXPERTS) for n in range(3))
    tri2, past = tiled(g, CHOSEN, EXPERTS, EXPERTS), tiled(g, PICKED, EXTRA_JOBS, EXPERTS)
    past2 = tiled(g, PICKED + 512, EXTRA_JOBS, EXPERTS)
    job_e, job_d, job_n, job_w = (at(g, EXPERT_ROW + 368 + 16 * n, EXTRA_JOBS) for n in range(4))
    b1_in, b2_in = at(g, B_IN, 2 * D_EXP)[0:EXPERTS], at(g, B_IN + 2 * D_EXP, D)[0:EXPERTS]
    b1_t = tiled(g, B1_T, EXPERTS, 2 * FT)
    gates_t = at(g, ZERO, SEQ)[0:EXPERTS]

    with nc.Block() as block:

        @block.gpsimd
        def _(pool):
            to_lists(g, io, pool, TT - 2)
            to_lists(g, io, pool, TT - 1)
            pool.wait_ge(g.listed, 16 * TK)
            pool.wait_ge(g.zeros, 16 * 2 * JH)
            first = g.entries[:, 0:2 * JH].rearrange("p (h c) -> p h c", c=2)
            pool.dma_start(first, io.lists[0:JOB, :].rearrange("(h p) c -> p h c", p=P)).then_inc(g.ent_in, 16)
            pool.wait_ge(g.ent_in, 16)
            nc.gpsimd.tensor_copy(g.rows[:, 0:JH], first.bitcast(I32)[:, :, 0]).then_inc(g.rows_known, 1)
            pool.wait_ge(g.rows_known, 1)
            gather_rows(g, io, pool, JH)

        @block.sync
        def _(sp):
            sp.dma_start(b2_in, io.b2).then_inc(bias_in, 16)
            sp.dma_start(b1_in, io.b1).then_inc(bias_in, 16)
            for slot in (2, 3):
                load_weights(g, io, sp, 0, slot)
            for t in range(TT):
                sp.wait_ge(based, t + 1)
                sp.dma_start(io.acc[t * P:(t + 1) * P, :], v.x2[:, t, :]).then_inc(g.acc_out, 16)

        @block.tensor
        def _(pe):
            nc.tensor.matmul(bank(g, 1)[:, 0:EXPERTS], g.ones[:, :], v.earlier[:, TT, :], start=True, stop=True).then_inc(counted, 1)
            for t in range(TT):
                last = nc.tensor.transpose(bank(g, 4, 2)[0:EXPERTS, t * P:(t + 1) * P], v.gates[:, t, :], g.ident[:, :])
            last.then_inc(gates_turned, 1)
            pe.wait_ge(gates_out, 1)
            pe.wait_ge(bias_in, 32)
            for t in range(TT):
                if t >= 2:
                    pe.wait_ge(based, t - 1)
                for h in range(2):
                    last = nc.tensor.matmul(bank(g, 4 + 2 * (t % 2) + h), gates_t[:, t * P:(t + 1) * P], b2_in[:, h * HALF:(h + 1) * HALF],
                                            start=True, stop=True)
                last.then_inc(bias_made, 1)
                if t == 4:
                    for f in range(2 * FT):
                        last = nc.tensor.transpose(bank(g, 2)[:, f * EXPERTS:(f + 1) * EXPERTS], b1_in[:, f * P:(f + 1) * P], g.ident[0:EXPERTS, 0:EXPERTS])
                    last.then_inc(bias_turned, 1)

        @block.scalar
        def _(act):
            act.wait_ge(gates_turned, 1)
            nc.scalar.activation(gates_t, bank(g, 4, 2)[0:EXPERTS], ACT.Copy).then_inc(gates_out, 1)

        @block.vector
        def _(dve):
            chain = g.chain

            def add_bias(t):
                dve.wait_ge(bias_made, t + 1)
                nc.vector.tensor_tensor(v.x2[:, t, :], v.x2[:, t, :], bank(g, 4 + 2 * (t % 2), 2), ALU.add).then_inc(based, 1)

            dve.wait_ge(counted, 1)
            chain.step(nc.vector.tensor_copy(cnt, bank(g, 1)[:, 0:EXPERTS]))
            chain.step(nc.vector.tensor_copy(g.job_count[:, 0:EXPERTS], cnt))
            chain.step(nc.vector.tensor_scalar(more, cnt, float(JOB), None, ALU.is_gt))
            for j in range(2, LIST // JOB):
                chain.step(nc.vector.scalar_tensor_tensor(out=more, in0=cnt, scalar=float(JOB * j), in1=more, op0=ALU.is_gt, op1=ALU.add))
            chain.step(nc.vector.tensor_tensor(tri2, v.tri, more.unsqueeze(1).broadcast_to([P, EXPERTS, EXPERTS]), ALU.mult))
            chain.step(nc.vector.reduce_sum(upto, tri2, AX))
            chain.step(nc.vector.tensor_scalar(g.total[:, 0:1], upto[:, EXPERTS - 1:EXPERTS], float(EXPERTS), None, ALU.add))
            add_bias(0)
            chain.step(nc.vector.tensor_copy(job_e, v.job_no))
            chain.step(nc.vector.tensor_tensor(past, job_e.unsqueeze(2).broadcast_to([P, EXTRA_JOBS, EXPERTS]),
                                               upto.unsqueeze(1).broadcast_to([P, EXTRA_JOBS, EXPERTS]), ALU.is_ge))
            chain.step(nc.vector.tensor_tensor(past2, past, more.unsqueeze(1).broadcast_to([P, EXTRA_JOBS, EXPERTS]), ALU.mult))
            chain.step(nc.vector.reduce_sum(job_d, past2, AX))
            add_bias(1)
            chain.step(nc.vector.tensor_tensor(job_d, job_e, job_d, ALU.subtract))
            chain.step(nc.vector.tensor_scalar(job_d, job_d, 1.0, None, ALU.add))
            chain.step(nc.vector.reduce_sum(job_e, past, AX))
            chain.step(nc.vector.tensor_scalar(job_e, job_e, float(EXPERTS - 1), None, ALU.min))
            chain.step(nc.vector.tensor_copy(g.job_expert[:, 0:EXPERTS], v.expert_row))
            chain.step(nc.vector.tensor_copy(g.job_expert[:, EXPERTS:JOBS], job_e))
            add_bias(2)
            chain.step(nc.vector.tensor_copy(job_w, job_d))
            chain.step(nc.vector.scalar_tensor_tensor(out=job_d, in0=job_e, scalar=float(LIST // JOB), in1=job_d, op0=ALU.mult, op1=ALU.add))
            chain.step(nc.vector.tensor_scalar(g.job_place[:, EXPERTS:JOBS], job_d, float(EXPERTS * LIST // JOB - 1), None, ALU.min))
            chain.step(nc.vector.tensor_scalar(g.job_place[:, 0:EXPERTS], v.expert_row, float(LIST // JOB), None, ALU.mult))
            chain.step(nc.vector.memset(g.job_place[:, JOBS:], 0))
            add_bias(3)
            chain.step(nc.vector.tensor_tensor(past, v.expert_row.unsqueeze(1).broadcast_to([P, EXTRA_JOBS, EXPERTS]),
                                               job_e.unsqueeze(2).broadcast_to([P, EXTRA_JOBS, EXPERTS]), ALU.is_equal))
            chain.step(nc.vector.tensor_tensor(past2, past, cnt.unsqueeze(1).broadcast_to([P, EXTRA_JOBS, EXPERTS]), ALU.mult))
            chain.step(nc.vector.reduce_sum(job_n, past2, AX))
            add_bias(4)
            chain.step(nc.vector.scalar_tensor_tensor(out=job_n, in0=job_w, scalar=-float(JOB), in1=job_n, op0=ALU.mult, op1=ALU.add))
            chain.step(nc.vector.tensor_scalar(g.job_count[:, EXPERTS:JOBS], job_n, 0.0, None, ALU.max))
            chain.step(nc.vector.memset(g.job_count[:, JOBS:], 0))
            add_bias(5)
            dve.wait_ge(bias_turned, 1)
            src = bank(g, 2)[:, :].rearrange("p (f e) -> p e f", e=EXPERTS)
            chain.step(nc.vector.tensor_copy(b1_t[:, :, 0:FT], src[:, :, 0:FT]))
            chain.step(nc.vector.tensor_scalar(b1_t[:, :, FT:], src[:, :, FT:], 1.0, None, ALU.add))
            add_bias(6)
            add_bias(7)


def weight_slots(g):
    return ([at(g, R + c * RING_SLOT, RING_SLOT).rearrange("p (s k n) -> p s k n", s=2, k=KT) for c in range(4)],
            [tiled(g, R + (4 + c) * RING_SLOT, FT, HALF) for c in range(2)])


def load_weights(g, io, eng, expert, slot):
    w1, w2 = weight_slots(g)
    if slot < 4:
        src = io.w1.rearrange("e (k p) n -> p e k n", p=P)
        for s in range(2):
            col = s * D_EXP + slot * 2 * P
            eng.dma_start(w1[slot][:, s].unsqueeze(1), src[:, bass.ds(expert, 1), :, col:col + 2 * P]).then_inc(g.w_in[slot], 16)
    else:
        src = io.w2.rearrange("e (k p) n -> p e k n", p=P)
        col = (slot - 4) * HALF
        eng.dma_start(w2[slot - 4].unsqueeze(1), src[:, bass.ds(expert, 1), :, col:col + HALF]).then_inc(g.w_in[slot], 16)


FEW = 16


def gather_rows(g, io, pool, halves):
    xg = tiled(g, XG, JH, D)
    for h in range(JH):
        rows = P if h < halves else FEW
        pool.indirect_dma_start(out=xg[0:rows, h, :], out_offset=None, in_=io.h2,
                                in_offset=bass.IndirectOffsetOnAxis(ap=g.rows[0:rows, h:h + 1], axis=0),
                                bounds_check=ROWS - 1, oob_is_err=True).then_inc(g.gathered, 16)


def stage_experts(g, io):
    nc = g.nc
    ent_in, gathered, rows_known = g.ent_in, g.gathered, g.rows_known
    scattered, x_turned, xt_dve, xt_act = (g.sem("moe_" + n) for n in ("scattered", "x_turned", "xt_dve", "xt_act"))
    yg_free = g.sem("moe_yg_free")
    made, g_ready, l_ready, s_ready, gs_ready, act_ready = (
        g.sem("moe_" + n) for n in ("made", "g_ready", "l_ready", "s_ready", "gs_ready", "act_ready"))
    y_made, yg_dve, yg_act = (g.sem("moe_" + n) for n in ("y_made", "yg_dve", "yg_act"))
    act_hi_ready, act_lo_ready, w_hi_ready, w_lo_ready, piece_used = (
        g.sem("moe_" + n) for n in ("act_hi_ready", "act_lo_ready", "w_hi_ready", "w_lo_ready", "piece_used"))
    w1, w2 = weight_slots(g)
    xg, yg = tiled(g, XG, JH, D), tiled(g, YG, JH, D)
    xt, act_t = tiled(g, XT, KT, JOB), tiled(g, ACT_T, FT, JOB)
    glu, sig, lin = at(g, EG, HALF), at(g, EG + HALF, HALF), at(g, EG + 2 * HALF, HALF)
    act_hi, act_lo = (g.parts[0][:, s * FT * JOB:(s + 1) * FT * JOB].rearrange("p (f t) -> p f t", f=FT) for s in range(2))
    PIECE = 2 * HALF
    piece_at = [g.parts[0][:, 2 * FT * JOB + 2 * PIECE * s:2 * FT * JOB + 2 * PIECE * (s + 1)] for s in range(2)] + [
        g.parts[1][:, 2 * PIECE * s:2 * PIECE * (s + 1)] for s in range(4)]
    pieces = [piece_at[q % 6].rearrange("p (s f n) -> p s f n", s=2, f=2) for q in range(8)]
    piece_of = lambda q: w2[q // 4][:, 2 * (q % 4):2 * (q % 4) + 2, :]
    ent = g.entries[:, :].rearrange("p (n h c) -> p n h c", h=JH, c=2)
    b1_t = tiled(g, B1_T, EXPERTS, 2 * FT)
    rows_in, rows_out = (g.rows[:, JH * s:JH * (s + 1)] for s in range(2))
    weight = lambda n, h: g.entries[:, bass.ds(2 * JH * n + (2 * h + 1), 1)]
    entries = io.lists.rearrange("(n h p) c -> p n h c", p=P, h=JH)

    with nc.Block() as block:

        @block.sync
        def _(sp):
            sp.wait_ge(gathered, 32)
            sp.wait_ge(g.acc_out, 16 * TT)
            for slot in (4, 5):
                load_weights(g, io, sp, 0, slot)
            total = sp.value_load(g.total[0:1, 0:1], min_val=EXPERTS, max_val=JOBS)
            with sp.Fori(1, JOBS) as n:
                with sp.If(total > n):
                    expert = sp.value_load(g.job_expert[0:1, bass.ds(n, 1)], min_val=0, max_val=EXPERTS - 1)
                    for c in range(6):
                        if c < 4:
                            sp.wait_ge(made, 8 * n + (2 * c - 6))
                        else:
                            sp.wait_ge(w_lo_ready, 8 * n + (4 * c - 20))
                        load_weights(g, io, sp, expert, c)
                with sp.Else():
                    sp.nop()

        @block.gpsimd
        def _(pool):
            def load_entries(n):
                place = pool.value_load(g.job_place[0:1, bass.ds(n, 1)], min_val=0, max_val=EXPERTS * LIST // JOB - 1)
                pool.dma_start(ent[:, bass.ds(n, 1)], entries[:, bass.ds(place, 1)]).then_inc(ent_in, 16)

            def find_rows(n, seen):
                nc.gpsimd.tensor_copy(rows_in, ent.bitcast(I32)[:, bass.ds(n, 1), :, 0]).then_inc(rows_known, 1)
                pool.wait_ge(rows_known, seen)
                pool.sem_inc(g.carried, 1)

            def scatter(halves):
                for h in range(JH):
                    rows = P if h < halves else FEW
                    pool.indirect_dma_start(out=io.acc, out_offset=bass.IndirectOffsetOnAxis(ap=rows_out[0:rows, h:h + 1], axis=0),
                                            in_=yg[0:rows, h, :], in_offset=None, compute_op=ALU.add,
                                            bounds_check=ROWS - 1, oob_is_err=True).then_inc(scattered, 16)

            def by_halves(n, step):
                count = pool.value_load(g.job_count[0:1, bass.ds(n, 1)], min_val=0, max_val=SEQ)
                with pool.If(count > P):
                    step(2)
                with pool.Else():
                    step(1)

            pool.sem_inc(yg_free, 1)
            load_entries(1)
            pool.wait_ge(g.acc_out, 16 * TT)
            total = pool.value_load(g.total[0:1, 0:1], min_val=EXPERTS, max_val=JOBS)
            with pool.Fori(0, JOBS) as n:
                with pool.If(total > n):
                    pool.wait_ge(ent_in, 16 * n + 32)
                    pool.wait_ge(x_turned, 4 * n + 4)
                    find_rows(n + 1, 2 * n + 2)
                    by_halves(n + 1, lambda halves: gather_rows(g, io, pool, halves))
                    load_entries(n + 2)
                    pool.wait_ge(yg_dve, 2 * n + 4)
                    pool.wait_ge(yg_act, 2 * n + 4)
                    nc.gpsimd.tensor_copy(rows_out, ent.bitcast(I32)[:, bass.ds(n, 1), :, 0]).then_inc(rows_known, 1)
                    pool.wait_ge(rows_known, 2 * n + 3)
                    pool.sem_inc(g.carried, 1)
                    by_halves(n, scatter)
                    pool.wait_ge(scattered, 32 * n + 32)
                    pool.sem_inc(yg_free, 1)
                with pool.Else():
                    pool.nop()
            pool.wait_ge(ent_in, 16 * total + 32)

        @block.tensor
        def _(pe):
            def turn_x(halves):
                for k in range(KT):
                    for h in range(halves):
                        last = nc.tensor.transpose(bank(g, 4 + k // 2)[:, (k % 2) * JOB + h * P:(k % 2) * JOB + (h + 1) * P],
                                                   xg[:, h, k * P:(k + 1) * P], g.ident[:, :])
                    if k % 2 == 1:
                        last.then_inc(x_turned, 1)

            def job(n, width, next_count):
                pe.wait_ge(xt_dve, 2 * n + 2)
                pe.wait_ge(xt_act, 4 * n + 4)
                for c in range(4):
                    pe.wait_ge(g.w_in[c], 32 * n + 32)
                    if c >= 2:
                        pe.wait_ge(act_ready, 4 * n + (c - 1))
                    for s in range(2):
                        if c < 2:
                            pe.wait_ge((yg_dve, yg_act)[s], 2 * n + (c + 1))
                        for a in range(2):
                            for k in range(KT):
                                last = nc.tensor.matmul(bank(g, 2 * (c % 2) + s)[:, a * JOB:a * JOB + width], w1[c][:, s, k, a * P:(a + 1) * P],
                                                        xt[:, k, 0:width], start=(k == 0), stop=(k == KT - 1))
                        last.then_inc(made, 1)
                pe.wait_ge(gathered, 32 * n + 64)
                with pe.If(next_count > P):
                    turn_x(2)
                with pe.Else():
                    turn_x(1)

                halves = 1 if width <= P else 2

                pe.wait_ge(act_lo_ready, 4 * n + 3)
                for c in range(2):
                    for h in range(halves):
                        rows = slice(h * P, (h + 1) * P)
                        for q in range(4 * c, 4 * c + 4):
                            if h == 0:
                                pe.wait_ge(w_lo_ready, 8 * n + (q + 1))
                            if c == 0 and h == 0 and q == 3:
                                pe.wait_ge(act_lo_ready, 4 * n + 4)
                            for a in range(2):
                                f = 2 * (q % 4) + a
                                for x, y in ((act_hi, 0), (act_hi, 1), (act_lo, 0)):
                                    last = nc.tensor.matmul(bank(g, 2 * h + c), x[:, f, rows], pieces[q][:, y, a, :],
                                                            start=(f == 0 and x is act_hi and y == 0), stop=(f == FT - 1 and x is act_lo))
                            if q < 2 and h == halves - 1:
                                last.then_inc(piece_used, 1)
                        last.then_inc(y_made, 3 - halves)

            def by_count(n, widths, count, next_count):
                if len(widths) == 1:
                    job(n, widths[0], next_count)
                    return
                with pe.If(count > widths[0]):
                    by_count(n, widths[1:], count, next_count)
                with pe.Else():
                    job(n, widths[0], next_count)

            pe.wait_ge(gathered, 32)
            turn_x(2)
            total = pe.value_load(g.total[0:1, 0:1], min_val=EXPERTS, max_val=JOBS)
            with pe.Fori(0, JOBS) as n:
                with pe.If(total > n):
                    count = pe.value_load(g.job_count[0:1, bass.ds(n, 1)], min_val=0, max_val=SEQ)
                    next_count = pe.value_load(g.job_count[0:1, bass.ds(n + 1, 1)], min_val=0, max_val=SEQ)
                    by_count(n, WIDTHS, count, next_count)
                with pe.Else():
                    pe.nop()

        @block.scalar
        def _(act):
            def take_x(n):
                for k in range(KT // 2, KT):
                    if k % 2 == 0:
                        act.wait_ge(x_turned, 4 * n + k // 2 + 1)
                    nc.scalar.activation(xt[:, k, :], bank(g, 4 + k // 2)[:, (k % 2) * JOB:(k % 2 + 1) * JOB], ACT.Copy,
                                         scale=g.gain_ffn[:, k:k + 1]).then_inc(xt_act, 1)

            def high(n, q):
                if q % 4 == 0:
                    act.wait_ge(g.w_in[4 + q // 4], 16 * n + 16)
                nc.scalar.activation(pieces[q][:, 0], piece_of(q), ACT.Copy).then_inc(w_hi_ready, 1)

            act.sem_inc(yg_act, 2)
            take_x(0)
            total = act.value_load(g.total[0:1, 0:1], min_val=EXPERTS, max_val=JOBS)
            with act.Fori(0, JOBS) as n:
                with act.If(total > n):
                    for c in range(4):
                        act.wait_ge(g_ready, 8 * n + 2 * c + 2)
                        nc.scalar.activation(sig, glu, ACT.Sigmoid, scale=ALPHA).then_inc(s_ready, 1)
                        act.wait_ge(act_ready, 4 * n + (c + 1))
                        nc.scalar.activation(act_hi[:, 2 * c:2 * c + 2, :], act_t[:, 2 * c:2 * c + 2, :], ACT.Copy).then_inc(act_hi_ready, 1)
                        if c < 3:
                            high(n, 2 * c)
                            high(n, 2 * c + 1)
                    take_x(n + 1)
                    for q in (6, 7):
                        act.wait_ge(piece_used, 2 * n + (q - 5))
                        high(n, q)
                    act.wait_ge(yg_free, n + 1)
                    for h in range(JH):
                        act.wait_ge(y_made, 4 * n + (3 + h))
                        nc.scalar.activation(yg[:, h, HALF:], bank(g, 2 * h + 1), ACT.Copy, scale=weight(n, h)).then_inc(yg_act, 1)
                with act.Else():
                    act.nop()

        @block.vector
        def _(dve):
            def take_x(n):
                for b in range(2):
                    dve.wait_ge(x_turned, 4 * n + b + 1)
                    nc.vector.tensor_tensor(xt[:, 2 * b:2 * b + 2, :], bank(g, 4 + b).rearrange("p (k t) -> p k t", k=2),
                                            g.gain_ffn[:, 2 * b:2 * b + 2].unsqueeze(2).broadcast_to([P, 2, JOB]), ALU.mult).then_inc(xt_dve, 1)

            def low(n, q):
                dve.wait_ge(w_hi_ready, 8 * n + (q + 1))
                nc.vector.tensor_tensor(pieces[q][:, 1], piece_of(q), pieces[q][:, 0], ALU.subtract).then_inc(w_lo_ready, 1)

            dve.sem_inc(yg_dve, 2)
            take_x(0)
            total = dve.value_load(g.total[0:1, 0:1], min_val=EXPERTS, max_val=JOBS)
            with dve.Fori(0, JOBS) as n:
                with dve.If(total > n):
                    expert = dve.value_load(g.job_expert[0:1, bass.ds(n, 1)], min_val=0, max_val=EXPERTS - 1)
                    for c in range(4):
                        for s, (dst, ready, limit) in enumerate(((glu, g_ready, LIMIT), (lin, l_ready, LIMIT + 1.0))):
                            dve.wait_ge(made, 8 * n + 2 * c + s + 1)
                            for a in range(2):
                                nc.vector.tensor_scalar(dst[:, a * JOB:(a + 1) * JOB], bank(g, 2 * (c % 2) + s)[:, a * JOB:(a + 1) * JOB],
                                                        b1_t[:, bass.ds(expert, 1), s * FT + 2 * c + a], limit, ALU.add, ALU.min).then_inc(ready, 1)
                        dve.wait_ge(s_ready, 4 * n + c + 1)
                        dve.wait_ge(g_ready, 8 * n + 2 * c + 2)
                        nc.vector.tensor_tensor(sig, glu, sig, ALU.mult).then_inc(gs_ready, 1)
                        dve.wait_ge(gs_ready, 4 * n + c + 1)
                        dve.wait_ge(l_ready, 8 * n + 2 * c + 2)
                        nc.vector.scalar_tensor_tensor(out=at(g, ACT_T + 2 * c * JOB, 2 * JOB), in0=lin, scalar=1.0 - LIMIT, in1=sig,
                                                       op0=ALU.max, op1=ALU.mult).then_inc(act_ready, 1)
                        dve.wait_ge(act_hi_ready, 4 * n + c + 1)
                        nc.vector.tensor_tensor(act_lo[:, 2 * c:2 * c + 2, :], act_t[:, 2 * c:2 * c + 2, :], act_hi[:, 2 * c:2 * c + 2, :],
                                                ALU.subtract).then_inc(act_lo_ready, 1)
                        if c < 3:
                            low(n, 2 * c)
                            low(n, 2 * c + 1)
                    take_x(n + 1)
                    low(n, 6)
                    low(n, 7)
                    dve.wait_ge(yg_free, n + 1)
                    for h in range(JH):
                        dve.wait_ge(y_made, 4 * n + (1 + h))
                        nc.vector.tensor_scalar(yg[:, h, 0:HALF], bank(g, 2 * h), weight(n, h), None, ALU.mult).then_inc(yg_dve, 1)
                with dve.Else():
                    dve.nop()


def stage_final(g, io):
    nc = g.nc
    rows_in = [g.sem(f"final_in{s}") for s in range(2)]
    stored, squared, rooted, inverted, normed = g.sem("final_stored"), g.squared, g.rooted, g.inverted, g.normed
    x, y, gain = tiled(g, R, TT, D), tiled(g, R + TT * D, TT, D), at(g, R + 2 * TT * D, D)
    total, root, inv = g.stat[:, 0:8], g.stat[:, 8:16], g.stat[:, 16:24]

    with nc.Block() as block:

        @block.sync
        def _(sp):
            sp.dma_start(gain, io.norm_final.partition_broadcast(P)).then_inc(rows_in[0], 16)
            for s, (a, b) in enumerate(((0, 2), (2, TT))):
                sp.dma_start(x[:, a:b, :], io.acc[a * P:b * P, :].rearrange("(t p) d -> p t d", p=P)).then_inc(rows_in[s], 16)

        @block.gpsimd
        def _(pool):
            for t in range(TT):
                pool.wait_ge(normed, TT + t + 1)
                pool.dma_start(io.out[0, t * P:(t + 1) * P, :], y[:, t, :]).then_inc(stored, 16)
            pool.wait_ge(stored, 16 * TT)

        @block.scalar
        def _(act):
            for t in range(TT):
                act.wait_ge(rows_in[min(t // 2, 1)], 32 if t < 2 else 16)
                nc.scalar.activation(y[:, t, :], x[:, t, :], ACT.Square, accum_out=total[:, t:t + 1]).then_inc(squared, 1)
                act.wait_ge(squared, TT + t + 1)
                nc.scalar.activation(root[:, t:t + 1], total[:, t:t + 1], ACT.Sqrt, scale=1.0 / D, bias=g.eps[:, 0:1]).then_inc(rooted, 1)

        @block.vector
        def _(dve):
            for t in range(TT):
                dve.wait_ge(rooted, TT + t + 1)
                nc.vector.reciprocal(inv[:, t:t + 1], root[:, t:t + 1]).then_inc(inverted, 1)
                dve.wait_ge(inverted, TT + t + 1)
                nc.vector.scalar_tensor_tensor(out=y[:, t, :], in0=x[:, t, :], scalar=inv[:, t:t + 1], in1=gain,
                                               op0=ALU.mult, op1=ALU.mult).then_inc(normed, 1)


def program(nc, io):
    ctx = ExitStack()
    with ctx, nc.allow_non_contiguous_dma(reason="columns of gains and biases: a few KiB"):
        g = setup(nc, ctx)
        with ExitStack() as scope:
            segments(g, scope, (3, 1, 5))
            for stage in (stage_norm, stage_latents, stage_mla, stage_diff):
                stage(g, io)
        with ExitStack() as scope:
            parts(g, scope, 3)
            stage_merge(g, io)
        segments(g, ctx, (3,))
        with ExitStack() as scope:
            segments(g, scope, (1, 5))
            stage_out(g, io)
            stage_route(g, io)
        with ExitStack() as scope:
            parts(g, scope, 2)
            stage_experts(g, io)
        stage_final(g, io)


_INS = ['x', 'positions', 'norm_mix', 'w_in', 'mla_q_norm', 'w_q_b', 'mla_kv_norm', 'w_kv_b', 'diff_lambda', 'diff_subln',
        'rel_bias', 'w_up_mla', 'w_up_diff', 'w_out', 'norm_ffn', 'w_router', 'b_router', 'w1', 'b1', 'w2', 'b2', 'norm_final']


def kernel(**inputs):
    import numpy as _np
    import concourse.bacc as _bacc
    from concourse import mybir as _mybir
    from concourse.bass_utils import run_bass_kernel_spmd as _run

    nc = _bacc.Bacc("TRN2", target_bir_lowering=False, num_devices=1)
    arrays, dram = {}, {}
    given = {name: inputs[name] for name in _INS} | {"rope_rows": rope_rows(), "bucket_rows": rel_buckets()}
    for name, a in given.items():
        a = _np.ascontiguousarray(a)
        if a.ndim > 1 and a.shape[0] == 1 and name not in ("x", "positions"):
            a = a.reshape(a.shape[1:])
        if a.ndim == 1:
            a = a.reshape(1, -1)
        arrays[f"in_{name}"] = a
        dram[name] = nc.dram_tensor(f"in_{name}", a.shape, _mybir.dt.from_np(a.dtype), kind="ExternalInput").ap()
    dram['out'] = nc.dram_tensor("out_0", (1, SEQ, D), _mybir.dt.float32, kind="ExternalOutput").ap()
    dram['acc'] = nc.dram_tensor("acc_rows", (ROWS, D), F32).ap()
    dram['h2'] = nc.dram_tensor("h2_rows", (ROWS, D), F32).ap()
    dram['pair_bias'] = nc.dram_tensor("pair_bias", (1 + DIFF_HEADS, SEQ, SEQ), F32).ap()
    dram['lists'] = nc.dram_tensor("lists", (EXPERTS * LIST, 2), F32).ap()
    program(nc, Dram(dram))
    r = _run(nc, [arrays], core_ids=[0])
    return r.results[0]["out_0"]
```
